# Optimizing a Trainium2 kernel written in Bass

```python
import math
import jax, jax.numpy as jnp
from jax import lax
import numpy as np

D_MODEL = 1024
BATCH = 1
SEQ = 256
DEPTH = 2

HEAD_DIM = 64
H_FOX = 4
H_DIFF = 4
H_STICK = 4
DIFF_V_DIM = 2 * HEAD_DIM
W_FOX = H_FOX * HEAD_DIM
W_DIFF_QK = 2 * H_DIFF * HEAD_DIM
W_DIFF = H_DIFF * DIFF_V_DIM
W_STICK = H_STICK * HEAD_DIM
N_BRANCH = 3
ROPE_THETA = 500000.0
ROPE_DIM = HEAD_DIM // 4
D_FF = 2816
CONV_WIDTH = 3
Q_BLOCK = 128
NORM_EPS = 1e-6
SPLITS = (W_FOX, W_FOX, W_FOX, W_DIFF_QK, W_DIFF_QK, W_DIFF, W_STICK, W_STICK, W_STICK, H_FOX, N_BRANCH * D_MODEL)
N_IN = 3 * W_FOX + 2 * W_DIFF_QK + W_DIFF + 3 * W_STICK + H_FOX + N_BRANCH * D_MODEL

kernel_name = "hybrid_fox_diff_stickbreaking_convffn"

def rmsnorm(x, g):
    xf = x.astype(jnp.float32)
    y = xf * lax.rsqrt(jnp.mean(xf * xf, axis=-1, keepdims=True) + NORM_EPS)
    return (y * g.astype(jnp.float32)).astype(x.dtype)

def heads(t, n, dh):
    b, s, _ = t.shape
    return t.reshape(b, s, n, dh).transpose(0, 2, 1, 3)

def merge_heads(t):
    b, n, s, dh = t.shape
    return t.transpose(0, 2, 1, 3).reshape(b, s, n * dh)

def split_blocks(t, axis):
    shp = t.shape
    t = t.reshape(shp[:axis] + (shp[axis] // Q_BLOCK, Q_BLOCK) + shp[axis + 1:])
    return jnp.moveaxis(t, axis, 0)

def merge_blocks(o, axis):
    o = jnp.moveaxis(o, 0, axis)
    shp = o.shape
    return o.reshape(shp[:axis] + (shp[axis] * shp[axis + 1],) + shp[axis + 2:])

def partial_rope(t, cos, sin):
    half = ROPE_DIM // 2
    t1 = t[..., :half]
    t2 = t[..., half:ROPE_DIM]
    return jnp.concatenate([t1 * cos - t2 * sin, t2 * cos + t1 * sin, t[..., ROPE_DIM:]], axis=-1)

def fox_attention(q, k, v, log_f):
    s_len = q.shape[2]
    c = jnp.cumsum(log_f, axis=-1)
    kpos = jnp.arange(s_len)
    scale = HEAD_DIM ** -0.5

    def one_block(args):
        qb, cq, i = args
        qpos = i * Q_BLOCK + jnp.arange(Q_BLOCK)
        s = jnp.einsum('bhqd,bhkd->bhqk', qb, k).astype(jnp.float32) * scale
        s = s + cq[..., :, None] - c[..., None, :]
        s = jnp.where(kpos[None, :] <= qpos[:, None], s, -jnp.inf)
        p = jax.nn.softmax(s, axis=-1).astype(v.dtype)
        return jnp.einsum('bhqk,bhkd->bhqd', p, v)

    out = lax.map(one_block, (split_blocks(q, 2), split_blocks(c, 2), jnp.arange(s_len // Q_BLOCK)))
    return merge_blocks(out, 2)

def diff_attention(q, k, v, lam):
    s_len = q.shape[3]
    kpos = jnp.arange(s_len)
    scale = HEAD_DIM ** -0.5

    def one_block(args):
        qb, i = args
        qpos = i * Q_BLOCK + jnp.arange(Q_BLOCK)
        s = jnp.einsum('bhcqd,bhckd->bhcqk', qb, k).astype(jnp.float32) * scale
        s = jnp.where(kpos[None, :] <= qpos[:, None], s, -jnp.inf)
        p = jax.nn.softmax(s, axis=-1)
        a = p[:, :, 0] - lam * p[:, :, 1]
        return jnp.einsum('bhqk,bhkd->bhqd', a.astype(v.dtype), v)

    out = lax.map(one_block, (split_blocks(q, 3), jnp.arange(s_len // Q_BLOCK)))
    return merge_blocks(out, 2)

def stick_breaking_attention(q, k, v):
    s_len = q.shape[2]
    kpos = jnp.arange(s_len)
    scale = HEAD_DIM ** -0.5

    def one_block(args):
        qb, i = args
        qpos = i * Q_BLOCK + jnp.arange(Q_BLOCK)
        z = jnp.einsum('bhqd,bhkd->bhqk', qb, k).astype(jnp.float32) * scale
        strict = kpos[None, :] < qpos[:, None]
        log_1m = jnp.where(strict, jax.nn.log_sigmoid(-z), 0.0)
        after = lax.cumsum(log_1m, axis=3, reverse=True) - log_1m
        w = jnp.where(strict, jnp.exp(jax.nn.log_sigmoid(z) + after), 0.0)
        return jnp.einsum('bhqk,bhkd->bhqd', w.astype(v.dtype), v)

    out = lax.map(one_block, (split_blocks(q, 2), jnp.arange(s_len // Q_BLOCK)))
    return merge_blocks(out, 2)

def causal_depthwise_conv(x, w, b):
    ch = x.shape[-1]
    y = lax.conv_general_dilated(x, w[:, None, :].astype(x.dtype), window_strides=(1,),
                                 padding=[(CONV_WIDTH - 1, 0)],
                                 dimension_numbers=('NWC', 'WIO', 'NWC'),
                                 feature_group_count=ch)
    return y + b

def setup_inputs(seed: int = 0) -> dict:
    key = jax.random.key(seed)
    ks = jax.random.split(key, 20)
    f32 = jnp.float32
    nrm = lambda k, shp, s: jax.random.normal(k, shp, f32) * s
    return {
        'x': nrm(ks[0], (BATCH, SEQ, D_MODEL), 1.0),
        'attn_norm_g': 1.0 + nrm(ks[1], (DEPTH, D_MODEL), 0.02),
        'w_in': nrm(ks[2], (DEPTH, D_MODEL, N_IN), D_MODEL ** -0.5),
        'forget_bias': 2.0 + nrm(ks[3], (DEPTH, H_FOX), 0.5),
        'lam_q1': nrm(ks[4], (DEPTH, HEAD_DIM), 0.1),
        'lam_k1': nrm(ks[5], (DEPTH, HEAD_DIM), 0.1),
        'lam_q2': nrm(ks[6], (DEPTH, HEAD_DIM), 0.1),
        'lam_k2': nrm(ks[7], (DEPTH, HEAD_DIM), 0.1),
        'diff_subln_g': 1.0 + nrm(ks[8], (DEPTH, DIFF_V_DIM), 0.02),
        'w_br_fox': nrm(ks[9], (DEPTH, W_FOX, D_MODEL), W_FOX ** -0.5),
        'w_br_diff': nrm(ks[10], (DEPTH, W_DIFF, D_MODEL), W_DIFF ** -0.5),
        'w_br_stick': nrm(ks[11], (DEPTH, W_STICK, D_MODEL), W_STICK ** -0.5),
        'w_out': nrm(ks[12], (DEPTH, D_MODEL, D_MODEL), D_MODEL ** -0.5),
        'ffn_norm_g': 1.0 + nrm(ks[13], (DEPTH, D_MODEL), 0.02),
        'w_up': nrm(ks[14], (DEPTH, D_MODEL, 2 * D_FF), D_MODEL ** -0.5),
        'conv_w': nrm(ks[15], (DEPTH, CONV_WIDTH, 2 * D_FF), CONV_WIDTH ** -0.5),
        'conv_b': nrm(ks[16], (DEPTH, 2 * D_FF), 0.02),
        'w_down': nrm(ks[17], (DEPTH, D_FF, D_MODEL), D_FF ** -0.5),
        'final_norm_g': 1.0 + nrm(ks[18], (D_MODEL,), 0.02),
    }

def reference(x, attn_norm_g, w_in, forget_bias, lam_q1, lam_k1, lam_q2, lam_k2, diff_subln_g,
              w_br_fox, w_br_diff, w_br_stick, w_out, ffn_norm_g, w_up, conv_w, conv_b, w_down,
              final_norm_g):
    f32 = jnp.float32
    b, s_len, _ = x.shape
    pos = jnp.arange(s_len, dtype=f32)
    inv_freq = ROPE_THETA ** (-jnp.arange(0, ROPE_DIM, 2, dtype=f32) / ROPE_DIM)
    ang = pos[:, None] * inv_freq[None, :]
    cos = jnp.cos(ang).astype(x.dtype)
    sin = jnp.sin(ang).astype(x.dtype)
    offs = np.cumsum(SPLITS)[:-1].tolist()

    for l in range(DEPTH):
        xn = rmsnorm(x, attn_norm_g[l])
        proj = xn @ w_in[l]
        fq, fk, fv, dq, dk, dv, sq, sk, sv, f_logit, g_logit = jnp.split(proj, offs, axis=-1)

        log_f = jax.nn.log_sigmoid(f_logit.astype(f32) + forget_bias[l].astype(f32)).transpose(0, 2, 1)
        o_fox = fox_attention(heads(fq, H_FOX, HEAD_DIM), heads(fk, H_FOX, HEAD_DIM),
                              heads(fv, H_FOX, HEAD_DIM), log_f)

        dq = partial_rope(dq.reshape(b, s_len, H_DIFF, 2, HEAD_DIM).transpose(0, 2, 3, 1, 4), cos, sin)
        dk = partial_rope(dk.reshape(b, s_len, H_DIFF, 2, HEAD_DIM).transpose(0, 2, 3, 1, 4), cos, sin)
        lam_init = 0.8 - 0.6 * math.exp(-0.3 * l)
        lam = (jnp.exp(jnp.sum(lam_q1[l].astype(f32) * lam_k1[l].astype(f32)))
               - jnp.exp(jnp.sum(lam_q2[l].astype(f32) * lam_k2[l].astype(f32))) + lam_init)
        o_diff = diff_attention(dq, dk, heads(dv, H_DIFF, DIFF_V_DIM), lam)
        o_diff = rmsnorm(o_diff, diff_subln_g[l]) * (1.0 - lam_init)

        o_stick = stick_breaking_attention(heads(sq, H_STICK, HEAD_DIM), heads(sk, H_STICK, HEAD_DIM),
                                           heads(sv, H_STICK, HEAD_DIM))

        gates = jax.nn.sigmoid(g_logit.astype(f32)).astype(x.dtype).reshape(b, s_len, N_BRANCH, D_MODEL)
        mixed = (gates[:, :, 0] * (merge_heads(o_fox) @ w_br_fox[l])
                 + gates[:, :, 1] * (merge_heads(o_diff) @ w_br_diff[l])
                 + gates[:, :, 2] * (merge_heads(o_stick) @ w_br_stick[l]))
        x = x + mixed @ w_out[l]

        hn = rmsnorm(x, ffn_norm_g[l])
        u = causal_depthwise_conv(hn @ w_up[l], conv_w[l], conv_b[l])
        u_gate, u_val = jnp.split(u, 2, axis=-1)
        x = x + (jax.nn.silu(u_gate) * u_val) @ w_down[l]

    return rmsnorm(x, final_norm_g)


_drawn_inputs = setup_inputs


def setup_inputs(seed=0):
    import zlib

    import numpy as np

    out = dict(_drawn_inputs(seed))
    spreads = {}
    factors = {'diff_subln_g': 5.201, 'ffn_norm_g': 2.912, 'conv_b': 2.925, 'final_norm_g': 2.908}
    for name, (base, spread) in spreads.items():
        noise = np.random.default_rng([zlib.crc32(name.encode()), seed]).standard_normal(out[name].shape)
        drawn = base * np.exp(spread * noise) if base else spread * noise
        out[name] = __import__('jax').numpy.asarray(drawn.astype(out[name].dtype))
    for name, factor in factors.items():
        out[name] = (out[name] * factor).astype(out[name].dtype)
    return out
```

```python
import math

import concourse.bass as bass
import numpy as np
from concourse import mybir

F32 = mybir.dt.float32
F32R = mybir.dt.float32r
BF16 = mybir.dt.bfloat16
ALU = mybir.AluOpType
ACT = mybir.ActivationFunctionType
AX = mybir.AxisListType

P = 128
D = 1024
S = 256
DEPTH = 2
HD = 64
MT = S // P
KC = D // P
COLS = 512
PIECE = 2 * COLS
RING = 6
QKV = 3072
QKV_BLOCKS = QKV // COLS
GATE_BLOCKS = 3 * D // COLS
OUT_BLOCKS = D // COLS
D_FF = 2816
STEPS = D_FF // (2 * P)
PER_BLOCK = 4
P_GATES = PER_BLOCK * QKV_BLOCKS
P_BRANCH = P_GATES + PER_BLOCK * GATE_BLOCKS
P_OUT = P_BRANCH + PER_BLOCK * OUT_BLOCKS
P_FFN = P_OUT + PER_BLOCK * OUT_BLOCKS
PIECES = P_FFN + 6 * STEPS
HALVES = QKV_BLOCKS + GATE_BLOCKS + OUT_BLOCKS
EPS = 1e-6
NEG = -1e30
UNITS = 8

STICK, FOX, DIFF = 0, 256, 1536
V_STICK, V_FOX, V_DIFF = 1024, 1280, 2560
G_ATTN, G_FFN, WF, FBIAS, SUBLN, NOW = 0, 8, 16, 48, 52, 180
CONV = NOW
PARAMS = CONV + 16 * STEPS
LAMS = 4 * HD
O_STICK, O_DIFF, O_FOX = 0, 256, 768

LAM_INIT = [0.8 - 0.6 * math.exp(-0.3 * l) for l in range(DEPTH)]

QUARTERS = [(0, 0), (0, 1), (1, 0), (1, 1), (0, 2), (0, 3), (1, 2), (1, 3)]

TICKS = 8 * 3
D0, D1, SB, FX = range(4)
UNIT_TICKS = [(2, 4, 8, 10), (7, 9, 13, 15), (11, 13, 17, 20), (15, 17, 21, 23)]
SUBLN_TICK = 18
IN_TURN = 2 * 4 + 2 + 6
SOFT = {D0: 0, D1: 1, FX: 2}
TURNS = {D0: 0, D1: 1, FX: 2}
SPLIT_TICKS = [3, 5, 7, 9, 11, 13, 15, 17, 19, 21, 23, 24]


class Tally:

    def __init__(self, sem):
        self.sem, self.base, self.n = sem, 0, 0

    def link(self, eng, ins):
        ins.then_inc(self.sem, 1)
        self.n += 1
        eng.wait_ge(self.sem, self.base + self.n)

    def enter(self, i, per_turn):
        kept = (self.base, self.n)
        self.base, self.n = self.base + self.n + i * per_turn, 0
        return kept

    def leave(self, kept, turns, per_turn):
        assert self.n == per_turn, (self.n, per_turn)
        self.base, self.n = kept[0], kept[1] + turns * per_turn


def build(nc, x_in, stream, params, lam_rows, rope_in, g_final, out):
    def sb(name, shape, dt=F32):
        return nc.alloc_sbuf_tensor(name, shape, dt)

    def sem(name):
        return nc.alloc_semaphore(name)

    raw = sb("raw", [P, RING, PIECE])
    w_hi = sb("w_hi", [P, RING, PIECE], F32R)
    w_lo = sb("w_lo", [P, RING, PIECE], F32R)
    x = sb("x", [P, MT, D])
    a_hi = sb("a_hi", [P, KC, S], F32R)
    a_lo = sb("a_lo", [P, KC, S], F32R)
    b_hi = sb("b_hi", [P, KC, S], F32R)
    b_lo = sb("b_lo", [P, KC, S], F32R)
    qkv = sb("qkv", [P, MT, QKV])
    gates = sb("gates", [P, MT, 3 * D])
    rows = sb("rows", [P, MT, D])
    o_all = sb("o_all", [P, MT, D])
    all_params = sb("all_params", [P, DEPTH, PARAMS])
    now = sb("now", [P, NOW])
    taps = sb("taps", [P, 2, 16])
    wf_hi = sb("wf_hi", [P, 4 * KC], F32R)
    wf_lo = sb("wf_lo", [P, 4 * KC], F32R)
    rope = sb("rope", [P, 2, 64])
    staged = sb("staged", [P, 2, 2 * MT * P])
    turned = sb("turned", [P, 2, 4 * P])
    prob = sb("prob", [P, 2, 2, 384])
    prob_t = rows[:, :, 0:768].rearrange("p u (c n) -> p u c n", c=2)
    square = rows[:, :, 768:D]
    decay = sb("decay", [P, 2, 3 * P])
    logf = sb("logf", [P, 3, 8])
    stats = sb("stats", [P, 2, 3, 4])
    norm = sb("norm", [P, 5, 8])
    rinv = sb("rinv", [P, 8])
    r_tok = sb("r_tok", [P, 4])
    r_row = sb("r_row", [P, S])
    lam_in = sb("lam_in", [P, DEPTH, LAMS])
    lam_first = sb("lam_first", [P, DEPTH, 2])
    lam = sb("lam", [P, 8])
    eps = sb("eps", [P, 2])
    ident = sb("ident", [P, P])
    ident_bf = sb("ident_bf", [P, P], BF16)
    mask_bf = sb("mask_bf", [P, P], BF16)
    later_bf = sb("later_bf", [P, P], BF16)
    later = sb("later", [P, P])
    tri_ones = sb("tri_ones", [P, 2 * P])
    ones_later = sb("ones_later", [P, 2 * P])
    neg_from = sb("neg_from", [P, 2 * P])
    zero_bf = sb("zero_bf", [P, COLS], BF16)
    conv = gates[:, 0, 0:2048].rearrange("p (s c g t) -> p s c g t", s=2, c=2, g=2)
    squash = gates[:, 1, 0:1024].rearrange("p (s c t) -> p s c t", s=2, c=2)
    g_fin = gates[:, 1, 2048:3072]
    hidden = gates[:, 0, 2048:3072].rearrange("p (c g t) -> p c g t", c=2, g=2)
    gated = [[qkv[:, m, b * COLS:(b + 1) * COLS] for b in range(3)] for m in range(MT)]

    ps = [nc.alloc_psum_tensor(f"bank{b}", [P, COLS], F32) for b in range(8)]
    QK_BANK, OUT_BANK = 2, 7
    ATTN_BANKS, FFN_BANKS = (2, 3, 4, 5), (6, 7, 4, 5)
    O_BANKS, MIXED_BANKS = (2, 3, 4, 7), (0, 1, 4, 5)

    def score_bank(unit, c):
        return ps[3 + 2 * (unit % 2) + c]

    raw_landed = [sem(f"raw_landed{i}") for i in range(RING)]
    landed_uses = [len(range(i, PIECES, RING)) for i in range(RING)]
    hi_ready = sem("hi_ready")
    split_done = sem("split_done")
    piece_used = sem("piece_used")
    x_loaded = sem("x_loaded")
    params_loaded = sem("params_loaded")
    g_loaded = sem("g_loaded")
    consts_ready = sem("consts_ready")
    lam_sums = sem("lam_sums")
    lam_exps = sem("lam_exps")
    ident_ready = sem("ident_ready")
    x_ready = sem("x_ready")
    mix_added = sem("mix_added")
    squares_ready = sem("squares_ready")
    guess_ready = sem("guess_ready")
    x_turned = sem("x_turned")
    r_ready = sem("r_ready")
    r_spread = sem("r_spread")
    r_row_ready = sem("r_row_ready")
    norm_hi = sem("norm_hi")
    norm_lo = sem("norm_lo")
    now_ready = sem("now_ready")
    half_ready = sem("half_ready")
    block_read = sem("block_read")
    wf_ready = sem("wf_ready")
    f_ready = sem("f_ready")
    f_biased = sem("f_biased")
    f_logs = sem("f_logs")
    logf_ready = sem("logf_ready")
    unit_staged = sem("unit_staged")
    unit_turned = sem("unit_turned")
    turned_ready = sem("turned_ready")
    scores_ready = sem("scores_ready")
    max_ready = sem("max_ready")
    exps_done = sem("exps_done")
    prob_ready = sem("prob_ready")
    prob_turned = sem("prob_turned")
    prob_t_ready = sem("prob_t_ready")
    stick_logs = sem("stick_logs")
    stick_softplus = sem("stick_softplus")
    stick_masked = sem("stick_masked")
    stick_sums = sem("stick_sums")
    stick_exps = sem("stick_exps")
    decay_ready = sem("decay_ready")
    unit_done = sem("unit_done")
    out_read = sem("out_read")
    subln_squares = sem("subln_squares")
    subln_guess = sem("subln_guess")
    diff_ready = sem("diff_ready")
    o_turned = sem("o_turned")
    o_hi = sem("o_hi")
    o_lo = sem("o_lo")
    gates_ready = sem("gates_ready")
    branch_ready = sem("branch_ready")
    branch_read = sem("branch_read")
    mixed_ready = sem("mixed_ready")
    mixed_turned = sem("mixed_turned")
    mixed_hi = sem("mixed_hi")
    mixed_lo = sem("mixed_lo")
    taps_ready = sem("taps_ready")
    conv_begun = sem("conv_begun")
    up_read = sem("up_read")
    conv_done = sem("conv_done")
    tanh_done = sem("tanh_done")
    h_ready = sem("h_ready")
    h_hi = sem("h_hi")
    h_lo = sem("h_lo")
    down_ready = sem("down_ready")
    y_ready = sem("y_ready")
    y_stored = sem("y_stored")
    act_step = Tally(sem("act_step"))
    dve_step = Tally(sem("dve_step"))
    pool_step = Tally(sem("pool_step"))

    def pair(hi_lo, i):
        return hi_lo[:, 2 * i:2 * i + 2, :].rearrange("p k t -> p (k t)")

    def gate_cols(m, j):
        return gates[:, m, :].rearrange("p (b n) -> p b n", b=3)[:, :, j * COLS:(j + 1) * COLS]

    def diagonals(tile):
        return tile.rearrange("p (b n) -> p b n", b=3)[:, 0:3:2, :]

    block = nc.Block()
    block.__enter__()

    @block.sync
    def _(sp):
        sp.dma_start(x[:, 0, :], x_in[0:P, :]).then_inc(x_loaded, 16)
        sp.dma_start(x[:, 1, :], x_in[P:S, :]).then_inc(x_loaded, 16)

        def load(l, n, slot, free):
            sp.wait_ge(split_done, free)
            sp.dma_start(raw[:, slot, :], stream[bass.ds(l * PIECES + n, 1)].rearrange("a p n -> (a p) n")) \
                .then_inc(raw_landed[slot], 16)

        with sp.Fori(0, DEPTH) as l:
            for k in range(RING):
                load(l, k, k, l * PIECES + RING + min(k + 1 - PIECES % RING, 0))
            with sp.Fori(1, PIECES // RING) as r:
                for k in range(RING):
                    load(l, r * RING + k, k, l * PIECES + r * RING + k + 1)
            for k in range(PIECES % RING):
                n = PIECES - PIECES % RING + k
                load(l, n, k, l * PIECES + n + 1)
        sp.wait_ge(mix_added, 4 * DEPTH)
        sp.dma_start(g_fin, g_final.partition_broadcast(P)).then_inc(g_loaded, 16)
        for m in range(MT):
            sp.wait_ge(y_ready, m + 1)
            sp.dma_start(out[m * P:(m + 1) * P, :], rows[:, m, :]).then_inc(y_stored, 16)
        sp.wait_ge(y_stored, 16 * MT)

    @block.gpsimd
    def _(pool):
        g = nc.gpsimd
        pool_step.link(pool, g.memset(ident[:], 0.0))

        def cut(tile, op, fill, row, col):
            return g.affine_select(out=tile, in_=tile, pattern=[[col, P]], compare_op=op, fill=fill,
                                   base=0, channel_multiplier=row)

        cut(ident[:], ALU.not_equal, 1.0, 1, -1).then_inc(ident_ready, 1)
        for l in range(DEPTH):
            g.memset(lam_first[:, l, 0:1], -LAM_INIT[l])
            g.memset(lam_first[:, l, 1:2], 1.0 - LAM_INIT[l])
        for tile, value in ((eps, EPS), (ident_bf, 0.0), (mask_bf, 0.0), (later_bf, 0.0), (later, 1.0),
                            (tri_ones, 1.0), (ones_later, 1.0), (neg_from, -1.0), (zero_bf, 0.0)):
            last = g.memset(tile[:], value)
        pool_step.link(pool, last)
        cut(ident_bf[:], ALU.not_equal, 1.0, 1, -1)
        cut(mask_bf[:], ALU.is_ge, NEG, 1, -1)
        cut(later_bf[:], ALU.is_gt, NEG, -1, 1)
        cut(later[:], ALU.is_gt, 0.0, -1, 1)
        cut(tri_ones[:, 0:P], ALU.is_ge, 0.0, -1, 1)
        cut(ones_later[:, P:2 * P], ALU.is_gt, 0.0, 1, -1)
        cut(neg_from[:, 0:P], ALU.is_ge, 0.0, 1, -1).then_inc(consts_ready, 1)

        def stage(u, unit, q_col):
            pool.wait_ge(unit_turned, unit + 1)
            dst = staged[:, u % 2, :].rearrange("p (a m n) -> p a m n", a=2, m=MT)
            for a in range(2):
                ins = g.tensor_copy(dst[:, a], qkv[:, :, bass.ds(q_col + a * COLS, P)])
            return ins

        def rotate(u):
            t = staged[:, u % 2, :].rearrange("p (g n) -> p g n", n=HD)
            t1, t2 = t[:, :, 0:8], t[:, :, 8:16]
            cos, sin = (rope[:, i, :].rearrange("p (g n) -> p g n", n=8) for i in range(2))
            p = [rope_tmp[:, i, :].rearrange("p (g n) -> p g n", n=8) for i in range(4)]
            g.tensor_tensor(p[0], t1, cos, ALU.mult)
            g.tensor_tensor(p[1], t2, sin, ALU.mult)
            g.tensor_tensor(p[2], t2, cos, ALU.mult)
            pool_step.link(pool, g.tensor_tensor(p[3], t1, sin, ALU.mult))
            g.tensor_tensor(t1, p[0], p[1], ALU.subtract)
            return g.tensor_tensor(t2, p[2], p[3], ALU.add)

        rope_tmp = sb("rope_tmp", [P, 4, 64])

        def keep_later(tile):
            d = diagonals(tile)
            return g.tensor_tensor(d, d, later[:].unsqueeze(1).broadcast_to([P, 2, P]), ALU.mult)

        def attention_turn(l, i):
            unit = UNITS * l + 4 * i
            pool.wait_ge(block_read, 2 + 2 * ((QKV_BLOCKS + GATE_BLOCKS) * l + QKV_BLOCKS))
            for u in (D0, D1):
                pool_step.link(pool, stage(u, unit + u, DIFF + 2 * P * i + P * u))
                rotate(u).then_inc(unit_staged, 1)
            stage(SB, unit + SB, STICK + P * i).then_inc(unit_staged, 1)
            stage(FX, unit + FX, FOX + P * i).then_inc(unit_staged, 1)
            for c in range(2):
                pool.wait_ge(stick_softplus, 4 * l + 2 * i + c + 1)
                keep_later(prob_t[:, 0, c, :]).then_inc(stick_masked, 1)

        def merge(l, j, m):
            pool.wait_ge(branch_read, 12 * l + 6 * j + 3 * m + 3)
            stick, diff, fox = gated[m]
            pool_step.link(pool, g.tensor_tensor(stick, stick, diff, ALU.add))
            g.tensor_tensor(rows[:, m, j * COLS:(j + 1) * COLS], stick, fox, ALU.add).then_inc(mixed_ready, 1)

        def step_taps(l, s, par):
            pool.wait_ge(conv_done, 2 * (l * STEPS + s) + 2)
            g.tensor_copy(taps[:, par, :], all_params[:, bass.ds(l, 1), bass.ds(s * 16 + CONV, 16)]
                          .rearrange("p a n -> p (a n)")).then_inc(taps_ready, 1)

        pool.wait_ge(params_loaded, 16 * 3)
        with pool.Fori(0, DEPTH) as l:
            per_layer = 2 * 4 + MT * OUT_BLOCKS
            kept = pool_step.enter(l, per_layer)
            g.tensor_copy(now[:], all_params[:, bass.ds(l, 1), 0:NOW].rearrange("p a n -> p (a n)")) \
                .then_inc(now_ready, 1)
            with pool.Fori(0, 2) as i:
                kept_turn = pool_step.enter(i, 4)
                attention_turn(l, i)
                pool_step.leave(kept_turn, 2, 4)
            for j in range(OUT_BLOCKS):
                for m in range(MT):
                    merge(l, j, m)
            pool.wait_ge(norm_lo, 4 * (2 * l + 2))
            step_taps(l, 0, 0)
            with pool.Fori(0, 4) as i:
                for k in range(2):
                    step_taps(l, 2 * i + k + 1, (k + 1) % 2)
            for s in (STEPS - 2, STEPS - 1):
                step_taps(l, s, s % 2)
            pool_step.leave(kept, DEPTH, per_layer)

    @block.scalar
    def _(act):
        a = nc.scalar

        def round_piece(l, n, slot, r, free=None):
            act.wait_ge(raw_landed[slot], 16 * (l * landed_uses[slot] + r + 1))
            act.wait_ge(piece_used, l * PIECES + n + 1 if free is None else free)
            a.activation(w_hi[:, slot, :], raw[:, slot, :], ACT.Copy).then_inc(hi_ready, 1)

        def ahead(l, used, i=0, per=0):
            n = used + RING
            if n < PIECES:
                round_piece(l, n + i * per, n % RING, n // RING + i * (per // RING))

        def norm_stats(n, ready, value):
            act.wait_ge(ready, value)
            for m in range(MT):
                last = a.activation(rows[:, m, :], x[:, m, :], ACT.Square, accum_out=norm[:, 0, m:m + 1])
            last.then_inc(squares_ready, 1)

        def norm_guess(n):
            act.wait_ge(squares_ready, n + 1)
            act_step.link(act, a.activation(norm[:, 2, 0:MT], norm[:, 0, 0:MT], ACT.Ln, bias=eps[:, 0:1],
                                            scale=1.0 / D))
            a.activation(norm[:, 3, 0:MT], norm[:, 2, 0:MT], ACT.Exp, scale=-0.5).then_inc(guess_ready, 1)

        def norm_round(n, i, banks, dst, gain):
            act.wait_ge(x_turned, 4 * n + i + 1)
            for k in range(2):
                kc = 2 * i + k
                ins = a.activation(dst[:, kc, :], ps[banks[i]][:, k * S:(k + 1) * S], ACT.Copy,
                                   scale=now[:, gain + kc:gain + kc + 1])
            ins.then_inc(norm_hi, 1)

        def read_block(l, b, m, piece, dst, factor):
            if m == 0:
                act.wait_ge(half_ready, HALVES * l + b + 1)
            else:
                act.wait_ge(piece_used, RING + PIECES * l + piece + PER_BLOCK)
            a.activation(dst, ps[m][:], ACT.Copy, scale=r_tok[:, factor + m:factor + m + 1]).then_inc(block_read, 1)

        def read_turned(unit, u):
            act.wait_ge(unit_turned, 2 + unit + 1)
            a.activation(turned[:, u % 2, :], ps[QK_BANK][:], ACT.Copy).then_inc(turned_ready, 1)

        def softmax_exp(l, i, u, c):
            k = 6 * l + 3 * i + SOFT[u]
            act.wait_ge(max_ready, 2 * k + c + 1)
            sc = score_bank(u, c)
            for q, (lo, hi) in enumerate(((0, P), (P, 3 * P))):
                col = 2 * c + q
                ins = a.activation(prob[:, u % 2, c, lo:hi], sc[:, lo:hi], ACT.Exp,
                                   bias=stats[:, u % 2, 0, col:col + 1],
                                   accum_out=stats[:, u % 2, 1, col:col + 1])
            ins.then_inc(exps_done, 1)

        def read_prob(k, u, c):
            act.wait_ge(prob_turned, k + 1)
            a.activation(prob_t[:, u % 2, c, :], score_bank(u, c)[:, 0:384], ACT.Copy).then_inc(prob_t_ready, 1)

        def read_out(unit, col):
            act.wait_ge(unit_done, unit + 1)
            a.activation(o_all[:, :, bass.ds(col, P)], ps[OUT_BANK][:, 0:2 * P].rearrange("p (m n) -> p m n", m=MT),
                         ACT.Copy).then_inc(out_read, 1)

        def stick_log(l, i, c):
            act.wait_ge(scores_ready, 2 * (UNITS * l + 4 * i + SB) + c + 1)
            t = prob[:, 0, c, :]
            act_step.link(act, a.activation(t, score_bank(0, c)[:, 0:384], ACT.Abs))
            act_step.link(act, a.activation(t, t, ACT.Exp, scale=-1.0))
            a.activation(t, t, ACT.Ln, bias=1.0).then_inc(stick_logs, 1)

        def stick_exp(l, i, c):
            act.wait_ge(stick_sums, 4 * l + 2 * i + c + 1)
            a.activation(prob[:, 0, c, :], score_bank(0, c)[:, 0:384], ACT.Exp).then_inc(stick_exps, 1)

        def round_pair(ready, value, bank, dst, i, done):
            act.wait_ge(ready, value)
            a.activation(pair(dst, i), ps[bank][:], ACT.Copy).then_inc(done, 1)

        def conv_begin(l, s, par, p):
            act.wait_ge(up_read, 4 + 2 * (STEPS * l + s) + p + 1)
            if p == 0:
                act.wait_ge(taps_ready, STEPS * l + s + 1)
            for g in range(2):
                c = 4 * (2 * p + g)
                ins = a.activation(conv[:, par, p, g, :], hidden[:, p, g, :], ACT.Identity,
                                   scale=taps[:, par, c + 2:c + 3], bias=taps[:, par, c + 3:c + 4])
            ins.then_inc(conv_begun, 1)

        def gate_tanh(l, s, par, p):
            act.wait_ge(conv_done, 4 + 2 * (STEPS * l + s) + p + 1)
            a.activation(squash[:, par, p, :], conv[:, par, p, 0, :], ACT.Tanh, scale=0.5).then_inc(tanh_done, 1)

        def round_h(l, s, par, p):
            act.wait_ge(h_ready, 2 * (STEPS * l + s) + p + 1)
            a.activation(a_hi[:, 2 * par + p, :], conv[:, par, p, 0, :], ACT.Copy).then_inc(h_hi, 1)

        def finish_step(l, s, par, j):
            if j == 0:
                gate_tanh(l, s, par, 1)
            if j == 1:
                round_h(l, s, par, 0)
            if j == 2:
                round_h(l, s, par, 1)

        def mlp_step(l, s, par, used):
            first, i, per, count = used
            for j in range(6):
                if j < count:
                    ahead(l, first + j, i, per)
                if count == 6:
                    finish_step(l, s - 1, 1 - par, j)
                if j == 3:
                    conv_begin(l, s, par, 0)
                if j == 4:
                    conv_begin(l, s, par, 1)
                if j == 5:
                    gate_tanh(l, s, par, 0)

        act.dma_start(all_params[:], params).then_inc(params_loaded, 16)
        act.dma_start(rope[:], rope_in).then_inc(params_loaded, 16)
        act.dma_start(lam_in[:], lam_rows.partition_broadcast(P)).then_inc(params_loaded, 16)
        act.sem_inc(block_read, 2)

        with act.Fori(0, DEPTH) as l:
            per_layer = 1 + 2 + 2 * 5 + 1
            kept = act_step.enter(l, per_layer)
            n1, n2 = 2 * l, 2 * l + 1
            a.preload_act_table_set("natural_log_exp_and_others")
            round_piece(l, 0, 0, 0, free=l * PIECES + RING)
            act.wait_ge(now_ready, l + 1)
            for k in range(4):
                norm_round(n1, k, ATTN_BANKS, a_hi, G_ATTN)
                if k < 3:
                    round_piece(l, k + 1, k + 1, 0, free=l * PIECES + RING)
            norm_stats(n1, x_ready, 4 * l + 4)
            round_piece(l, 4, 4, 0, free=l * PIECES + RING)
            norm_guess(n1)
            round_piece(l, 5, 5, 0, free=l * PIECES + RING)
            act.wait_ge(r_ready, n1 + 1)
            with act.Fori(0, 2) as i:
                for b in range(3):
                    B = 3 * i + b
                    for j in range(PER_BLOCK):
                        ahead(l, PER_BLOCK * b + j, i, 3 * PER_BLOCK)
                        if j >= 2:
                            read_block(l, B, j - 2, PER_BLOCK * B, qkv[:, j - 2, bass.ds(B * COLS, COLS)],
                                       2 if b == 0 else 0)
            act.wait_ge(lam_sums, l + 1)
            a.activation(lam[:, 2:4], lam[:, 0:2], ACT.Exp).then_inc(lam_exps, 1)
            act.wait_ge(f_biased, l + 1)
            act_step.link(act, a.activation(logf[:, 1, :], logf[:, 0, :], ACT.Abs))
            act_step.link(act, a.activation(logf[:, 1, :], logf[:, 1, :], ACT.Exp, scale=-1.0))
            a.activation(logf[:, 1, :], logf[:, 1, :], ACT.Ln, bias=1.0).then_inc(f_logs, 1)
            with act.Fori(0, 2) as i:
                kept_turn = act_step.enter(i, 5)
                unit = UNITS * l + 4 * i
                for tick in range(TICKS + 1):
                    for u, (turn, score, third, values) in enumerate(UNIT_TICKS):
                        if tick == turn:
                            read_turned(unit + u, u)
                        if u == SB:
                            if tick in (score, score + 1):
                                stick_log(l, i, tick - score)
                            if tick == third:
                                stick_exp(l, i, 0)
                                stick_exp(l, i, 1)
                        else:
                            if tick in (score, score + 1):
                                softmax_exp(l, i, u, tick - score)
                            if tick == third:
                                k = 8 * l + 4 * i + TURNS[u]
                                for c in range(2 if u == FX else 1):
                                    read_prob(k + c, u, c)
                        if tick == values:
                            col = (O_DIFF + 2 * P * i, O_DIFF + 2 * P * i + P, O_STICK + P * i, O_FOX + P * i)[u]
                            read_out(unit + u, col)
                    if tick == SUBLN_TICK:
                        act.wait_ge(subln_squares, 2 * l + i + 1)
                        act_step.link(act, a.activation(norm[:, 2, 0:4], norm[:, 0, 0:4], ACT.Ln,
                                                        bias=eps[:, 0:1], scale=1.0 / (2 * HD)))
                        a.activation(norm[:, 3, 0:4], norm[:, 2, 0:4], ACT.Exp, scale=-0.5) \
                            .then_inc(subln_guess, 1)
                    if tick % 8 in (6, 0) and tick:
                        b, m = (tick - 1) // 8, int(tick % 8 == 0)
                        B = QKV_BLOCKS + 3 * i + b
                        read_block(l, B, m, PER_BLOCK * B, gates[:, m, bass.ds((3 * i + b) * COLS, COLS)], 0)
                    for j in range(3 * PER_BLOCK):
                        if SPLIT_TICKS[j] == tick:
                            ahead(l, P_GATES + j, i, 3 * PER_BLOCK)
                act_step.leave(kept_turn, 2, 5)
            a.preload_act_table_set("exp_and_others")
            for i in range(4):
                round_pair(o_turned, 4 * l + i + 1, O_BANKS[i], b_hi, i, o_hi)
            for j in range(OUT_BLOCKS):
                for m in range(MT):
                    g = gate_cols(m, j)
                    a.activation(g, g, ACT.Tanh, scale=0.5).then_inc(gates_ready, 1)
                for k in range(2):
                    ahead(l, P_BRANCH + PER_BLOCK * j + k)
                if j == 1:
                    for i in range(2):
                        round_pair(mixed_turned, 4 * l + i + 1, i, a_hi, i, mixed_hi)
                for k in range(2, PER_BLOCK):
                    ahead(l, P_BRANCH + PER_BLOCK * j + k)
            ahead(l, P_OUT)
            ahead(l, P_OUT + 1)
            for i in (2, 3):
                round_pair(mixed_turned, 4 * l + i + 1, 2 + i, a_hi, i, mixed_hi)
            for k in range(2, 7):
                ahead(l, P_OUT + k)
                if k >= 5:
                    norm_round(n2, k - 5, FFN_BANKS, b_hi, G_FFN)
            norm_round(n2, 2, FFN_BANKS, b_hi, G_FFN)
            norm_round(n2, 3, FFN_BANKS, b_hi, G_FFN)
            norm_stats(n2, mix_added, 4 * l + 4)
            a.preload_act_table_set("natural_log_exp_and_others")
            norm_guess(n2)
            a.preload_act_table_set("exp_and_others")
            ahead(l, P_OUT + 7)
            act.wait_ge(r_spread, l + 1)
            a.activation(r_row[:], ps[6][:, 0:S], ACT.Copy).then_inc(r_row_ready, 1)
            mlp_step(l, 0, 0, (P_FFN, 0, 0, 4))
            with act.Fori(0, 4) as i:
                for k in range(2):
                    mlp_step(l, 2 * i + k + 1, (k + 1) % 2, (P_FFN + 4 + 6 * k, i, 12, 6))
            for s in (STEPS - 2, STEPS - 1):
                mlp_step(l, s, s % 2, (P_FFN + 4 + 6 * (s - 1), 0, 0, 6))
            for j in range(3):
                finish_step(l, STEPS - 1, (STEPS - 1) % 2, j)
            act_step.leave(kept, DEPTH, per_layer)
        a.preload_act_table_set("natural_log_exp_and_others")
        norm_stats(2 * DEPTH, x_ready, 4 * DEPTH + 4)
        norm_guess(2 * DEPTH)

    @block.vector
    def _(dve):
        v = nc.vector

        def rest(l, n, slot):
            dve.wait_ge(hi_ready, l * PIECES + n + 1)
            v.tensor_tensor(w_lo[:, slot, :], raw[:, slot, :], w_hi[:, slot, :].bitcast(F32), ALU.subtract) \
                .then_inc(split_done, 1)

        def ahead(l, used, i=0, per=0):
            n = used + RING
            if n < PIECES:
                rest(l, n + i * per, n % RING)

        def newton(cols):
            guess, mean, t = norm[:, 3, 0:cols], norm[:, 1, 0:cols], norm[:, 4, 0:cols]
            dve_step.link(dve, v.tensor_tensor(t, guess, guess, ALU.mult))
            dve_step.link(dve, v.tensor_tensor(t, t, mean, ALU.mult))
            dve_step.link(dve, v.tensor_scalar(t, t, -0.5, 1.5, ALU.mult, ALU.add))
            dve_step.link(dve, v.tensor_tensor(rinv[:, 0:cols], guess, t, ALU.mult))

        def norm_factor(n):
            dve.wait_ge(squares_ready, n + 1)
            dve_step.link(dve, v.tensor_scalar(norm[:, 1, 0:MT], norm[:, 0, 0:MT], 1.0 / D, EPS, ALU.mult, ALU.add))
            dve.wait_ge(guess_ready, n + 1)
            newton(MT)

        def keep_factor():
            v.tensor_copy(r_tok[:, 0:MT], rinv[:, 0:MT])
            v.tensor_scalar(r_tok[:, MT:2 * MT], rinv[:, 0:MT], HD ** -0.5, None, ALU.mult).then_inc(r_ready, 1)

        def norm_rest(n, i, banks, hi, lo, gain):
            dve.wait_ge(norm_hi, 4 * n + i + 1)
            for k in range(2):
                kc = 2 * i + k
                ins = v.scalar_tensor_tensor(out=lo[:, kc, :], in0=ps[banks[i]][:, k * S:(k + 1) * S],
                                             scalar=now[:, gain + kc:gain + kc + 1],
                                             in1=hi[:, kc, :].bitcast(F32), op0=ALU.mult, op1=ALU.subtract)
            ins.then_inc(norm_lo, 1)

        def rest_pair(ready, value, bank, hi, lo, i, done):
            dve.wait_ge(ready, value)
            v.tensor_tensor(pair(lo, i), ps[bank][:], pair(hi, i).bitcast(F32), ALU.subtract).then_inc(done, 1)

        def decays(l, i):
            dve.wait_ge(logf_ready, l + 1)
            for c in range(2):
                head = 2 * i + c
                v.tensor_scalar(decay[:, c, 0:2 * P], tri_ones[:], logf[:, 2, bass.ds(head, 1)], None, ALU.mult)
                ins = v.tensor_scalar(decay[:, c, 2 * P:3 * P], tri_ones[:, 0:P], logf[:, 2, bass.ds(head + 4, 1)],
                                      None, ALU.mult)
            ins.then_inc(decay_ready, 1)

        def softmax_max(l, i, u, c):
            dve.wait_ge(scores_ready, 2 * (UNITS * l + 4 * i + u) + c + 1)
            sc = score_bank(u, c)
            for q, (lo, hi) in enumerate(((0, P), (P, 3 * P))):
                col = 2 * c + q
                ins = v.tensor_reduce(stats[:, u % 2, 0, col:col + 1], sc[:, lo:hi], AX.X, ALU.max, negate=True)
            ins.then_inc(max_ready, 1)

        def softmax_scale(l, i, u, c):
            dve.wait_ge(exps_done, 2 * (6 * l + 3 * i + SOFT[u]) + c + 1)
            r = stats[:, u % 2, 2, 2 * c:2 * c + 2]
            dve_step.link(dve, v.reciprocal(r, stats[:, u % 2, 1, 2 * c:2 * c + 2]))
            parts = ((0, P), (P, 3 * P))
            if u != FX and c == 1:
                dve_step.link(dve, v.tensor_scalar(r, r, lam[:, 7:8], None, ALU.mult))
                for q, (lo, hi) in enumerate(parts):
                    ins = v.scalar_tensor_tensor(out=prob[:, u % 2, 0, lo:hi], in0=prob[:, u % 2, 1, lo:hi],
                                                 scalar=r[:, q:q + 1], in1=prob[:, u % 2, 0, lo:hi],
                                                 op0=ALU.mult, op1=ALU.add)
            else:
                for q, (lo, hi) in enumerate(parts):
                    p = prob[:, u % 2, c, lo:hi]
                    ins = v.tensor_scalar(p, p, r[:, q:q + 1], None, ALU.mult)
            if u == FX or c == 1:
                ins.then_inc(prob_ready, 1)
            else:
                dve_step.link(dve, ins)

        def subln_square(l, i):
            dve.wait_ge(out_read, UNITS * l + 4 * i + D1 + 1)
            both = o_all[:, :, bass.ds(O_DIFF + 2 * P * i, 2 * P)]
            dve_step.link(dve, v.tensor_tensor(square, both, both, ALU.mult))
            v.tensor_reduce(norm[:, 0, 0:4].rearrange("p (m h) -> p m h", m=MT),
                            square.rearrange("p m (h n) -> p m h n", h=2), AX.X, ALU.add).then_inc(subln_squares, 1)

        def subln_scale(l, i):
            dve.wait_ge(subln_squares, 2 * l + i + 1)
            dve_step.link(dve, v.tensor_scalar(norm[:, 1, 0:4], norm[:, 0, 0:4], 1.0 / (2 * HD), EPS,
                                               ALU.mult, ALU.add))
            dve.wait_ge(subln_guess, 2 * l + i + 1)
            newton(4)
            for m in range(MT):
                for h in range(2):
                    o = o_all[:, m, bass.ds(O_DIFF + 2 * P * i + P * h, P)]
                    ins = v.scalar_tensor_tensor(out=o, in0=o, scalar=rinv[:, 2 * m + h:2 * m + h + 1],
                                                 in1=now[:, SUBLN:SUBLN + P], op0=ALU.mult, op1=ALU.mult)
            ins.then_inc(diff_ready, 1)

        def softplus(l, i, c):
            dve.wait_ge(stick_logs, 4 * l + 2 * i + c + 1)
            v.scalar_tensor_tensor(out=prob_t[:, 0, c, :], in0=score_bank(0, c)[:, 0:384], scalar=0.0,
                                   in1=prob[:, 0, c, :], op0=ALU.max, op1=ALU.add).then_inc(stick_softplus, 1)

        def scale_hidden(l, s, par, p, piece):
            dve.wait_ge(piece_used, RING + PIECES * l + piece + 2 * p + 2)
            dve.wait_ge(r_row_ready, l + 1)
            v.tensor_tensor(hidden[:, p], ps[2 * par + p][:].rearrange("p (g t) -> p g t", g=2),
                            r_row[:].unsqueeze(1).broadcast_to([P, 2, S]), ALU.mult).then_inc(up_read, 1)

        def conv_finish(l, s, par, p):
            dve.wait_ge(conv_begun, 2 * (STEPS * l + s) + p + 1)
            for tap in (1, 0):
                back = 2 - tap
                for g in range(2):
                    c = 4 * (2 * p + g)
                    y = conv[:, par, p, g, back:S]
                    ins = v.scalar_tensor_tensor(out=y, in0=hidden[:, p, g, 0:S - back],
                                                 scalar=taps[:, par, c + tap:c + tap + 1], in1=y,
                                                 op0=ALU.mult, op1=ALU.add)
                if tap:
                    dve_step.link(dve, ins)
            ins.then_inc(conv_done, 1)

        def gate_value(l, s, par, p):
            dve.wait_ge(tanh_done, 2 * (STEPS * l + s) + p + 1)
            t, gate, value = squash[:, par, p, :], conv[:, par, p, 0, :], conv[:, par, p, 1, :]
            dve_step.link(dve, v.scalar_tensor_tensor(out=t, in0=t, scalar=1.0, in1=gate, op0=ALU.add, op1=ALU.mult))
            v.tensor_tensor(gate, t, value, ALU.mult).then_inc(h_ready, 1)

        def rest_h(l, s, par, p):
            dve.wait_ge(h_hi, 2 * (STEPS * l + s) + p + 1)
            v.tensor_tensor(a_lo[:, 2 * par + p, :], conv[:, par, p, 0, :], a_hi[:, 2 * par + p, :].bitcast(F32),
                            ALU.subtract).then_inc(h_lo, 1)

        def finish_step(l, s, par, j):
            if j == 0:
                gate_value(l, s, par, 0)
            if j == 1:
                gate_value(l, s, par, 1)
            if j == 2:
                rest_h(l, s, par, 0)
            if j == 3:
                rest_h(l, s, par, 1)

        def mlp_step(l, s, par, used):
            first, i, per, count = used
            for j in range(6):
                if j < count:
                    ahead(l, first + j, i, per)
                if count == 6:
                    finish_step(l, s - 1, 1 - par, j)
                if j in (2, 3):
                    scale_hidden(l, s, par, j - 2, first + i * per)
                if j in (4, 5):
                    conv_finish(l, s, par, j - 4)

        def add_out(ready, value, bank, m, j, done):
            dve.wait_ge(ready, value)
            part = x[:, m, j * COLS:(j + 1) * COLS]
            v.scalar_tensor_tensor(out=part, in0=ps[bank][:], scalar=0.5, in1=part,
                                   op0=ALU.mult, op1=ALU.add).then_inc(done, 1)

        dve.sem_inc(split_done, RING)
        dve.sem_inc(conv_done, 4)
        dve.sem_inc(up_read, 4)
        dve.wait_ge(x_loaded, 16 * MT)
        dve.sem_inc(x_ready, 4)

        with dve.Fori(0, DEPTH) as l:
            n1, n2 = 2 * l, 2 * l + 1
            per_layer = 5 + 4 + 2 * IN_TURN + 5 + 2 * 2 * STEPS
            kept = dve_step.enter(l, per_layer)
            dve.wait_ge(now_ready, l + 1)
            rest(l, 0, 0)
            for i in range(4):
                norm_rest(n1, i, ATTN_BANKS, a_hi, a_lo, G_ATTN)
                if i < 3:
                    rest(l, i + 1, i + 1)
            norm_factor(n1)
            keep_factor()
            rest(l, 4, 4)
            rest(l, 5, 5)
            dve_step.link(dve, v.tensor_copy(wf_hi[:], now[:, WF:WF + 4 * KC]))
            v.tensor_tensor(wf_lo[:], now[:, WF:WF + 4 * KC], wf_hi[:].bitcast(F32), ALU.subtract) \
                .then_inc(wf_ready, 1)
            q_k = lam_in[:, bass.ds(l, 1), :].rearrange("p a (b c d) -> p (a b) c d", b=2, c=2)
            products = square[:, 0, 0:2 * HD].rearrange("p (b d) -> p b d", b=2)
            dve_step.link(dve, v.tensor_tensor(products, q_k[:, :, 0, :], q_k[:, :, 1, :], ALU.mult))
            v.tensor_reduce(lam[:, 0:2], products, AX.X, ALU.add).then_inc(lam_sums, 1)
            with dve.Fori(0, 2) as i:
                for b in range(3):
                    for j in range(PER_BLOCK):
                        ahead(l, PER_BLOCK * b + j, i, 3 * PER_BLOCK)
            dve.wait_ge(lam_exps, l + 1)
            dve_step.link(dve, v.tensor_tensor(lam[:, 4:5], lam[:, 3:4], lam[:, 2:3], ALU.subtract))
            first = lam_first[:, bass.ds(l, 1), :].rearrange("p a n -> p (a n)")
            v.tensor_tensor(lam[:, 7:8], lam[:, 4:5], first[:, 0:1], ALU.add)
            gain = now[:, SUBLN:SUBLN + P]
            dve_step.link(dve, v.tensor_scalar(gain, gain, first[:, 1:2], None, ALU.mult))
            dve.wait_ge(f_ready, l + 1)
            for m in range(MT):
                ins = v.scalar_tensor_tensor(out=logf[:, 0, 4 * m:4 * m + 4], in0=ps[OUT_BANK][:, 4 * m:4 * m + 4],
                                             scalar=r_tok[:, m:m + 1], in1=now[:, FBIAS:FBIAS + 4],
                                             op0=ALU.mult, op1=ALU.add)
            ins.then_inc(f_biased, 1)
            dve.wait_ge(f_logs, l + 1)
            v.scalar_tensor_tensor(out=logf[:, 2, :], in0=logf[:, 0, :], scalar=0.0, in1=logf[:, 1, :],
                                   op0=ALU.min, op1=ALU.subtract).then_inc(logf_ready, 1)
            with dve.Fori(0, 2) as i:
                kept_turn = dve_step.enter(i, IN_TURN)
                for tick in range(TICKS + 1):
                    for u, (turn, score, third, values) in enumerate(UNIT_TICKS):
                        c = tick - score
                        if u == SB:
                            if c in (0, 1):
                                softplus(l, i, c)
                        else:
                            if c in (0, 1):
                                softmax_max(l, i, u, c)
                            if c - 1 in (0, 1):
                                softmax_scale(l, i, u, c - 1)
                    if tick == 6:
                        decays(l, i)
                    if tick == SUBLN_TICK - 1:
                        subln_square(l, i)
                    if tick == SUBLN_TICK:
                        subln_scale(l, i)
                    for j in range(3 * PER_BLOCK):
                        if SPLIT_TICKS[j] == tick:
                            ahead(l, P_GATES + j, i, 3 * PER_BLOCK)
                dve_step.leave(kept_turn, 2, IN_TURN)
            for i in range(4):
                rest_pair(o_hi, 4 * l + i + 1, O_BANKS[i], b_hi, b_lo, i, o_lo)
            for j in range(OUT_BLOCKS):
                for m in range(MT):
                    dve.wait_ge(gates_ready, 4 * l + 2 * j + m + 1)
                    if j == 1:
                        dve.wait_ge(mixed_ready, 4 * l + m + 1)
                    for b in range(3):
                        if m == 0:
                            dve.wait_ge(branch_ready, 6 * l + 3 * j + b + 1)
                        else:
                            dve.wait_ge(piece_used, RING + PIECES * l + P_BRANCH + PER_BLOCK * j + (1, 3, 4)[b])
                        v.scalar_tensor_tensor(out=gated[m][b], in0=gate_cols(m, j)[:, 2 - b, :], scalar=1.0,
                                               in1=ps[2 + 3 * m + b][:], op0=ALU.add, op1=ALU.mult) \
                            .then_inc(branch_read, 1)
                    if m == 0:
                        ahead(l, P_BRANCH + PER_BLOCK * j)
                        ahead(l, P_BRANCH + PER_BLOCK * j + 1)
                        if j == 1:
                            for i in range(2):
                                rest_pair(mixed_hi, 4 * l + i + 1, i, a_hi, a_lo, i, mixed_lo)
                for k in range(2, PER_BLOCK):
                    ahead(l, P_BRANCH + PER_BLOCK * j + k)
            ahead(l, P_OUT)
            ahead(l, P_OUT + 1)
            for i in (2, 3):
                rest_pair(mixed_hi, 4 * l + i + 1, 2 + i, a_hi, a_lo, i, mixed_lo)
            out_half = HALVES * l + QKV_BLOCKS + GATE_BLOCKS
            out_used = RING + PIECES * l + P_OUT
            for k in (2, 3, 4):
                ahead(l, P_OUT + k)
            add_out(half_ready, out_half + 1, 0, 0, 0, mix_added)
            add_out(piece_used, out_used + 6, 1, 1, 0, mix_added)
            ahead(l, P_OUT + 5)
            norm_rest(n2, 0, FFN_BANKS, b_hi, b_lo, G_FFN)
            ahead(l, P_OUT + 6)
            add_out(half_ready, out_half + 2, 2, 0, 1, mix_added)
            norm_rest(n2, 1, FFN_BANKS, b_hi, b_lo, G_FFN)
            add_out(piece_used, out_used + 8, 3, 1, 1, mix_added)
            norm_rest(n2, 2, FFN_BANKS, b_hi, b_lo, G_FFN)
            norm_rest(n2, 3, FFN_BANKS, b_hi, b_lo, G_FFN)
            norm_factor(n2)
            keep_factor()
            ahead(l, P_OUT + 7)
            mlp_step(l, 0, 0, (P_FFN, 0, 0, 4))
            with dve.Fori(0, 4) as i:
                kept_turn = dve_step.enter(i, 8)
                for k in range(2):
                    mlp_step(l, 2 * i + k + 1, (k + 1) % 2, (P_FFN + 4 + 6 * k, i, 12, 6))
                dve_step.leave(kept_turn, 4, 8)
            for s in (STEPS - 2, STEPS - 1):
                mlp_step(l, s, s % 2, (P_FFN + 4 + 6 * (s - 1), 0, 0, 6))
            for j in range(4):
                finish_step(l, STEPS - 1, (STEPS - 1) % 2, j)
            for k, (j, m) in enumerate(((0, 0), (0, 1), (1, 0), (1, 1))):
                if k < 3:
                    add_out(down_ready, 3 * l + k + 1, 4 + 2 * m + j, m, j, x_ready)
                else:
                    add_out(piece_used, RING + PIECES * (l + 1), 4 + 2 * m + j, m, j, x_ready)
            dve_step.leave(kept, DEPTH, per_layer)
        norm_factor(2 * DEPTH)
        dve.wait_ge(g_loaded, 16)
        for m in range(MT):
            v.scalar_tensor_tensor(out=rows[:, m, :], in0=x[:, m, :], scalar=rinv[:, m:m + 1], in1=g_fin,
                                   op0=ALU.mult, op1=ALU.mult).then_inc(y_ready, 1)

    @block.tensor
    def _(pe):
        t = nc.tensor

        def product(out_ap, left, right, start, stop):
            (lh, ll), (rh, rl) = left, right
            t.matmul(out_ap, lh, rh, start=start, stop=False, skip_group_check=True)
            t.matmul(out_ap, lh, rl, start=False, stop=False, skip_group_check=True)
            return t.matmul(out_ap, ll, rh, start=False, stop=stop, skip_group_check=True)

        def left_of(act_pair, kc, m):
            return [z[:, kc, m * P:(m + 1) * P] for z in act_pair]

        def right_of(slot, k):
            return [z[:, slot, k * COLS:(k + 1) * COLS] for z in (w_hi, w_lo)]

        def quarter(l, n, slot, act_pair, bank, m, i):
            if m == 0:
                pe.wait_ge(split_done, RING + PIECES * l + n + 1)
            for k in range(2):
                ins = product(bank[:], left_of(act_pair, 2 * i + k, m), right_of(slot, k),
                              start=(i == 0 and k == 0), stop=(i == 3 and k == 1))
            if m == 1:
                ins.then_inc(piece_used, 1)
            elif i == 3:
                ins.then_inc(half_ready, 1)

        def turn_rows(src, i, bank, done):
            for k in range(2):
                for m in range(MT):
                    ins = t.transpose(ps[bank][:, k * S + m * P:k * S + (m + 1) * P],
                                      src[:, m, (2 * i + k) * P:(2 * i + k + 1) * P], ident[:])
            ins.then_inc(done, 1)

        def turn_unit(unit, u):
            pe.wait_ge(unit_staged, unit + 1)
            for b in range(4):
                ins = t.transpose(ps[QK_BANK][:, b * P:(b + 1) * P], staged[:, u % 2, b * P:(b + 1) * P], ident[:])
            ins.then_inc(unit_turned, 1)

        def heads_of(u, c):
            both = turned[c * HD:(c + 1) * HD, u % 2, :]
            return both[:, 0:S], both[:, S:2 * S]

        def add(out_ap, left, right, start=False, stop=False):
            return t.matmul(out_ap, left, right, start=start, stop=stop, skip_group_check=True)

        def softmax_scores(l, i, u):
            pe.wait_ge(turned_ready, UNITS * l + 4 * i + u + 1)
            if u == FX:
                pe.wait_ge(decay_ready, 2 * l + i + 1)
            for c in range(2):
                q, k = heads_of(u, c)
                sc = score_bank(u, c)
                add(sc[:, 0:P], q[:, 0:P], k[:, 0:P], start=True)
                if u == FX:
                    add(sc[:, 0:P], decay[:, c, 0:P], ones_later[:, P:2 * P])
                add(sc[:, 0:P], ident_bf[:], mask_bf[:], stop=True)
                add(sc[:, P:3 * P], q[:, P:S], k, start=True)
                if u == FX:
                    add(sc[:, P:2 * P], decay[:, c, P:2 * P], ones_later[:, P:2 * P])
                    add(sc[:, P:3 * P], decay[:, c, 2 * P:3 * P], ones_later[:])
                add(sc[:, 2 * P:3 * P], ident_bf[:], mask_bf[:], stop=True).then_inc(scores_ready, 1)

        def turn_prob(l, i, u):
            k = 8 * l + 4 * i + TURNS[u]
            for c in range(2 if u == FX else 1):
                pe.wait_ge(prob_ready, k + c + 1)
                for b in range(3):
                    ins = t.transpose(score_bank(u, c)[:, b * P:(b + 1) * P], prob[:, u % 2, c, b * P:(b + 1) * P],
                                      ident[:])
                ins.then_inc(prob_turned, 1)

        def stick_scores(l, i):
            pe.wait_ge(turned_ready, UNITS * l + 4 * i + SB + 1)
            for c in range(2):
                q, k = heads_of(SB, c)
                sc = score_bank(SB, c)
                add(sc[:, 0:S], k[:, 0:P], q, start=True)
                add(sc[:, S:3 * P], k[:, P:S], q[:, P:S]).then_inc(scores_ready, 1)

        def stick_sum(l, i):
            for c in range(2):
                pe.wait_ge(stick_masked, 4 * l + 2 * i + c + 1)
                sc, sp = score_bank(SB, c), prob_t[:, 0, c, :]
                add(sc[:, 0:S], neg_from[:, 0:P], sp[:, 0:S])
                add(sc[:, P:S], neg_from[:, P:2 * P], sp[:, S:3 * P])
                add(sc[:, S:3 * P], neg_from[:, 0:P], sp[:, S:3 * P])
                add(sc[:, 0:P], ident_bf[:], later_bf[:])
                add(sc[:, S:3 * P], ident_bf[:], later_bf[:], stop=True).then_inc(stick_sums, 1)

        def values(l, i, u):
            if u == SB:
                pe.wait_ge(stick_exps, 4 * l + 2 * i + 2)
            else:
                pe.wait_ge(prob_t_ready, 8 * l + 4 * i + TURNS[u] + (2 if u == FX else 1))
            v_col = (V_DIFF + 2 * P * i, V_DIFF + 2 * P * i + P, V_STICK + P * i, V_FOX + P * i)[u]
            width = P if u in (D0, D1) else HD
            for c in range(P // width):
                w = prob[:, 0, c, :] if u == SB else prob_t[:, u % 2, c, :]
                v = [qkv[:, m, bass.ds(v_col + c * width, width)] for m in range(MT)]
                o = ps[OUT_BANK]
                add(o[:, c * width:(c + 1) * width], w[:, 0:P], v[0], start=True, stop=True)
                o1 = o[:, P + c * width:P + (c + 1) * width]
                add(o1, w[:, P:2 * P], v[0], start=True)
                ins = add(o1, w[:, 2 * P:3 * P], v[1], stop=True)
            ins.then_inc(unit_done, 1)

        def branch(l, j, m, i):
            b = (0, 1, 1, 2)[i]
            if m == 0 and j == 0:
                pe.wait_ge(o_lo, 4 * l + i + 1)
            if i != 2 and j == 1:
                pe.wait_ge(branch_read, 12 * l + 3 * m + b + 1)
            n = P_BRANCH + PER_BLOCK * j + i
            if m == 0:
                pe.wait_ge(split_done, RING + PIECES * l + n + 1)
            for k in range(2):
                ins = product(ps[2 + 3 * m + b][:], left_of((b_hi, b_lo), 2 * i + k, m),
                              right_of(n % RING, k), start=(i != 2 and k == 0), stop=(i != 1 and k == 1))
            if m == 1:
                ins.then_inc(piece_used, 1)
            elif i != 1:
                ins.then_inc(branch_ready, 1)

        def chunk(l, s, par, j, kcs, slot):
            p, g = j // 2, j % 2
            for kc in kcs:
                ins = product(ps[2 * par + p][:, g * S:(g + 1) * S],
                              [z[:, slot, kc * P:(kc + 1) * P] for z in (w_hi, w_lo)],
                              [z[:, kc, :] for z in (b_hi, b_lo)],
                              start=(kc == 0 and g == 0), stop=(kc == KC - 1 and g == 1))
            return ins

        def up(l, s, par, slots, piece):
            for j in range(4):
                if j % 2 == 0:
                    pe.wait_ge(up_read, 2 * (STEPS * l + s) + j // 2 + 1)
                pe.wait_ge(split_done, RING + PIECES * l + piece + j + 1)
                chunk(l, s, par, j, range(KC), slots[j]).then_inc(piece_used, 1)

        def spread_factor(l):
            pe.wait_ge(r_ready, 2 * l + 2)
            for m in range(MT):
                ins = add(ps[6][:, m * P:(m + 1) * P], r_tok[:, m:m + 1].broadcast_to([P, P]), ident[:],
                          start=True, stop=True)
            ins.then_inc(r_spread, 1)

        def first_up(l, n2, slots):
            for j in range(4):
                pe.wait_ge(split_done, RING + PIECES * l + P_FFN + j + 1)
                for i in range(2):
                    if j == 0:
                        pe.wait_ge(norm_lo, 4 * n2 + i + 1)
                    chunk(l, 0, 0, j, (2 * i, 2 * i + 1), slots[j])
            for j in range(4):
                for i in (2, 3):
                    if j == 0:
                        pe.wait_ge(norm_lo, 4 * n2 + i + 1)
                    last = chunk(l, 0, 0, j, (2 * i, 2 * i + 1), slots[j])
                last.then_inc(piece_used, 1)
                if j == 1:
                    spread_factor(l)

        def down(l, s, par, slots, piece, final=False):
            for p in range(2):
                pe.wait_ge(h_lo, 2 * (STEPS * l + s) + p + 1)
                pe.wait_ge(split_done, RING + PIECES * l + piece + p + 1)
                for k, (j, m) in enumerate(((0, 0), (0, 1), (1, 0), (1, 1))):
                    ins = product(ps[4 + 2 * m + j][:], left_of((a_hi, a_lo), 2 * par + p, m),
                                  right_of(slots[p], j), start=False, stop=final and p == 1)
                    if final and p == 1 and k < 3:
                        ins.then_inc(down_ready, 1)
                ins.then_inc(piece_used, 1)

        def slots_from(n, count):
            return [(n + k) % RING for k in range(count)]

        def turn_x(ready, value, pairs, banks):
            pe.wait_ge(ready, value)
            for i in pairs:
                turn_rows(x, i, banks[i], x_turned)

        pe.sem_inc(piece_used, RING)
        pe.sem_inc(unit_turned, 2)
        pe.wait_ge(ident_ready, 1)
        with pe.Fori(0, DEPTH) as l:
            n1, n2 = 2 * l, 2 * l + 1
            turn_x(x_ready, 4 * l + 2, (0, 1), ATTN_BANKS)
            turn_x(x_ready, 4 * l + 4, (2, 3), ATTN_BANKS)
            with pe.Fori(0, 2) as turn:
                for b in range(3):
                    B = 3 * turn + b
                    for m, i in QUARTERS:
                        if i == 0:
                            pe.wait_ge(block_read, 2 * ((QKV_BLOCKS + GATE_BLOCKS) * l + B) + m + 1)
                        if m == 0 and b == 0:
                            pe.wait_ge(norm_lo, 4 * n1 + i + 1)
                        quarter(l, PER_BLOCK * B + i, (PER_BLOCK * b + i) % RING, (a_hi, a_lo), ps[m], m, i)
            pe.wait_ge(wf_ready, l + 1)
            for m in range(MT):
                for kc in range(KC):
                    ins = product(ps[OUT_BANK][:, 4 * m:4 * m + 4], left_of((a_hi, a_lo), kc, m),
                                  [z[:, 4 * kc:4 * kc + 4] for z in (wf_hi, wf_lo)],
                                  start=(kc == 0), stop=(kc == KC - 1))
            ins.then_inc(f_ready, 1)
            pe.wait_ge(consts_ready, 1)
            with pe.Fori(0, 2) as turn:
                for tick in range(TICKS):
                    for u, (first, score, third, value) in enumerate(UNIT_TICKS):
                        if tick == first:
                            turn_unit(UNITS * l + 4 * turn + u, u)
                        if tick == score:
                            stick_scores(l, turn) if u == SB else softmax_scores(l, turn, u)
                        if tick == third:
                            stick_sum(l, turn) if u == SB else turn_prob(l, turn, u)
                        if tick == value:
                            values(l, turn, u)
                    b = tick // 8
                    m, i = QUARTERS[tick % 8]
                    B = 3 * turn + b
                    if i == 0:
                        pe.wait_ge(block_read, 2 * ((QKV_BLOCKS + GATE_BLOCKS) * l + QKV_BLOCKS + B) + m + 1)
                    quarter(l, P_GATES + PER_BLOCK * B + i, (PER_BLOCK * b + i) % RING, (a_hi, a_lo), ps[m], m, i)
            pe.wait_ge(out_read, UNITS * l + 4 + SB + 1)
            turn_rows(o_all, 0, O_BANKS[0], o_turned)
            pe.wait_ge(diff_ready, 2 * l + 2)
            turn_rows(o_all, 1, O_BANKS[1], o_turned)
            turn_rows(o_all, 2, O_BANKS[2], o_turned)
            pe.wait_ge(out_read, UNITS * (l + 1))
            turn_rows(o_all, 3, O_BANKS[3], o_turned)
            for j in range(OUT_BLOCKS):
                for k, (m, i) in enumerate(QUARTERS):
                    if j == 1 and k == 4:
                        pe.wait_ge(mixed_ready, 4 * l + 2)
                        pe.wait_ge(block_read, 2 + 2 * (QKV_BLOCKS + GATE_BLOCKS) * (l + 1))
                        for pair_ in (0, 1):
                            turn_rows(rows, pair_, MIXED_BANKS[pair_], mixed_turned)
                    branch(l, j, m, i)
            for half in range(2):
                for j in range(OUT_BLOCKS):
                    for m in range(MT):
                        if half == 0 and j == 1:
                            pe.wait_ge(branch_read, 12 * l + 6 + m + 1)
                        if half == 0 and (j, m) == (1, 1):
                            pe.wait_ge(mixed_ready, 4 * l + 4)
                            for pair_ in (2, 3):
                                turn_rows(rows, pair_, MIXED_BANKS[pair_], mixed_turned)
                        if half == 1 and (j, m) == (1, 1):
                            turn_x(mix_added, 4 * l + 2, (0, 1), FFN_BANKS)
                        for i in (2 * half, 2 * half + 1):
                            if j == 0 and m == 0:
                                pe.wait_ge(mixed_lo, 4 * l + i + 1)
                            n = P_OUT + 4 * half + 2 * j + i % 2
                            quarter(l, n, n % RING, (a_hi, a_lo), ps[2 * j + m], m, i)
            turn_x(mix_added, 4 * l + 4, (2, 3), FFN_BANKS)
            first_up(l, n2, slots_from(P_FFN, 4))
            pe.wait_ge(r_row_ready, l + 1)
            for b in range(4):
                add(ps[4 + b][:], zero_bf[:, 0:P], zero_bf[:], start=True)
            with pe.Fori(0, 4) as turn:
                for k in range(2):
                    s, n = 2 * turn + k + 1, P_FFN + 4 + 6 * k
                    up(l, s, (k + 1) % 2, slots_from(n, 4), n + 12 * turn)
                    down(l, s - 1, k % 2, slots_from(n + 4, 2), n + 12 * turn + 4)
            for s in (STEPS - 2, STEPS - 1):
                n = P_FFN + 4 + 6 * (s - 1)
                up(l, s, s % 2, slots_from(n, 4), n)
                down(l, s - 1, (s - 1) % 2, slots_from(n + 4, 2), n + 4)
            n = PIECES - 2
            down(l, STEPS - 1, (STEPS - 1) % 2, slots_from(n, 2), n, final=True)

    block.__exit__(None, None, None)


def _blocks(w):
    n = w.shape[1] // COLS
    return w.reshape(PER_BLOCK, 2, P, n, COLS).transpose(3, 0, 2, 1, 4).reshape(n * PER_BLOCK, P, PIECE)


def _stream(w_in, w_br, w_out, w_up, w_down):
    cuts = {name: (lo, hi) for name, lo, hi in (
        ("fq", 0, 256), ("fk", 256, 512), ("fv", 512, 768), ("dq", 768, 1280), ("dk", 1280, 1792),
        ("dv", 1792, 2304), ("sq", 2304, 2560), ("sk", 2560, 2816), ("sv", 2816, 3072))}
    order = ("sq", "fq", "sk", "fk", "sv", "fv", "dq", "dk", "dv")
    parts = [w_in[:, cuts[k][0]:cuts[k][1]] for k in order] + [w_in[:, QKV + 4:], w_br]
    blocks = [_blocks(np.concatenate(parts, axis=1))]
    halves = _blocks(w_out).reshape(OUT_BLOCKS, 2, 2, P, PIECE).transpose(1, 0, 2, 3, 4)
    blocks.append(halves.reshape(-1, P, PIECE))
    ups = w_up.reshape(KC, P, 2, STEPS, 2, P).transpose(3, 4, 2, 1, 0, 5).reshape(STEPS, 4, P, PIECE)
    downs = w_down.reshape(STEPS, 2, P, D)
    blocks.append(ups[0])
    for s in range(1, STEPS):
        blocks += [ups[s], downs[s - 1]]
    blocks.append(downs[STEPS - 1])
    return np.concatenate(blocks, axis=0)


def _params(l, g_attn, w_in, g_ffn, bias, subln, conv_w, conv_b):
    def tall(v):
        return v.reshape(-1, P).T

    def wide(v):
        return np.broadcast_to(v.reshape(1, -1), (P, v.size))

    wf = w_in[:, QKV:QKV + 4].reshape(KC, P, 4).transpose(1, 0, 2).reshape(P, 4 * KC)
    conv = np.concatenate([conv_w, conv_b[None]], axis=0)
    conv = conv.reshape(4, 2, STEPS, 2, P).transpose(4, 2, 3, 1, 0).reshape(P, 16 * STEPS)
    return np.concatenate([tall(g_attn), tall(g_ffn), wf, wide(bias), wide(subln), conv], axis=1)


def kernel(x, attn_norm_g, w_in, forget_bias, lam_q1, lam_k1, lam_q2, lam_k2, diff_subln_g, w_br_fox,
           w_br_diff, w_br_stick, w_out, ffn_norm_g, w_up, conv_w, conv_b, w_down, final_norm_g):
    import concourse.bacc as _bacc
    from concourse.bass_utils import run_bass_kernel_spmd as _run

    a = {k: np.asarray(v) for k, v in locals().items() if not k.startswith("_")}
    stream, params = [], []
    for l in range(DEPTH):
        w_br = np.concatenate([a["w_br_stick"][l], a["w_br_diff"][l], a["w_br_fox"][l]], axis=0)
        stream.append(_stream(a["w_in"][l], w_br, a["w_out"][l], a["w_up"][l], a["w_down"][l]))
        params.append(_params(l, a["attn_norm_g"][l], a["w_in"][l], a["ffn_norm_g"][l], a["forget_bias"][l],
                              a["diff_subln_g"][l], a["conv_w"][l], a["conv_b"][l]))
    lam_rows = np.stack([a["lam_q1"], a["lam_k1"], a["lam_q2"], a["lam_k2"]], axis=1)
    half = HD // 8
    inv_freq = np.float32(500000.0) ** (-np.arange(0, 2 * half, 2, dtype=np.float32) / np.float32(2 * half))
    ang = np.arange(S, dtype=np.float32)[:, None] * inv_freq[None, :].astype(np.float32)
    table = np.stack([np.cos(ang), np.sin(ang)]).astype(np.float32).reshape(2, MT, P, half).transpose(2, 0, 1, 3)
    table = np.broadcast_to(table[:, :, None, :, None, :], (P, 2, 2, MT, 2, half)).reshape(P, 2, 64)

    nc = _bacc.Bacc("TRN2", target_bir_lowering=False, num_devices=1)
    arrays = {
        "x_in": a["x"].reshape(S, D),
        "stream": np.concatenate(stream, axis=0),
        "params": np.ascontiguousarray(np.stack(params, axis=1)),
        "lam_rows": np.ascontiguousarray(lam_rows.reshape(DEPTH, LAMS)),
        "rope_in": np.ascontiguousarray(table),
        "g_final": np.ascontiguousarray(a["final_norm_g"]),
    }
    args = [nc.dram_tensor(n, v.shape, F32, kind="ExternalInput").ap() for n, v in arrays.items()]
    args.append(nc.dram_tensor("y", (S, D), F32, kind="ExternalOutput").ap())
    build(nc, *args)
    r = _run(nc, [arrays], core_ids=[0])
    return r.results[0]["y"].reshape(1, S, D)
```

```python
import math

import concourse.bass as bass
import numpy as np
from concourse import mybir

F32 = mybir.dt.float32
F32R = mybir.dt.float32r
BF16 = mybir.dt.bfloat16
I32 = mybir.dt.int32
ALU = mybir.AluOpType
ACT = mybir.ActivationFunctionType
AX = mybir.AxisListType

P = 128
D = 1024
S = 256
DEPTH = 2
HD = 64
MT = S // P
KC = D // P
COLS = 512
PIECE = 2 * COLS
RING = 6
QKV = 3072
QKV_BLOCKS = QKV // COLS
GATE_BLOCKS = 3 * D // COLS
OUT_BLOCKS = D // COLS
D_FF = 2816
STEPS = D_FF // (2 * P)
PER_BLOCK = 4
P_GATES = PER_BLOCK * QKV_BLOCKS
P_BRANCH = P_GATES + PER_BLOCK * GATE_BLOCKS
P_OUT = P_BRANCH + PER_BLOCK * OUT_BLOCKS
P_FFN = P_OUT + PER_BLOCK * OUT_BLOCKS
PIECES = P_FFN + 6 * STEPS
H_AT = KC // 2
HALVES = QKV_BLOCKS + GATE_BLOCKS + OUT_BLOCKS
EPS = 1e-6
NEG = -1e30
READ_AT_START = 6
UNITS = 8

STICK, FOX, DIFF = 0, 256, 1536
V_STICK, V_FOX, V_DIFF = 1024, 1280, 2560
G_ATTN, G_FFN, WF, FBIAS, SUBLN, NOW = 0, 8, 16, 48, 52, 180
CONV = NOW
PARAMS = CONV + 16 * STEPS
LAMS = 4 * HD
O_STICK, O_DIFF, O_FOX = 0, 256, 768

LAM_INIT = [0.8 - 0.6 * math.exp(-0.3 * l) for l in range(DEPTH)]

QUARTERS = [(0, 0), (0, 1), (1, 0), (1, 1), (0, 2), (0, 3), (1, 2), (1, 3)]

TICKS = 8 * 3
D0, D1, SB, FX = range(4)
UNIT_TICKS = [(2, 4, 8, 10), (7, 9, 13, 15), (11, 13, 17, 20), (15, 17, 21, 23)]
SUBLN_TICK = 18
IN_TURN = 2 * 4 + 2 + 3 + 10
SOFT = {D0: 0, D1: 1, FX: 2}
TURNS = {D0: 0, D1: 1, FX: 2}
SPLIT_TICKS = [3, 5, 7, 9, 11, 13, 15, 17, 19, 21, 23, 24]


class Tally:

    def __init__(self, sem):
        self.sem, self.base, self.n = sem, 0, 0

    def link(self, eng, ins):
        ins.then_inc(self.sem, 1)
        self.n += 1
        eng.wait_ge(self.sem, self.base + self.n)

    def enter(self, i, per_turn):
        kept = (self.base, self.n)
        self.base, self.n = self.base + self.n + i * per_turn, 0
        return kept

    def leave(self, kept, turns, per_turn):
        assert self.n == per_turn, (self.n, per_turn)
        self.base, self.n = kept[0], kept[1] + turns * per_turn


def build(nc, x_in, stream, params, lam_rows, rope_in, g_final, out):
    def sb(name, shape, dt=F32):
        return nc.alloc_sbuf_tensor(name, shape, dt)

    def sem(name):
        return nc.alloc_semaphore(name)

    raw = sb("raw", [P, RING, PIECE])
    w_hi = sb("w_hi", [P, RING, PIECE], F32R)
    w_lo = sb("w_lo", [P, RING, PIECE], F32R)
    x = sb("x", [P, MT, D])
    a_hi = sb("a_hi", [P, KC, S], F32R)
    a_lo = sb("a_lo", [P, KC, S], F32R)
    b_hi = sb("b_hi", [P, KC, S], F32R)
    b_lo = sb("b_lo", [P, KC, S], F32R)
    qkv = sb("qkv", [P, MT, QKV])
    gates = sb("gates", [P, MT, 3 * D])
    rows = sb("rows", [P, MT, D])
    o_all = sb("o_all", [P, MT, D])
    all_params = sb("all_params", [P, DEPTH, PARAMS])
    now = sb("now", [P, NOW])
    taps = sb("taps", [P, 2, 16])
    wf_hi = sb("wf_hi", [P, 4 * KC], F32R)
    wf_lo = sb("wf_lo", [P, 4 * KC], F32R)
    rope = sb("rope", [P, 2, 64])
    staged = sb("staged", [P, 2, 2 * MT * P])
    turned = sb("turned", [P, 2, 4 * P])
    prob = sb("prob", [P, 2, 2, 384])
    prob_t = rows[:, :, 0:768].rearrange("p u (c n) -> p u c n", c=2)
    square = rows[:, :, 768:D]
    f_row = square[0:4, 1, :]
    decay = sb("decay", [P, 2, 3 * P])
    logf = sb("logf", [P, 3, 8])
    stats = sb("stats", [P, 2, 3, 4])
    norm = sb("norm", [P, 4, 4])
    r_tok = sb("r_tok", [P, 4])
    r_row = sb("r_row", [P, S])
    lam_in = sb("lam_in", [P, DEPTH, LAMS])
    lam_first = sb("lam_first", [P, DEPTH, 2])
    lam = sb("lam", [P, 8])
    ident = sb("ident", [P, P])
    ident_bf = sb("ident_bf", [P, P], BF16)
    mask_bf = sb("mask_bf", [P, P], BF16)
    later_bf = sb("later_bf", [P, P], BF16)
    later = sb("later", [P, P])
    tri_ones = sb("tri_ones", [P, 2 * P])
    ones_later = sb("ones_later", [P, 2 * P])
    neg_from = sb("neg_from", [P, 2 * P])
    zero_bf = sb("zero_bf", [P, COLS], BF16)
    conv = gates[:, 0, 0:2048].rearrange("p (s c g t) -> p s c g t", s=2, c=2, g=2)
    squash = gates[:, 1, 0:1024].rearrange("p (s c t) -> p s c t", s=2, c=2)
    g_fin = gates[:, 1, 2048:3072]
    unused = (gates[:, 1, 1024:2048], gates[:, 0, 2048:3072])
    hidden = gates[:, 0, 2048:3072].rearrange("p (c g t) -> p c g t", c=2, g=2)
    gated = [[qkv[:, m, b * COLS:(b + 1) * COLS] for b in range(3)] for m in range(MT)]

    ps = [nc.alloc_psum_tensor(f"bank{b}", [P, COLS], F32) for b in range(8)]
    QK_BANK, OUT_BANK = 2, 7
    QKV_BANKS = ((0, 1), (6, 7), (4, 5))
    ATTN_BANKS, FFN_BANKS = (2, 3, 4, 5), (6, 7, 4, 5)
    O_BANKS, MIXED_BANKS = (2, 3, 4, 7), (0, 1, 4, 5)

    def score_bank(unit, c):
        return ps[3 + 2 * (unit % 2) + c]

    raw_landed = [sem(f"raw_landed{i}") for i in range(RING)]
    landed_uses = [len(range(i, PIECES, RING)) for i in range(RING)]
    hi_ready = sem("hi_ready")
    split_done = sem("split_done")
    piece_used = sem("piece_used")
    x_loaded = [sem(f"x_loaded{j}") for j in range(2)]
    params_loaded = sem("params_loaded")
    g_loaded = sem("g_loaded")
    consts_ready = sem("consts_ready")
    lam_sums = sem("lam_sums")
    lam_exps = sem("lam_exps")
    ident_ready = sem("ident_ready")
    x_ready = sem("x_ready")
    mix_added = sem("mix_added")
    squares_ready = sem("squares_ready")
    x_turned = sem("x_turned")
    r_ready = sem("r_ready")
    r_spread = sem("r_spread")
    r_row_ready = sem("r_row_ready")
    norm_hi = sem("norm_hi")
    norm_lo = sem("norm_lo")
    now_ready = sem("now_ready")
    half_ready = sem("half_ready")
    block_read = sem("block_read")
    wf_ready = sem("wf_ready")
    f_summed = sem("f_summed")
    f_copied = sem("f_copied")
    f_ready = sem("f_ready")
    f_biased = sem("f_biased")
    f_logs = sem("f_logs")
    logf_ready = sem("logf_ready")
    unit_staged = sem("unit_staged")
    unit_turned = sem("unit_turned")
    turned_ready = sem("turned_ready")
    scores_ready = sem("scores_ready")
    max_ready = sem("max_ready")
    exps_done = sem("exps_done")
    prob_ready = sem("prob_ready")
    prob_turned = sem("prob_turned")
    prob_t_ready = sem("prob_t_ready")
    stick_logs = sem("stick_logs")
    stick_softplus = sem("stick_softplus")
    stick_masked = sem("stick_masked")
    stick_sums = sem("stick_sums")
    stick_exps = sem("stick_exps")
    decay_ready = sem("decay_ready")
    unit_done = sem("unit_done")
    out_read = sem("out_read")
    diff_ready = sem("diff_ready")
    o_turned = sem("o_turned")
    o_hi = sem("o_hi")
    o_lo = sem("o_lo")
    gates_ready = sem("gates_ready")
    branch_ready = sem("branch_ready")
    branch_read = sem("branch_read")
    mixed_ready = sem("mixed_ready")
    mixed_turned = sem("mixed_turned")
    mixed_hi = sem("mixed_hi")
    mixed_lo = sem("mixed_lo")
    taps_ready = sem("taps_ready")
    conv_begun = sem("conv_begun")
    up_read = sem("up_read")
    conv_done = sem("conv_done")
    tanh_done = sem("tanh_done")
    h_ready = sem("h_ready")
    h_hi = sem("h_hi")
    h_lo = sem("h_lo")
    down_ready = sem("down_ready")
    xg_ready = sem("xg_ready")
    r_last = sem("r_last")
    y_ready = [sem(f"y_ready{m}") for m in range(MT)]
    y_stored = sem("y_stored")
    act_step = Tally(sem("act_step"))
    dve_step = Tally(sem("dve_step"))
    pool_step = Tally(sem("pool_step"))

    def pair(hi_lo, i):
        return hi_lo[:, 2 * i:2 * i + 2, :].rearrange("p k t -> p (k t)")

    def gate_cols(m, j):
        return gates[:, m, :].rearrange("p (b n) -> p b n", b=3)[:, :, j * COLS:(j + 1) * COLS]

    def diagonals(tile):
        return tile.rearrange("p (b n) -> p b n", b=3)[:, 0:3:2, :]

    block = nc.Block()
    block.__enter__()

    @block.sync
    def _(sp):
        for j in range(2):
            sp.dma_start(x[:, :, j * COLS:(j + 1) * COLS],
                         x_in.rearrange("(m p) n -> p m n", p=P)[:, :, j * COLS:(j + 1) * COLS]) \
                .then_inc(x_loaded[j], 16)

        def load(l, n, slot, free):
            sp.wait_ge(split_done, free)
            sp.dma_start(raw[:, slot, :], stream[bass.ds(l * PIECES + n, 1)].rearrange("a p n -> (a p) n")) \
                .then_inc(raw_landed[slot], 16)

        with sp.Fori(0, DEPTH) as l:
            for k in range(RING):
                load(l, k, k, l * PIECES + RING + min(k + 1 - PIECES % RING, 0))
            with sp.Fori(1, PIECES // RING) as r:
                for k in range(RING):
                    load(l, r * RING + k, k, l * PIECES + r * RING + k + 1)
            for k in range(PIECES % RING):
                n = PIECES - PIECES % RING + k
                load(l, n, k, l * PIECES + n + 1)
        sp.wait_ge(mix_added, 4 * DEPTH)
        sp.dma_start(g_fin, g_final.partition_broadcast(P)).then_inc(g_loaded, 16)
        for m in range(MT):
            sp.wait_ge(y_ready[m], 1)
            sp.dma_start(out[m * P:(m + 1) * P, :], rows[:, m, :]).then_inc(y_stored, 16)
        sp.wait_ge(y_stored, 16 * MT)

    @block.gpsimd
    def _(pool):
        g = nc.gpsimd
        pool_step.link(pool, g.memset(ident[:], 0.0))

        def cut(tile, op, fill, row, col):
            return g.affine_select(out=tile, in_=tile, pattern=[[col, P]], compare_op=op, fill=fill,
                                   base=0, channel_multiplier=row)

        cut(ident[:], ALU.not_equal, 1.0, 1, -1).then_inc(ident_ready, 1)
        for l in range(DEPTH):
            g.memset(lam_first[:, l, 0:1], -LAM_INIT[l])
            g.memset(lam_first[:, l, 1:2], 1.0 - LAM_INIT[l])
        for tile, value in ((ident_bf, 0.0), (mask_bf, 0.0), (later_bf, 0.0), (later, 1.0),
                            (tri_ones, 1.0), (ones_later, 1.0), (neg_from, -1.0), (zero_bf, 0.0)):
            last = g.memset(tile[:], value)
        pool_step.link(pool, last)
        cut(ident_bf[:], ALU.not_equal, 1.0, 1, -1)
        cut(mask_bf[:], ALU.is_ge, NEG, 1, -1)
        cut(later_bf[:], ALU.is_gt, NEG, -1, 1)
        cut(later[:], ALU.is_gt, 0.0, -1, 1)
        cut(tri_ones[:, 0:P], ALU.is_ge, 0.0, -1, 1)
        cut(ones_later[:, P:2 * P], ALU.is_gt, 0.0, 1, -1)
        cut(neg_from[:, 0:P], ALU.is_ge, 0.0, 1, -1).then_inc(consts_ready, 1)

        def stage(u, unit, q_col):
            pool.wait_ge(unit_turned, unit + 1)
            dst = staged[:, u % 2, :].rearrange("p (a m n) -> p a m n", a=2, m=MT)
            for a in range(2):
                ins = g.tensor_copy(dst[:, a], qkv[:, :, bass.ds(q_col + a * COLS, P)])
            return ins

        def rotate(u):
            t = staged[:, u % 2, :].rearrange("p (g n) -> p g n", n=HD)
            t1, t2 = t[:, :, 0:8], t[:, :, 8:16]
            cos, sin = (rope[:, i, :].rearrange("p (g n) -> p g n", n=8) for i in range(2))
            p = [rope_tmp[:, i, :].rearrange("p (g n) -> p g n", n=8) for i in range(4)]
            g.tensor_tensor(p[0], t1, cos, ALU.mult)
            g.tensor_tensor(p[1], t2, sin, ALU.mult)
            g.tensor_tensor(p[2], t2, cos, ALU.mult)
            pool_step.link(pool, g.tensor_tensor(p[3], t1, sin, ALU.mult))
            g.tensor_tensor(t1, p[0], p[1], ALU.subtract)
            return g.tensor_tensor(t2, p[2], p[3], ALU.add)

        rope_tmp = sb("rope_tmp", [P, 4, 64])

        def keep_later(tile):
            d = diagonals(tile)
            return g.tensor_tensor(d, d, later[:].unsqueeze(1).broadcast_to([P, 2, P]), ALU.mult)

        def attention_turn(l, i):
            unit = UNITS * l + 4 * i
            pool.wait_ge(block_read, READ_AT_START + 2 * ((QKV_BLOCKS + GATE_BLOCKS) * l + QKV_BLOCKS))
            for u in (D0, D1):
                pool_step.link(pool, stage(u, unit + u, DIFF + 2 * P * i + P * u))
                rotate(u).then_inc(unit_staged, 1)
            stage(SB, unit + SB, STICK + P * i).then_inc(unit_staged, 1)
            stage(FX, unit + FX, FOX + P * i).then_inc(unit_staged, 1)
            for c in range(2):
                pool.wait_ge(stick_softplus, 4 * l + 2 * i + c + 1)
                keep_later(prob_t[:, 0, c, :]).then_inc(stick_masked, 1)

        def merge(l, j, m):
            pool.wait_ge(branch_read, 12 * l + 6 * j + 3 * m + 3)
            stick, diff, fox = gated[m]
            pool_step.link(pool, g.tensor_tensor(stick, stick, diff, ALU.add))
            g.tensor_tensor(rows[:, m, j * COLS:(j + 1) * COLS], stick, fox, ALU.add).then_inc(mixed_ready, 1)

        def step_taps(l, s, par):
            pool.wait_ge(conv_done, 2 * (l * STEPS + s) + 2)
            g.tensor_copy(taps[:, par, :], all_params[:, bass.ds(l, 1), bass.ds(s * 16 + CONV, 16)]
                          .rearrange("p a n -> p (a n)")).then_inc(taps_ready, 1)

        pool.wait_ge(params_loaded, 16 * 3)
        with pool.Fori(0, DEPTH) as l:
            per_layer = 2 * 4 + MT * OUT_BLOCKS
            kept = pool_step.enter(l, per_layer)
            g.tensor_copy(now[:], all_params[:, bass.ds(l, 1), 0:NOW].rearrange("p a n -> p (a n)")) \
                .then_inc(now_ready, 1)
            with pool.Fori(0, 2) as i:
                kept_turn = pool_step.enter(i, 4)
                attention_turn(l, i)
                pool_step.leave(kept_turn, 2, 4)
            for j in range(OUT_BLOCKS):
                for m in range(MT):
                    merge(l, j, m)
            pool.wait_ge(norm_lo, 4 * (2 * l + 2))
            step_taps(l, 0, 0)
            with pool.Fori(0, 4) as i:
                for k in range(2):
                    step_taps(l, 2 * i + k + 1, (k + 1) % 2)
            for s in (STEPS - 2, STEPS - 1):
                step_taps(l, s, s % 2)
            pool_step.leave(kept, DEPTH, per_layer)
        pool.wait_ge(g_loaded, 16)
        for j in range(2):
            cols = slice(j * COLS, (j + 1) * COLS)
            pool.wait_ge(x_ready, 4 * DEPTH + 2 * j + 2)
            for m in range(MT):
                ins = g.tensor_tensor(rows[:, m, cols], x[:, m, cols], g_fin[:, cols], ALU.mult)
        ins.then_inc(xg_ready, 1)

    @block.scalar
    def _(act):
        a = nc.scalar

        def round_piece(l, n, slot, r, free=None):
            act.wait_ge(raw_landed[slot], 16 * (l * landed_uses[slot] + r + 1))
            act.wait_ge(piece_used, l * PIECES + n + 1 if free is None else free)
            a.activation(w_hi[:, slot, :], raw[:, slot, :], ACT.Copy).then_inc(hi_ready, 1)

        def first_piece(l, k):
            before = PIECES - PIECES % RING + k - (0 if k < PIECES % RING else RING)
            round_piece(l, k, k, 0, free=RING + l * PIECES - (PIECES - before - 1))

        def ahead(l, used, i=0, per=0):
            n = used + RING
            if n < PIECES:
                round_piece(l, n + i * per, n % RING, n // RING + i * (per // RING))

        def norm_stats(j, ready, value):
            act.wait_ge(ready, value)
            for m in range(MT):
                last = a.activation(unused[j][:, m * COLS:(m + 1) * COLS], x[:, m, j * COLS:(j + 1) * COLS], ACT.Square,
                                    accum_out=norm[:, 0, MT * j + m:MT * j + m + 1])
            last.then_inc(squares_ready, 1)

        def norm_round(n, i, banks, dst, gain):
            act.wait_ge(x_turned, 4 * n + i + 1)
            for k in range(2):
                kc = 2 * i + k
                ins = a.activation(dst[:, kc, :], ps[banks[i]][:, k * S:(k + 1) * S], ACT.Copy,
                                   scale=now[:, gain + kc:gain + kc + 1])
            ins.then_inc(norm_hi, 1)

        def read_block(l, b, m, bank, piece, dst, factor):
            if m == 0:
                act.wait_ge(half_ready, HALVES * l + b + 1)
            else:
                act.wait_ge(piece_used, RING + PIECES * l + piece + PER_BLOCK)
            a.activation(dst, ps[bank][:], ACT.Copy, scale=r_tok[:, factor + m:factor + m + 1]).then_inc(block_read, 1)

        def read_turned(unit, u):
            act.wait_ge(unit_turned, 2 + unit + 1)
            a.activation(turned[:, u % 2, :], ps[QK_BANK][:], ACT.Copy).then_inc(turned_ready, 1)

        def softmax_exp(l, i, u, c):
            k = 6 * l + 3 * i + SOFT[u]
            act.wait_ge(max_ready, 2 * k + c + 1)
            sc = score_bank(u, c)
            for q, (lo, hi) in enumerate(((0, P), (P, 3 * P))):
                col = 2 * c + q
                ins = a.activation(prob[:, u % 2, c, lo:hi], sc[:, lo:hi], ACT.Exp,
                                   bias=stats[:, u % 2, 0, col:col + 1],
                                   accum_out=stats[:, u % 2, 1, col:col + 1])
            ins.then_inc(exps_done, 1)

        def read_prob(k, u, c):
            act.wait_ge(prob_turned, k + 1)
            a.activation(prob_t[:, u % 2, c, :], score_bank(u, c)[:, 0:384], ACT.Copy).then_inc(prob_t_ready, 1)

        def read_out(unit, col):
            act.wait_ge(unit_done, unit + 1)
            a.activation(o_all[:, :, bass.ds(col, P)], ps[OUT_BANK][:, 0:2 * P].rearrange("p (m n) -> p m n", m=MT),
                         ACT.Copy).then_inc(out_read, 1)

        def stick_log(l, i, c):
            act.wait_ge(scores_ready, 2 * (UNITS * l + 4 * i + SB) + c + 1)
            t = prob[:, 0, c, :]
            act_step.link(act, a.activation(t, score_bank(0, c)[:, 0:384], ACT.Abs))
            act_step.link(act, a.activation(t, t, ACT.Exp, scale=-1.0))
            a.activation(t, t, ACT.Ln, bias=1.0).then_inc(stick_logs, 1)

        def stick_exp(l, i, c):
            act.wait_ge(stick_sums, 4 * l + 2 * i + c + 1)
            a.activation(prob[:, 0, c, :], score_bank(0, c)[:, 0:384], ACT.Exp).then_inc(stick_exps, 1)

        def round_pair(ready, value, bank, dst, i, done):
            act.wait_ge(ready, value)
            a.activation(pair(dst, i), ps[bank][:], ACT.Copy).then_inc(done, 1)

        def conv_begin(l, s, par, p):
            act.wait_ge(up_read, 4 + 2 * (STEPS * l + s) + p + 1)
            if p == 0:
                act.wait_ge(taps_ready, STEPS * l + s + 1)
            for g in range(2):
                c = 4 * (2 * p + g)
                ins = a.activation(conv[:, par, p, g, :], hidden[:, p, g, :], ACT.Identity,
                                   scale=taps[:, par, c + 2:c + 3], bias=taps[:, par, c + 3:c + 4])
            ins.then_inc(conv_begun, 1)

        def gate_tanh(l, s, par, p):
            act.wait_ge(conv_done, 4 + 2 * (STEPS * l + s) + p + 1)
            a.activation(squash[:, par, p, :], conv[:, par, p, 0, :], ACT.Tanh, scale=0.5).then_inc(tanh_done, 1)

        def round_h(l, s, par, p):
            act.wait_ge(h_ready, 2 * (STEPS * l + s) + p + 1)
            a.activation(a_hi[:, H_AT + 2 * par + p, :], conv[:, par, p, 0, :], ACT.Copy).then_inc(h_hi, 1)

        def finish_step(l, s, par, j):
            if j == 0:
                gate_tanh(l, s, par, 1)
            if j == 1:
                round_h(l, s, par, 0)
            if j == 2:
                round_h(l, s, par, 1)

        def mlp_step(l, s, par, used):
            first, i, per, count = used
            for j in range(6):
                if j < count:
                    ahead(l, first + j, i, per)
                if count == 6:
                    finish_step(l, s - 1, 1 - par, j)
                if j == 3:
                    conv_begin(l, s, par, 0)
                if j == 4:
                    conv_begin(l, s, par, 1)
                if j == 5:
                    gate_tanh(l, s, par, 0)

        act.dma_start(all_params[:], params).then_inc(params_loaded, 16)
        act.dma_start(rope[:], rope_in).then_inc(params_loaded, 16)
        act.dma_start(lam_in[:], lam_rows.partition_broadcast(P)).then_inc(params_loaded, 16)
        act.sem_inc(block_read, READ_AT_START)

        with act.Fori(0, DEPTH) as l:
            per_layer = 2 + 2 * 4
            kept = act_step.enter(l, per_layer)
            n1, n2 = 2 * l, 2 * l + 1
            first_piece(l, 0)
            first_piece(l, 1)
            act.wait_ge(now_ready, l + 1)
            norm_round(n1, 0, ATTN_BANKS, a_hi, G_ATTN)
            norm_round(n1, 1, ATTN_BANKS, a_hi, G_ATTN)
            norm_stats(0, x_ready, 4 * l + 2)
            first_piece(l, 2)
            norm_round(n1, 2, ATTN_BANKS, a_hi, G_ATTN)
            norm_round(n1, 3, ATTN_BANKS, a_hi, G_ATTN)
            first_piece(l, 3)
            norm_stats(1, x_ready, 4 * l + 4)
            first_piece(l, 4)
            first_piece(l, 5)
            a.preload_act_table_set("natural_log_exp_and_others")
            act.wait_ge(r_ready, n1 + 1)
            with act.Fori(0, 2) as i:
                for b in range(3):
                    B = 3 * i + b
                    for j in range(PER_BLOCK):
                        ahead(l, PER_BLOCK * b + j, i, 3 * PER_BLOCK)
                        if j >= 2:
                            m = j - 2
                            read_block(l, B, m, QKV_BANKS[b][m], PER_BLOCK * B, qkv[:, m, bass.ds(B * COLS, COLS)],
                                       2 if b == 0 else 0)
            act.wait_ge(f_summed, l + 1)
            a.activation(f_row[:], ps[OUT_BANK][0:4, 0:S], ACT.Copy).then_inc(f_copied, 1)
            act.wait_ge(lam_sums, l + 1)
            a.activation(lam[:, 2:4], lam[:, 0:2], ACT.Exp).then_inc(lam_exps, 1)
            act.wait_ge(f_biased, l + 1)
            act_step.link(act, a.activation(logf[:, 1, :], logf[:, 0, :], ACT.Abs))
            act_step.link(act, a.activation(logf[:, 1, :], logf[:, 1, :], ACT.Exp, scale=-1.0))
            a.activation(logf[:, 1, :], logf[:, 1, :], ACT.Ln, bias=1.0).then_inc(f_logs, 1)
            with act.Fori(0, 2) as i:
                kept_turn = act_step.enter(i, 4)
                unit = UNITS * l + 4 * i
                for tick in range(TICKS + 1):
                    for u, (turn, score, third, values) in enumerate(UNIT_TICKS):
                        if tick == turn:
                            read_turned(unit + u, u)
                        if u == SB:
                            if tick in (score, score + 1):
                                stick_log(l, i, tick - score)
                            if tick == third:
                                stick_exp(l, i, 0)
                                stick_exp(l, i, 1)
                        else:
                            if tick in (score, score + 1):
                                softmax_exp(l, i, u, tick - score)
                            if tick == third:
                                k = 8 * l + 4 * i + TURNS[u]
                                for c in range(2 if u == FX else 1):
                                    read_prob(k + c, u, c)
                        if tick == values:
                            col = (O_DIFF + 2 * P * i, O_DIFF + 2 * P * i + P, O_STICK + P * i, O_FOX + P * i)[u]
                            read_out(unit + u, col)
                    if tick % 8 in (6, 0) and tick:
                        b, m = (tick - 1) // 8, int(tick % 8 == 0)
                        B = QKV_BLOCKS + 3 * i + b
                        read_block(l, B, m, m, PER_BLOCK * B, gates[:, m, bass.ds((3 * i + b) * COLS, COLS)], 0)
                    for j in range(3 * PER_BLOCK):
                        if SPLIT_TICKS[j] == tick:
                            ahead(l, P_GATES + j, i, 3 * PER_BLOCK)
                act_step.leave(kept_turn, 2, 4)
            for i in range(4):
                round_pair(o_turned, 4 * l + i + 1, O_BANKS[i], b_hi, i, o_hi)
            a.preload_act_table_set("exp_and_others")
            for j in range(OUT_BLOCKS):
                for m in range(MT):
                    g = gate_cols(m, j)
                    a.activation(g, g, ACT.Tanh, scale=0.5).then_inc(gates_ready, 1)
                for k in range(2):
                    ahead(l, P_BRANCH + PER_BLOCK * j + k)
                if j == 1:
                    for i in range(2):
                        round_pair(mixed_turned, 4 * l + i + 1, i, a_hi, i, mixed_hi)
                for k in range(2, PER_BLOCK):
                    ahead(l, P_BRANCH + PER_BLOCK * j + k)
            ahead(l, P_OUT)
            ahead(l, P_OUT + 1)
            for i in (2, 3):
                round_pair(mixed_turned, 4 * l + i + 1, 2 + i, a_hi, i, mixed_hi)
            for k in range(2, 6):
                ahead(l, P_OUT + k)
            norm_stats(0, mix_added, 4 * l + 2)
            norm_round(n2, 0, FFN_BANKS, b_hi, G_FFN)
            norm_round(n2, 1, FFN_BANKS, b_hi, G_FFN)
            ahead(l, P_OUT + 6)
            norm_round(n2, 2, FFN_BANKS, b_hi, G_FFN)
            norm_round(n2, 3, FFN_BANKS, b_hi, G_FFN)
            norm_stats(1, mix_added, 4 * l + 4)
            ahead(l, P_OUT + 7)
            act.wait_ge(r_spread, l + 1)
            a.activation(r_row[:], ps[6][:, 0:S], ACT.Copy).then_inc(r_row_ready, 1)
            mlp_step(l, 0, 0, (P_FFN, 0, 0, 4))
            with act.Fori(0, 4) as i:
                for k in range(2):
                    mlp_step(l, 2 * i + k + 1, (k + 1) % 2, (P_FFN + 4 + 6 * k, i, 12, 6))
            for s in (STEPS - 2, STEPS - 1):
                mlp_step(l, s, s % 2, (P_FFN + 4 + 6 * (s - 1), 0, 0, 6))
            for j in range(3):
                finish_step(l, STEPS - 1, (STEPS - 1) % 2, j)
            act_step.leave(kept, DEPTH, per_layer)
        norm_stats(0, x_ready, 4 * DEPTH + 2)
        norm_stats(1, x_ready, 4 * DEPTH + 4)
        act.wait_ge(r_last, 1)
        act.wait_ge(xg_ready, 1)
        a.activation(rows[:, 0, :], rows[:, 0, :], ACT.Copy, scale=norm[:, 2, 0:1]).then_inc(y_ready[0], 1)

    @block.vector
    def _(dve):
        v = nc.vector

        def rest(l, n, slot):
            dve.wait_ge(hi_ready, l * PIECES + n + 1)
            v.tensor_tensor(w_lo[:, slot, :], raw[:, slot, :], w_hi[:, slot, :].bitcast(F32), ALU.subtract) \
                .then_inc(split_done, 1)

        def ahead(l, used, i=0, per=0):
            n = used + RING
            if n < PIECES:
                rest(l, n + i * per, n % RING)

        def inverse_root(cols):
            mean, y, t = norm[:, 1, 0:cols], norm[:, 2, 0:cols], norm[:, 3, 0:cols]
            dve_step.link(dve, v.tensor_scalar(y.bitcast(I32), mean.bitcast(I32), -0.5, float(0x5F3759DF),
                                               ALU.mult, ALU.add))
            for _ in range(3):
                dve_step.link(dve, v.tensor_tensor(t, y, mean, ALU.mult))
                dve_step.link(dve, v.scalar_tensor_tensor(out=t, in0=t, scalar=-0.5, in1=y, op0=ALU.mult, op1=ALU.mult))
                last = v.scalar_tensor_tensor(out=y, in0=t, scalar=1.5, in1=y, op0=ALU.add, op1=ALU.mult)
                if _ < 2:
                    dve_step.link(dve, last)
            return last

        def norm_factor(n):
            dve.wait_ge(squares_ready, 2 * n + 2)
            mean = norm[:, 1, 0:MT]
            dve_step.link(dve, v.tensor_tensor(mean, norm[:, 0, 0:MT], norm[:, 0, MT:2 * MT], ALU.add))
            dve_step.link(dve, v.tensor_scalar(mean, mean, 1.0 / D, EPS, ALU.mult, ALU.add))
            return inverse_root(MT)

        def keep_factor(n):
            dve_step.link(dve, norm_factor(n))
            v.tensor_copy(r_tok[:, 0:MT], norm[:, 2, 0:MT])
            v.tensor_scalar(r_tok[:, MT:2 * MT], norm[:, 2, 0:MT], HD ** -0.5, None, ALU.mult).then_inc(r_ready, 1)

        def norm_rest(n, i, banks, hi, lo, gain):
            dve.wait_ge(norm_hi, 4 * n + i + 1)
            for k in range(2):
                kc = 2 * i + k
                ins = v.scalar_tensor_tensor(out=lo[:, kc, :], in0=ps[banks[i]][:, k * S:(k + 1) * S],
                                             scalar=now[:, gain + kc:gain + kc + 1],
                                             in1=hi[:, kc, :].bitcast(F32), op0=ALU.mult, op1=ALU.subtract)
            ins.then_inc(norm_lo, 1)

        def rest_pair(ready, value, bank, hi, lo, i, done):
            dve.wait_ge(ready, value)
            v.tensor_tensor(pair(lo, i), ps[bank][:], pair(hi, i).bitcast(F32), ALU.subtract).then_inc(done, 1)

        def decays(l, i):
            dve.wait_ge(logf_ready, l + 1)
            for c in range(2):
                head = 2 * i + c
                v.tensor_scalar(decay[:, c, 0:2 * P], tri_ones[:], logf[:, 2, bass.ds(head, 1)], None, ALU.mult)
                ins = v.tensor_scalar(decay[:, c, 2 * P:3 * P], tri_ones[:, 0:P], logf[:, 2, bass.ds(head + 4, 1)],
                                      None, ALU.mult)
            ins.then_inc(decay_ready, 1)

        def softmax_max(l, i, u, c):
            dve.wait_ge(scores_ready, 2 * (UNITS * l + 4 * i + u) + c + 1)
            sc = score_bank(u, c)
            for q, (lo, hi) in enumerate(((0, P), (P, 3 * P))):
                col = 2 * c + q
                ins = v.tensor_reduce(stats[:, u % 2, 0, col:col + 1], sc[:, lo:hi], AX.X, ALU.max, negate=True)
            ins.then_inc(max_ready, 1)

        def softmax_scale(l, i, u, c):
            dve.wait_ge(exps_done, 2 * (6 * l + 3 * i + SOFT[u]) + c + 1)
            r = stats[:, u % 2, 2, 2 * c:2 * c + 2]
            dve_step.link(dve, v.reciprocal(r, stats[:, u % 2, 1, 2 * c:2 * c + 2]))
            parts = ((0, P), (P, 3 * P))
            if u != FX and c == 1:
                dve_step.link(dve, v.tensor_scalar(r, r, lam[:, 7:8], None, ALU.mult))
                for q, (lo, hi) in enumerate(parts):
                    ins = v.scalar_tensor_tensor(out=prob[:, u % 2, 0, lo:hi], in0=prob[:, u % 2, 1, lo:hi],
                                                 scalar=r[:, q:q + 1], in1=prob[:, u % 2, 0, lo:hi],
                                                 op0=ALU.mult, op1=ALU.add)
            else:
                for q, (lo, hi) in enumerate(parts):
                    p = prob[:, u % 2, c, lo:hi]
                    ins = v.tensor_scalar(p, p, r[:, q:q + 1], None, ALU.mult)
            if u == FX or c == 1:
                ins.then_inc(prob_ready, 1)
            else:
                dve_step.link(dve, ins)

        def subln_square(l, i):
            dve.wait_ge(out_read, UNITS * l + 4 * i + D1 + 1)
            both = o_all[:, :, bass.ds(O_DIFF + 2 * P * i, 2 * P)]
            dve_step.link(dve, v.tensor_tensor(square, both, both, ALU.mult))
            dve_step.link(dve, v.tensor_reduce(norm[:, 0, :].rearrange("p (m h) -> p m h", m=MT),
                                               square.rearrange("p m (h n) -> p m h n", h=2), AX.X, ALU.add))

        def subln_scale(l, i):
            dve_step.link(dve, v.tensor_scalar(norm[:, 1, :], norm[:, 0, :], 1.0 / (2 * HD), EPS, ALU.mult, ALU.add))
            dve_step.link(dve, inverse_root(4))
            for m in range(MT):
                for h in range(2):
                    o = o_all[:, m, bass.ds(O_DIFF + 2 * P * i + P * h, P)]
                    ins = v.scalar_tensor_tensor(out=o, in0=o, scalar=norm[:, 2, 2 * m + h:2 * m + h + 1],
                                                 in1=now[:, SUBLN:SUBLN + P], op0=ALU.mult, op1=ALU.mult)
            ins.then_inc(diff_ready, 1)

        def softplus(l, i, c):
            dve.wait_ge(stick_logs, 4 * l + 2 * i + c + 1)
            v.scalar_tensor_tensor(out=prob_t[:, 0, c, :], in0=score_bank(0, c)[:, 0:384], scalar=0.0,
                                   in1=prob[:, 0, c, :], op0=ALU.max, op1=ALU.add).then_inc(stick_softplus, 1)

        def scale_hidden(l, s, par, p, piece):
            dve.wait_ge(piece_used, RING + PIECES * l + piece + 2 * p + 2)
            dve.wait_ge(r_row_ready, l + 1)
            v.tensor_tensor(hidden[:, p], ps[2 * par + p][:].rearrange("p (g t) -> p g t", g=2),
                            r_row[:].unsqueeze(1).broadcast_to([P, 2, S]), ALU.mult).then_inc(up_read, 1)

        def conv_finish(l, s, par, p):
            dve.wait_ge(conv_begun, 2 * (STEPS * l + s) + p + 1)
            for tap in (1, 0):
                back = 2 - tap
                for g in range(2):
                    c = 4 * (2 * p + g)
                    y = conv[:, par, p, g, back:S]
                    ins = v.scalar_tensor_tensor(out=y, in0=hidden[:, p, g, 0:S - back],
                                                 scalar=taps[:, par, c + tap:c + tap + 1], in1=y,
                                                 op0=ALU.mult, op1=ALU.add)
                if tap:
                    dve_step.link(dve, ins)
            ins.then_inc(conv_done, 1)

        def gate_value(l, s, par, p):
            dve.wait_ge(tanh_done, 2 * (STEPS * l + s) + p + 1)
            t, gate, value = squash[:, par, p, :], conv[:, par, p, 0, :], conv[:, par, p, 1, :]
            dve_step.link(dve, v.scalar_tensor_tensor(out=t, in0=t, scalar=1.0, in1=gate, op0=ALU.add, op1=ALU.mult))
            v.tensor_tensor(gate, t, value, ALU.mult).then_inc(h_ready, 1)

        def rest_h(l, s, par, p):
            dve.wait_ge(h_hi, 2 * (STEPS * l + s) + p + 1)
            v.tensor_tensor(a_lo[:, H_AT + 2 * par + p, :], conv[:, par, p, 0, :], a_hi[:, H_AT + 2 * par + p, :].bitcast(F32),
                            ALU.subtract).then_inc(h_lo, 1)

        def finish_step(l, s, par, j):
            if j == 0:
                gate_value(l, s, par, 0)
            if j == 1:
                gate_value(l, s, par, 1)
            if j == 2:
                rest_h(l, s, par, 0)
            if j == 3:
                rest_h(l, s, par, 1)

        def mlp_step(l, s, par, used):
            first, i, per, count = used
            for j in range(6):
                if j < count:
                    ahead(l, first + j, i, per)
                if count == 6:
                    finish_step(l, s - 1, 1 - par, j)
                if j in (2, 3):
                    scale_hidden(l, s, par, j - 2, first + i * per)
                if j in (4, 5):
                    conv_finish(l, s, par, j - 4)

        def add_out(ready, value, bank, m, j, done):
            dve.wait_ge(ready, value)
            part = x[:, m, j * COLS:(j + 1) * COLS]
            v.scalar_tensor_tensor(out=part, in0=ps[bank][:], scalar=0.5, in1=part,
                                   op0=ALU.mult, op1=ALU.add).then_inc(done, 1)

        dve.sem_inc(split_done, RING)
        dve.sem_inc(conv_done, 4)
        dve.sem_inc(up_read, 4)
        for j in range(2):
            dve.wait_ge(x_loaded[j], 16)
            dve.sem_inc(x_ready, 2)

        with dve.Fori(0, DEPTH) as l:
            n1, n2 = 2 * l, 2 * l + 1
            per_layer = 12 + 4 + 2 * IN_TURN + 12 + 2 * 2 * STEPS
            kept = dve_step.enter(l, per_layer)
            dve.wait_ge(now_ready, l + 1)
            norm_rest(n1, 0, ATTN_BANKS, a_hi, a_lo, G_ATTN)
            rest(l, 0, 0)
            norm_rest(n1, 1, ATTN_BANKS, a_hi, a_lo, G_ATTN)
            rest(l, 1, 1)
            norm_rest(n1, 2, ATTN_BANKS, a_hi, a_lo, G_ATTN)
            rest(l, 2, 2)
            norm_rest(n1, 3, ATTN_BANKS, a_hi, a_lo, G_ATTN)
            rest(l, 3, 3)
            keep_factor(n1)
            rest(l, 4, 4)
            rest(l, 5, 5)
            dve_step.link(dve, v.tensor_copy(wf_hi[:], now[:, WF:WF + 4 * KC]))
            v.tensor_tensor(wf_lo[:], now[:, WF:WF + 4 * KC], wf_hi[:].bitcast(F32), ALU.subtract) \
                .then_inc(wf_ready, 1)
            q_k = lam_in[:, bass.ds(l, 1), :].rearrange("p a (b c d) -> p (a b) c d", b=2, c=2)
            products = square[:, 0, 0:2 * HD].rearrange("p (b d) -> p b d", b=2)
            dve_step.link(dve, v.tensor_tensor(products, q_k[:, :, 0, :], q_k[:, :, 1, :], ALU.mult))
            v.tensor_reduce(lam[:, 0:2], products, AX.X, ALU.add).then_inc(lam_sums, 1)
            with dve.Fori(0, 2) as i:
                for b in range(3):
                    for j in range(PER_BLOCK):
                        ahead(l, PER_BLOCK * b + j, i, 3 * PER_BLOCK)
            dve.wait_ge(lam_exps, l + 1)
            dve_step.link(dve, v.tensor_tensor(lam[:, 4:5], lam[:, 3:4], lam[:, 2:3], ALU.subtract))
            first = lam_first[:, bass.ds(l, 1), :].rearrange("p a n -> p (a n)")
            v.tensor_tensor(lam[:, 7:8], lam[:, 4:5], first[:, 0:1], ALU.add)
            gain = now[:, SUBLN:SUBLN + P]
            dve_step.link(dve, v.tensor_scalar(gain, gain, first[:, 1:2], None, ALU.mult))
            dve.wait_ge(f_ready, l + 1)
            for m in range(MT):
                ins = v.scalar_tensor_tensor(out=logf[:, 0, 4 * m:4 * m + 4], in0=ps[OUT_BANK][:, 4 * m:4 * m + 4],
                                             scalar=r_tok[:, m:m + 1], in1=now[:, FBIAS:FBIAS + 4],
                                             op0=ALU.mult, op1=ALU.add)
            ins.then_inc(f_biased, 1)
            dve.wait_ge(f_logs, l + 1)
            v.scalar_tensor_tensor(out=logf[:, 2, :], in0=logf[:, 0, :], scalar=0.0, in1=logf[:, 1, :],
                                   op0=ALU.min, op1=ALU.subtract).then_inc(logf_ready, 1)
            with dve.Fori(0, 2) as i:
                kept_turn = dve_step.enter(i, IN_TURN)
                for tick in range(TICKS + 1):
                    for u, (turn, score, third, values) in enumerate(UNIT_TICKS):
                        c = tick - score
                        if u == SB:
                            if c in (0, 1):
                                softplus(l, i, c)
                        else:
                            if c in (0, 1):
                                softmax_max(l, i, u, c)
                            if c - 1 in (0, 1):
                                softmax_scale(l, i, u, c - 1)
                    if tick == 6:
                        decays(l, i)
                    if tick == SUBLN_TICK - 1:
                        subln_square(l, i)
                    if tick == SUBLN_TICK:
                        subln_scale(l, i)
                    for j in range(3 * PER_BLOCK):
                        if SPLIT_TICKS[j] == tick:
                            ahead(l, P_GATES + j, i, 3 * PER_BLOCK)
                dve_step.leave(kept_turn, 2, IN_TURN)
            for i in range(4):
                rest_pair(o_hi, 4 * l + i + 1, O_BANKS[i], b_hi, b_lo, i, o_lo)
            for j in range(OUT_BLOCKS):
                for m in range(MT):
                    dve.wait_ge(gates_ready, 4 * l + 2 * j + m + 1)
                    if j == 1:
                        dve.wait_ge(mixed_ready, 4 * l + m + 1)
                    for b in range(3):
                        if m == 0:
                            dve.wait_ge(branch_ready, 6 * l + 3 * j + b + 1)
                        else:
                            dve.wait_ge(piece_used, RING + PIECES * l + P_BRANCH + PER_BLOCK * j + (1, 3, 4)[b])
                        v.scalar_tensor_tensor(out=gated[m][b], in0=gate_cols(m, j)[:, 2 - b, :], scalar=1.0,
                                               in1=ps[2 + 3 * m + b][:], op0=ALU.add, op1=ALU.mult) \
                            .then_inc(branch_read, 1)
                    if m == 0:
                        if j == 1:
                            for i in range(2):
                                rest_pair(mixed_hi, 4 * l + i + 1, i, a_hi, a_lo, i, mixed_lo)
                        ahead(l, P_BRANCH + PER_BLOCK * j)
                        ahead(l, P_BRANCH + PER_BLOCK * j + 1)
                for k in range(2, PER_BLOCK):
                    ahead(l, P_BRANCH + PER_BLOCK * j + k)
            ahead(l, P_OUT)
            ahead(l, P_OUT + 1)
            for i in (2, 3):
                rest_pair(mixed_hi, 4 * l + i + 1, 2 + i, a_hi, a_lo, i, mixed_lo)
            out_half = HALVES * l + QKV_BLOCKS + GATE_BLOCKS
            out_used = RING + PIECES * l + P_OUT
            ahead(l, P_OUT + 2)
            ahead(l, P_OUT + 3)
            add_out(half_ready, out_half + 1, 0, 0, 0, mix_added)
            add_out(piece_used, out_used + 6, 1, 1, 0, mix_added)
            ahead(l, P_OUT + 4)
            ahead(l, P_OUT + 5)
            add_out(half_ready, out_half + 2, 2, 0, 1, mix_added)
            norm_rest(n2, 0, FFN_BANKS, b_hi, b_lo, G_FFN)
            add_out(piece_used, out_used + 8, 3, 1, 1, mix_added)
            norm_rest(n2, 1, FFN_BANKS, b_hi, b_lo, G_FFN)
            norm_rest(n2, 2, FFN_BANKS, b_hi, b_lo, G_FFN)
            norm_rest(n2, 3, FFN_BANKS, b_hi, b_lo, G_FFN)
            ahead(l, P_OUT + 6)
            keep_factor(n2)
            ahead(l, P_OUT + 7)
            mlp_step(l, 0, 0, (P_FFN, 0, 0, 4))
            with dve.Fori(0, 4) as i:
                kept_turn = dve_step.enter(i, 8)
                for k in range(2):
                    mlp_step(l, 2 * i + k + 1, (k + 1) % 2, (P_FFN + 4 + 6 * k, i, 12, 6))
                dve_step.leave(kept_turn, 4, 8)
            for s in (STEPS - 2, STEPS - 1):
                mlp_step(l, s, s % 2, (P_FFN + 4 + 6 * (s - 1), 0, 0, 6))
            for j in range(4):
                finish_step(l, STEPS - 1, (STEPS - 1) % 2, j)
            for k, (j, m) in enumerate(((0, 0), (0, 1), (1, 0), (1, 1))):
                if k < 3:
                    add_out(down_ready, 3 * l + k + 1, 4 + 2 * m + j, m, j, x_ready)
                else:
                    add_out(piece_used, RING + PIECES * (l + 1), 4 + 2 * m + j, m, j, x_ready)
            dve_step.leave(kept, DEPTH, per_layer)
        norm_factor(2 * DEPTH).then_inc(r_last, 1)
        dve.wait_ge(r_last, 1)
        dve.wait_ge(xg_ready, 1)
        v.tensor_scalar(rows[:, 1, :], rows[:, 1, :], norm[:, 2, 1:2], None, ALU.mult).then_inc(y_ready[1], 1)

    @block.tensor
    def _(pe):
        t = nc.tensor

        def product(out_ap, left, right, start, stop):
            (lh, ll), (rh, rl) = left, right
            t.matmul(out_ap, lh, rh, start=start, stop=False, skip_group_check=True)
            t.matmul(out_ap, lh, rl, start=False, stop=False, skip_group_check=True)
            return t.matmul(out_ap, ll, rh, start=False, stop=stop, skip_group_check=True)

        def left_of(act_pair, kc, m):
            return [z[:, kc, m * P:(m + 1) * P] for z in act_pair]

        def right_of(slot, k):
            return [z[:, slot, k * COLS:(k + 1) * COLS] for z in (w_hi, w_lo)]

        def quarter(l, n, slot, act_pair, bank, m, i):
            if m == 0:
                pe.wait_ge(split_done, RING + PIECES * l + n + 1)
            for k in range(2):
                ins = product(bank[:], left_of(act_pair, 2 * i + k, m), right_of(slot, k),
                              start=(i == 0 and k == 0), stop=(i == 3 and k == 1))
            if m == 1:
                ins.then_inc(piece_used, 1)
            elif i == 3:
                ins.then_inc(half_ready, 1)

        def turn_rows(src, i, bank, done):
            for k in range(2):
                for m in range(MT):
                    ins = t.transpose(ps[bank][:, k * S + m * P:k * S + (m + 1) * P],
                                      src[:, m, (2 * i + k) * P:(2 * i + k + 1) * P], ident[:])
            ins.then_inc(done, 1)

        def turn_x(ready, value, pairs, banks):
            pe.wait_ge(ready, value)
            for i in pairs:
                turn_rows(x, i, banks[i], x_turned)

        def turn_unit(unit, u):
            pe.wait_ge(unit_staged, unit + 1)
            for b in range(4):
                ins = t.transpose(ps[QK_BANK][:, b * P:(b + 1) * P], staged[:, u % 2, b * P:(b + 1) * P], ident[:])
            ins.then_inc(unit_turned, 1)

        def heads_of(u, c):
            both = turned[c * HD:(c + 1) * HD, u % 2, :]
            return both[:, 0:S], both[:, S:2 * S]

        def add(out_ap, left, right, start=False, stop=False):
            return t.matmul(out_ap, left, right, start=start, stop=stop, skip_group_check=True)

        def softmax_scores(l, i, u):
            pe.wait_ge(turned_ready, UNITS * l + 4 * i + u + 1)
            if u == FX:
                pe.wait_ge(decay_ready, 2 * l + i + 1)
            for c in range(2):
                q, k = heads_of(u, c)
                sc = score_bank(u, c)
                add(sc[:, 0:P], q[:, 0:P], k[:, 0:P], start=True)
                if u == FX:
                    add(sc[:, 0:P], decay[:, c, 0:P], ones_later[:, P:2 * P])
                add(sc[:, 0:P], ident_bf[:], mask_bf[:], stop=True)
                add(sc[:, P:3 * P], q[:, P:S], k, start=True)
                if u == FX:
                    add(sc[:, P:2 * P], decay[:, c, P:2 * P], ones_later[:, P:2 * P])
                    add(sc[:, P:3 * P], decay[:, c, 2 * P:3 * P], ones_later[:])
                add(sc[:, 2 * P:3 * P], ident_bf[:], mask_bf[:], stop=True).then_inc(scores_ready, 1)

        def turn_prob(l, i, u):
            k = 8 * l + 4 * i + TURNS[u]
            for c in range(2 if u == FX else 1):
                pe.wait_ge(prob_ready, k + c + 1)
                for b in range(3):
                    ins = t.transpose(score_bank(u, c)[:, b * P:(b + 1) * P], prob[:, u % 2, c, b * P:(b + 1) * P],
                                      ident[:])
                ins.then_inc(prob_turned, 1)

        def stick_scores(l, i):
            pe.wait_ge(turned_ready, UNITS * l + 4 * i + SB + 1)
            for c in range(2):
                q, k = heads_of(SB, c)
                sc = score_bank(SB, c)
                add(sc[:, 0:S], k[:, 0:P], q, start=True)
                add(sc[:, S:3 * P], k[:, P:S], q[:, P:S]).then_inc(scores_ready, 1)

        def stick_sum(l, i):
            for c in range(2):
                pe.wait_ge(stick_masked, 4 * l + 2 * i + c + 1)
                sc, sp = score_bank(SB, c), prob_t[:, 0, c, :]
                add(sc[:, 0:S], neg_from[:, 0:P], sp[:, 0:S])
                add(sc[:, P:S], neg_from[:, P:2 * P], sp[:, S:3 * P])
                add(sc[:, S:3 * P], neg_from[:, 0:P], sp[:, S:3 * P])
                add(sc[:, 0:P], ident_bf[:], later_bf[:])
                add(sc[:, S:3 * P], ident_bf[:], later_bf[:], stop=True).then_inc(stick_sums, 1)

        def values(l, i, u):
            if u == SB:
                pe.wait_ge(stick_exps, 4 * l + 2 * i + 2)
            else:
                pe.wait_ge(prob_t_ready, 8 * l + 4 * i + TURNS[u] + (2 if u == FX else 1))
            v_col = (V_DIFF + 2 * P * i, V_DIFF + 2 * P * i + P, V_STICK + P * i, V_FOX + P * i)[u]
            width = P if u in (D0, D1) else HD
            for c in range(P // width):
                w = prob[:, 0, c, :] if u == SB else prob_t[:, u % 2, c, :]
                v = [qkv[:, m, bass.ds(v_col + c * width, width)] for m in range(MT)]
                o = ps[OUT_BANK]
                add(o[:, c * width:(c + 1) * width], w[:, 0:P], v[0], start=True, stop=True)
                o1 = o[:, P + c * width:P + (c + 1) * width]
                add(o1, w[:, P:2 * P], v[0], start=True)
                ins = add(o1, w[:, 2 * P:3 * P], v[1], stop=True)
            ins.then_inc(unit_done, 1)

        def branch(l, j, m, i):
            b = (0, 1, 1, 2)[i]
            if m == 0 and j == 0:
                pe.wait_ge(o_lo, 4 * l + i + 1)
            if i != 2 and j == 1:
                pe.wait_ge(branch_read, 12 * l + 3 * m + b + 1)
            n = P_BRANCH + PER_BLOCK * j + i
            if m == 0:
                pe.wait_ge(split_done, RING + PIECES * l + n + 1)
            for k in range(2):
                ins = product(ps[2 + 3 * m + b][:], left_of((b_hi, b_lo), 2 * i + k, m),
                              right_of(n % RING, k), start=(i != 2 and k == 0), stop=(i != 1 and k == 1))
            if m == 1:
                ins.then_inc(piece_used, 1)
            elif i != 1:
                ins.then_inc(branch_ready, 1)

        def chunk(l, s, par, j, kcs, slot):
            p, g = j // 2, j % 2
            for kc in kcs:
                ins = product(ps[2 * par + p][:, g * S:(g + 1) * S],
                              [z[:, slot, kc * P:(kc + 1) * P] for z in (w_hi, w_lo)],
                              [z[:, kc, :] for z in (b_hi, b_lo)],
                              start=(kc == 0 and g == 0), stop=(kc == KC - 1 and g == 1))
            return ins

        def up(l, s, par, slots, piece):
            for j in range(4):
                if j % 2 == 0:
                    pe.wait_ge(up_read, 2 * (STEPS * l + s) + j // 2 + 1)
                pe.wait_ge(split_done, RING + PIECES * l + piece + j + 1)
                chunk(l, s, par, j, range(KC), slots[j]).then_inc(piece_used, 1)

        def spread_factor(l):
            pe.wait_ge(r_ready, 2 * l + 2)
            for m in range(MT):
                ins = add(ps[6][:, m * P:(m + 1) * P], r_tok[:, m:m + 1].broadcast_to([P, P]), ident[:],
                          start=True, stop=True)
            ins.then_inc(r_spread, 1)

        def first_up(l, n2, slots):
            for j in range(4):
                pe.wait_ge(split_done, RING + PIECES * l + P_FFN + j + 1)
                for i in range(2):
                    if j == 0:
                        pe.wait_ge(norm_lo, 4 * n2 + i + 1)
                    chunk(l, 0, 0, j, (2 * i, 2 * i + 1), slots[j])
                if j == 0:
                    turn_x(mix_added, 4 * l + 4, (2, 3), FFN_BANKS)
            for j in range(4):
                for i in (2, 3):
                    if j == 0:
                        pe.wait_ge(norm_lo, 4 * n2 + i + 1)
                    last = chunk(l, 0, 0, j, (2 * i, 2 * i + 1), slots[j])
                last.then_inc(piece_used, 1)
                if j == 1:
                    spread_factor(l)

        def down(l, s, par, slots, piece, final=False):
            for p in range(2):
                pe.wait_ge(h_lo, 2 * (STEPS * l + s) + p + 1)
                pe.wait_ge(split_done, RING + PIECES * l + piece + p + 1)
                ending = final and p == 1
                for k, (j, m) in enumerate(((0, 0), (0, 1), (1, 0), (1, 1))):
                    if ending and k == 3:
                        turn_x(x_ready, 4 * (l + 1) + 2, (0, 1), ATTN_BANKS)
                    ins = product(ps[4 + 2 * m + j][:], left_of((a_hi, a_lo), H_AT + 2 * par + p, m),
                                  right_of(slots[p], j), start=False, stop=ending)
                    if ending and k < 3:
                        ins.then_inc(down_ready, 1)
                ins.then_inc(piece_used, 1)
            if final:
                turn_x(x_ready, 4 * (l + 1) + 4, (2, 3), ATTN_BANKS)

        def slots_from(n, count):
            return [(n + k) % RING for k in range(count)]

        pe.sem_inc(piece_used, RING)
        pe.sem_inc(unit_turned, 2)
        pe.wait_ge(ident_ready, 1)
        turn_x(x_ready, 2, (0, 1), ATTN_BANKS)
        turn_x(x_ready, 4, (2, 3), ATTN_BANKS)
        with pe.Fori(0, DEPTH) as l:
            n1, n2 = 2 * l, 2 * l + 1
            with pe.Fori(0, 2) as turn:
                for b in range(3):
                    B = 3 * turn + b
                    for m, i in QUARTERS:
                        if i == 0:
                            pe.wait_ge(block_read, 2 * ((QKV_BLOCKS + GATE_BLOCKS) * l + B) + m + 1)
                        if m == 0 and b == 0:
                            pe.wait_ge(norm_lo, 4 * n1 + i + 1)
                        quarter(l, PER_BLOCK * B + i, (PER_BLOCK * b + i) % RING, (a_hi, a_lo), ps[QKV_BANKS[b][m]],
                                m, i)
            pe.wait_ge(wf_ready, l + 1)
            pe.wait_ge(block_read, READ_AT_START + 2 * ((QKV_BLOCKS + GATE_BLOCKS) * l + QKV_BLOCKS - 1))
            for kc in range(KC):
                ins = product(ps[OUT_BANK][0:4, 0:S], [z[:, 4 * kc:4 * kc + 4] for z in (wf_hi, wf_lo)],
                              [z[:, kc, :] for z in (a_hi, a_lo)], start=(kc == 0), stop=(kc == KC - 1))
            ins.then_inc(f_summed, 1)
            pe.wait_ge(f_copied, l + 1)
            for m in range(MT):
                ins = add(ps[OUT_BANK][:, 4 * m:4 * m + 4], f_row[:, m * P:(m + 1) * P], ident[0:4, 0:4],
                          start=True, stop=True)
            ins.then_inc(f_ready, 1)
            pe.wait_ge(consts_ready, 1)
            with pe.Fori(0, 2) as turn:
                for tick in range(TICKS):
                    for u, (first, score, third, value) in enumerate(UNIT_TICKS):
                        if tick == first:
                            turn_unit(UNITS * l + 4 * turn + u, u)
                        if tick == score:
                            stick_scores(l, turn) if u == SB else softmax_scores(l, turn, u)
                        if tick == third:
                            stick_sum(l, turn) if u == SB else turn_prob(l, turn, u)
                        if tick == value:
                            values(l, turn, u)
                    b = tick // 8
                    m, i = QUARTERS[tick % 8]
                    B = 3 * turn + b
                    if i == 0:
                        pe.wait_ge(block_read, 4 + 2 * ((QKV_BLOCKS + GATE_BLOCKS) * l + QKV_BLOCKS + B) + m + 1)
                    quarter(l, P_GATES + PER_BLOCK * B + i, (PER_BLOCK * b + i) % RING, (a_hi, a_lo), ps[m], m, i)
            pe.wait_ge(out_read, UNITS * l + 4 + SB + 1)
            turn_rows(o_all, 0, O_BANKS[0], o_turned)
            pe.wait_ge(diff_ready, 2 * l + 2)
            turn_rows(o_all, 1, O_BANKS[1], o_turned)
            turn_rows(o_all, 2, O_BANKS[2], o_turned)
            pe.wait_ge(out_read, UNITS * (l + 1))
            turn_rows(o_all, 3, O_BANKS[3], o_turned)
            for j in range(OUT_BLOCKS):
                for k, (m, i) in enumerate(QUARTERS):
                    if j == 1 and k == 4:
                        pe.wait_ge(mixed_ready, 4 * l + 2)
                        pe.wait_ge(block_read, READ_AT_START + 2 * (QKV_BLOCKS + GATE_BLOCKS) * (l + 1))
                        for pair_ in (0, 1):
                            turn_rows(rows, pair_, MIXED_BANKS[pair_], mixed_turned)
                    branch(l, j, m, i)
            for half in range(2):
                for j in range(OUT_BLOCKS):
                    for m in range(MT):
                        if half == 0 and j == 1:
                            pe.wait_ge(branch_read, 12 * l + 6 + m + 1)
                        if half == 0 and (j, m) == (1, 1):
                            pe.wait_ge(mixed_ready, 4 * l + 4)
                            for pair_ in (2, 3):
                                turn_rows(rows, pair_, MIXED_BANKS[pair_], mixed_turned)
                        if half == 1 and (j, m) == (1, 1):
                            turn_x(mix_added, 4 * l + 2, (0, 1), FFN_BANKS)
                        for i in (2 * half, 2 * half + 1):
                            if j == 0 and m == 0:
                                pe.wait_ge(mixed_lo, 4 * l + i + 1)
                            n = P_OUT + 4 * half + 2 * j + i % 2
                            quarter(l, n, n % RING, (a_hi, a_lo), ps[2 * j + m], m, i)
            first_up(l, n2, slots_from(P_FFN, 4))
            pe.wait_ge(r_row_ready, l + 1)
            for b in range(4):
                add(ps[4 + b][:], zero_bf[:, 0:P], zero_bf[:], start=True)
            with pe.Fori(0, 4) as turn:
                for k in range(2):
                    s, n = 2 * turn + k + 1, P_FFN + 4 + 6 * k
                    up(l, s, (k + 1) % 2, slots_from(n, 4), n + 12 * turn)
                    down(l, s - 1, k % 2, slots_from(n + 4, 2), n + 12 * turn + 4)
            for s in (STEPS - 2, STEPS - 1):
                n = P_FFN + 4 + 6 * (s - 1)
                up(l, s, s % 2, slots_from(n, 4), n)
                down(l, s - 1, (s - 1) % 2, slots_from(n + 4, 2), n + 4)
            n = PIECES - 2
            down(l, STEPS - 1, (STEPS - 1) % 2, slots_from(n, 2), n, final=True)

    block.__exit__(None, None, None)


def _blocks(w):
    n = w.shape[1] // COLS
    return w.reshape(PER_BLOCK, 2, P, n, COLS).transpose(3, 0, 2, 1, 4).reshape(n * PER_BLOCK, P, PIECE)


def _stream(w_in, w_br, w_out, w_up, w_down):
    cuts = {name: (lo, hi) for name, lo, hi in (
        ("fq", 0, 256), ("fk", 256, 512), ("fv", 512, 768), ("dq", 768, 1280), ("dk", 1280, 1792),
        ("dv", 1792, 2304), ("sq", 2304, 2560), ("sk", 2560, 2816), ("sv", 2816, 3072))}
    order = ("sq", "fq", "sk", "fk", "sv", "fv", "dq", "dk", "dv")
    parts = [w_in[:, cuts[k][0]:cuts[k][1]] for k in order] + [w_in[:, QKV + 4:], w_br]
    blocks = [_blocks(np.concatenate(parts, axis=1))]
    halves = _blocks(w_out).reshape(OUT_BLOCKS, 2, 2, P, PIECE).transpose(1, 0, 2, 3, 4)
    blocks.append(halves.reshape(-1, P, PIECE))
    ups = w_up.reshape(KC, P, 2, STEPS, 2, P).transpose(3, 4, 2, 1, 0, 5).reshape(STEPS, 4, P, PIECE)
    downs = w_down.reshape(STEPS, 2, P, D)
    blocks.append(ups[0])
    for s in range(1, STEPS):
        blocks += [ups[s], downs[s - 1]]
    blocks.append(downs[STEPS - 1])
    return np.concatenate(blocks, axis=0)


def _params(l, g_attn, w_in, g_ffn, bias, subln, conv_w, conv_b):
    def tall(v):
        return v.reshape(-1, P).T

    def wide(v):
        return np.broadcast_to(v.reshape(1, -1), (P, v.size))

    wf = w_in[:, QKV:QKV + 4].reshape(KC, P, 4).transpose(1, 0, 2).reshape(P, 4 * KC)
    conv = np.concatenate([conv_w, conv_b[None]], axis=0)
    conv = conv.reshape(4, 2, STEPS, 2, P).transpose(4, 2, 3, 1, 0).reshape(P, 16 * STEPS)
    return np.concatenate([tall(g_attn), tall(g_ffn), wf, wide(bias), wide(subln), conv], axis=1)


def kernel(x, attn_norm_g, w_in, forget_bias, lam_q1, lam_k1, lam_q2, lam_k2, diff_subln_g, w_br_fox,
           w_br_diff, w_br_stick, w_out, ffn_norm_g, w_up, conv_w, conv_b, w_down, final_norm_g):
    import concourse.bacc as _bacc
    from concourse.bass_utils import run_bass_kernel_spmd as _run

    a = {k: np.asarray(v) for k, v in locals().items() if not k.startswith("_")}
    stream, params = [], []
    for l in range(DEPTH):
        w_br = np.concatenate([a["w_br_stick"][l], a["w_br_diff"][l], a["w_br_fox"][l]], axis=0)
        stream.append(_stream(a["w_in"][l], w_br, a["w_out"][l], a["w_up"][l], a["w_down"][l]))
        params.append(_params(l, a["attn_norm_g"][l], a["w_in"][l], a["ffn_norm_g"][l], a["forget_bias"][l],
                              a["diff_subln_g"][l], a["conv_w"][l], a["conv_b"][l]))
    lam_rows = np.stack([a["lam_q1"], a["lam_k1"], a["lam_q2"], a["lam_k2"]], axis=1)
    half = HD // 8
    inv_freq = np.float32(500000.0) ** (-np.arange(0, 2 * half, 2, dtype=np.float32) / np.float32(2 * half))
    ang = np.arange(S, dtype=np.float32)[:, None] * inv_freq[None, :].astype(np.float32)
    table = np.stack([np.cos(ang), np.sin(ang)]).astype(np.float32).reshape(2, MT, P, half).transpose(2, 0, 1, 3)
    table = np.broadcast_to(table[:, :, None, :, None, :], (P, 2, 2, MT, 2, half)).reshape(P, 2, 64)

    nc = _bacc.Bacc("TRN2", target_bir_lowering=False, num_devices=1)
    arrays = {
        "x_in": a["x"].reshape(S, D),
        "stream": np.concatenate(stream, axis=0),
        "params": np.ascontiguousarray(np.stack(params, axis=1)),
        "lam_rows": np.ascontiguousarray(lam_rows.reshape(DEPTH, LAMS)),
        "rope_in": np.ascontiguousarray(table),
        "g_final": np.ascontiguousarray(a["final_norm_g"]),
    }
    args = [nc.dram_tensor(n, v.shape, F32, kind="ExternalInput").ap() for n, v in arrays.items()]
    args.append(nc.dram_tensor("y", (S, D), F32, kind="ExternalOutput").ap())
    build(nc, *args)
    r = _run(nc, [arrays], core_ids=[0])
    return r.results[0]["y"].reshape(1, S, D)
```

```python
import math

import concourse.bass as bass
import numpy as np
from concourse import mybir

F32 = mybir.dt.float32
F32R = mybir.dt.float32r
BF16 = mybir.dt.bfloat16
I32 = mybir.dt.int32
ALU = mybir.AluOpType
ACT = mybir.ActivationFunctionType
AX = mybir.AxisListType

P = 128
D = 1024
S = 256
DEPTH = 2
HD = 64
MT = S // P
KC = D // P
COLS = 512
PIECE = 2 * COLS
RING = 6
QKV = 3072
QKV_BLOCKS = QKV // COLS
GATE_BLOCKS = 3 * D // COLS
OUT_BLOCKS = D // COLS
D_FF = 2816
STEPS = D_FF // (2 * P)
PER_BLOCK = 4
P_GATES = PER_BLOCK * QKV_BLOCKS
P_BRANCH = P_GATES + PER_BLOCK * GATE_BLOCKS
P_OUT = P_BRANCH + PER_BLOCK * OUT_BLOCKS
P_FFN = P_OUT + PER_BLOCK * OUT_BLOCKS
PIECES = P_FFN + 6 * STEPS
ZEROS = 64
H_AT = KC // 2
HALVES = QKV_BLOCKS + GATE_BLOCKS + OUT_BLOCKS
EPS = 1e-6
NEG = -1e30
READ_AT_START = 6
UNITS = 8

STICK, FOX, DIFF = 0, 256, 1536
V_STICK, V_FOX, V_DIFF = 1024, 1280, 2560
G_ATTN, G_FFN, WF, FBIAS, SUBLN, NOW = 0, 8, 16, 48, 52, 180
CONV = NOW
PARAMS = CONV + 16 * STEPS
LAMS = 4 * HD
O_STICK, O_DIFF, O_FOX = 0, 256, 768

LAM_INIT = [0.8 - 0.6 * math.exp(-0.3 * l) for l in range(DEPTH)]

QUARTERS = [(0, 0), (0, 1), (1, 0), (1, 1), (0, 2), (0, 3), (1, 2), (1, 3)]

TICKS = 8 * 3
D0, D1, SB, FX = range(4)
UNIT_TICKS = [(2, 4, 8, 10), (7, 9, 13, 15), (11, 13, 17, 20), (15, 17, 21, 23)]
SUBLN_TICK = 20
IN_TURN = 2 * 4 + 2 + 3 + 10
SOFT = {D0: 0, D1: 1, FX: 2}
TURNS = {D0: 0, D1: 1, FX: 2}
SPLIT_TICKS = [1, 3, 5, 7, 9, 11, 13, 15, 17, 19, 21, 23]


class Tally:

    def __init__(self, sem):
        self.sem, self.base, self.n = sem, 0, 0

    def link(self, eng, ins):
        ins.then_inc(self.sem, 1)
        self.n += 1
        eng.wait_ge(self.sem, self.base + self.n)

    def enter(self, i, per_turn):
        kept = (self.base, self.n)
        self.base, self.n = self.base + self.n + i * per_turn, 0
        return kept

    def leave(self, kept, turns, per_turn):
        assert self.n == per_turn, (self.n, per_turn)
        self.base, self.n = kept[0], kept[1] + turns * per_turn


def build(nc, x_in, stream, params, lam_rows, rope_in, g_final, out):
    def sb(name, shape, dt=F32):
        return nc.alloc_sbuf_tensor(name, shape, dt)

    def sem(name):
        return nc.alloc_semaphore(name)

    raw = sb("raw", [P, RING, PIECE])
    w_hi = sb("w_hi", [P, RING, PIECE], F32R)
    w_lo = sb("w_lo", [P, RING, PIECE], F32R)
    x = sb("x", [P, MT, D])
    a_hi = sb("a_hi", [P, KC, S], F32R)
    a_lo = sb("a_lo", [P, KC, S], F32R)
    b_hi = sb("b_hi", [P, KC, S], F32R)
    b_lo = sb("b_lo", [P, KC, S], F32R)
    qkv = sb("qkv", [P, MT, QKV])
    gates = sb("gates", [P, MT, 3 * D])
    rows = sb("rows", [P, MT, D])
    o_all = sb("o_all", [P, MT, D])
    all_params = sb("all_params", [P, DEPTH, PARAMS])
    now = sb("now", [P, NOW])
    taps = sb("taps", [P, 2, 16])
    wf = sb("wf", [P, KC, 8], F32R)
    rope = sb("rope", [P, 2, 64])
    staged = sb("staged", [P, 2, 2 * MT * P])
    turned = sb("turned", [P, 2, 4 * P])
    prob = sb("prob", [P, 2, 2, 384])
    prob_t = rows[:, :, 0:768].rearrange("p u (c n) -> p u c n", c=2)
    square = rows[:, :, 768:D]
    f_row = square[0:8, 1, :]
    decay = sb("decay", [P, 2, 3 * P])
    logf = sb("logf", [P, 3, 8])
    stats = sb("stats", [P, 2, 3, 4])
    norm = sb("norm", [P, 4, 4])
    r_tok = sb("r_tok", [P, 4])
    r_row = sb("r_row", [P, S])
    lam_in = sb("lam_in", [P, DEPTH, LAMS])
    lam_first = sb("lam_first", [P, DEPTH, 2])
    lam = sb("lam", [P, 8])
    ident = sb("ident", [P, P])
    fold = sb("fold", [8, 4])
    ident_bf = sb("ident_bf", [P, P], BF16)
    mask_bf = sb("mask_bf", [P, P], BF16)
    later_bf = sb("later_bf", [P, P], BF16)
    later = sb("later", [P, P])
    tri_ones = sb("tri_ones", [P, 2 * P])
    ones_later = sb("ones_later", [P, 2 * P])
    neg_from = sb("neg_from", [P, 2 * P])
    zero_bf = sb("zero_bf", [P, P], BF16)
    conv = gates[:, 0, 0:2048].rearrange("p (s c g t) -> p s c g t", s=2, c=2, g=2)
    squash = gates[:, 1, 0:1024].rearrange("p (s c t) -> p s c t", s=2, c=2)
    g_fin = gates[:, 1, 2048:3072]
    unused = (gates[:, 1, 1024:2048], gates[:, 0, 2048:3072])
    hidden = gates[:, 0, 2048:3072].rearrange("p (c g t) -> p c g t", c=2, g=2)
    gated = [[qkv[:, m, b * COLS:(b + 1) * COLS] for b in range(3)] for m in range(MT)]

    ps = [nc.alloc_psum_tensor(f"bank{b}", [P, COLS], F32) for b in range(8)]
    QK_BANK, OUT_BANK = 2, 7
    QKV_BANKS = ((0, 1), (6, 7), (4, 5))
    ATTN_BANKS, FFN_BANKS = (2, 3, 4, 5), (6, 7, 4, 5)
    O_BANKS, MIXED_BANKS = (2, 3, 4, 7), (0, 1, 4, 5)

    def score_bank(unit, c):
        return ps[3 + 2 * (unit % 2) + c]

    raw_landed = [sem(f"raw_landed{i}") for i in range(RING)]
    landed_uses = [len(range(i, PIECES, RING)) for i in range(RING)]
    hi_ready = sem("hi_ready")
    split_done = sem("split_done")
    piece_used = sem("piece_used")
    x_loaded = [sem(f"x_loaded{j}") for j in range(2)]
    gains_loaded = sem("gains_loaded")
    rope_loaded = sem("rope_loaded")
    conv_loaded = sem("conv_loaded")
    lam_loaded = sem("lam_loaded")
    g_loaded = sem("g_loaded")
    consts_ready = sem("consts_ready")
    lam_sums = sem("lam_sums")
    lam_exps = sem("lam_exps")
    ident_ready = sem("ident_ready")
    x_ready = sem("x_ready")
    mix_added = sem("mix_added")
    squares_ready = sem("squares_ready")
    x_turned = sem("x_turned")
    r_ready = sem("r_ready")
    r_spread = sem("r_spread")
    r_row_ready = sem("r_row_ready")
    norm_hi = sem("norm_hi")
    norm_lo = sem("norm_lo")
    now_ready = sem("now_ready")
    half_ready = sem("half_ready")
    block_read = sem("block_read")
    wf_ready = sem("wf_ready")
    f_summed = sem("f_summed")
    f_copied = sem("f_copied")
    f_ready = sem("f_ready")
    f_biased = sem("f_biased")
    f_logs = sem("f_logs")
    logf_ready = sem("logf_ready")
    unit_staged = sem("unit_staged")
    unit_turned = sem("unit_turned")
    turned_ready = sem("turned_ready")
    scores_ready = sem("scores_ready")
    max_ready = sem("max_ready")
    exps_done = sem("exps_done")
    prob_ready = sem("prob_ready")
    prob_turned = sem("prob_turned")
    prob_t_ready = sem("prob_t_ready")
    stick_logs = sem("stick_logs")
    stick_softplus = sem("stick_softplus")
    stick_masked = sem("stick_masked")
    stick_sums = sem("stick_sums")
    stick_exps = sem("stick_exps")
    decay_ready = sem("decay_ready")
    unit_done = sem("unit_done")
    out_read = sem("out_read")
    diff_ready = sem("diff_ready")
    o_turned = sem("o_turned")
    o_hi = sem("o_hi")
    o_lo = sem("o_lo")
    gates_ready = sem("gates_ready")
    branch_ready = sem("branch_ready")
    branch_read = sem("branch_read")
    mixed_ready = sem("mixed_ready")
    mixed_turned = sem("mixed_turned")
    mixed_hi = sem("mixed_hi")
    mixed_lo = sem("mixed_lo")
    taps_ready = sem("taps_ready")
    conv_begun = sem("conv_begun")
    up_read = sem("up_read")
    conv_done = sem("conv_done")
    tanh_done = sem("tanh_done")
    h_ready = sem("h_ready")
    h_hi = sem("h_hi")
    h_lo = sem("h_lo")
    down_ready = sem("down_ready")
    xg_ready = sem("xg_ready")
    r_last = sem("r_last")
    y_ready = [sem(f"y_ready{m}") for m in range(MT)]
    y_stored = sem("y_stored")
    act_step = Tally(sem("act_step"))
    dve_step = Tally(sem("dve_step"))
    pool_step = Tally(sem("pool_step"))

    def pair(hi_lo, i):
        return hi_lo[:, 2 * i:2 * i + 2, :].rearrange("p k t -> p (k t)")

    def gate_cols(m, j):
        return gates[:, m, :].rearrange("p (b n) -> p b n", b=3)[:, :, j * COLS:(j + 1) * COLS]

    def diagonals(tile):
        return tile.rearrange("p (b n) -> p b n", b=3)[:, 0:3:2, :]

    def load_x(eng, j):
        cols = slice(j * COLS, (j + 1) * COLS)
        eng.dma_start(x[:, :, cols], x_in.rearrange("(m p) n -> p m n", p=P)[:, :, cols]).then_inc(x_loaded[j], 16)

    block = nc.Block()
    block.__enter__()

    @block.sync
    def _(sp):
        load_x(sp, 0)

        def load(l, n, slot, free):
            sp.wait_ge(split_done, free)
            sp.dma_start(raw[:, slot, :], stream[bass.ds(l * PIECES + n, 1)].rearrange("a p n -> (a p) n")) \
                .then_inc(raw_landed[slot], 16)

        with sp.Fori(0, DEPTH) as l:
            for k in range(RING):
                load(l, k, k, l * PIECES + RING + min(k + 1 - PIECES % RING, 0))
            with sp.Fori(1, PIECES // RING) as r:
                for k in range(RING):
                    load(l, r * RING + k, k, l * PIECES + r * RING + k + 1)
            for k in range(PIECES % RING):
                n = PIECES - PIECES % RING + k
                load(l, n, k, l * PIECES + n + 1)
        sp.wait_ge(mix_added, 4 * DEPTH)
        sp.dma_start(g_fin, g_final.partition_broadcast(P)).then_inc(g_loaded, 16)
        for j in range(2):
            cols = slice(j * COLS, (j + 1) * COLS)
            for m in (1, 0):
                sp.wait_ge(y_ready[m], j + 1)
                sp.dma_start(out[m * P:(m + 1) * P, cols], rows[:, m, cols]).then_inc(y_stored, 16)
        sp.wait_ge(y_stored, 16 * 2 * MT)

    @block.gpsimd
    def _(pool):
        g = nc.gpsimd
        pool_step.link(pool, g.memset(ident[:], 0.0))

        def cut(tile, op, fill, row, col, base=0):
            return g.affine_select(out=tile, in_=tile, pattern=[[col, tile.shape[1]]], compare_op=op, fill=fill,
                                   base=base, channel_multiplier=row)

        cut(ident[:], ALU.not_equal, 1.0, 1, -1).then_inc(ident_ready, 1)
        for l in range(DEPTH):
            g.memset(lam_first[:, l, 0:1], -LAM_INIT[l])
            g.memset(lam_first[:, l, 1:2], 1.0 - LAM_INIT[l])
        for tile, value in ((ident_bf, 0.0), (mask_bf, 0.0), (later_bf, 0.0), (later, 1.0),
                            (tri_ones, 1.0), (ones_later, 1.0), (neg_from, -1.0), (zero_bf, 0.0), (fold, 0.0)):
            last = g.memset(tile[:], value)
        pool_step.link(pool, last)
        cut(ident_bf[:], ALU.not_equal, 1.0, 1, -1)
        cut(mask_bf[:], ALU.is_ge, NEG, 1, -1)
        cut(later_bf[:], ALU.is_gt, NEG, -1, 1)
        cut(later[:], ALU.is_gt, 0.0, -1, 1)
        cut(tri_ones[:, 0:P], ALU.is_ge, 0.0, -1, 1)
        cut(ones_later[:, P:2 * P], ALU.is_gt, 0.0, 1, -1)
        cut(neg_from[:, 0:P], ALU.is_ge, 0.0, 1, -1)
        pool_step.link(pool, cut(fold[:], ALU.not_equal, 1.0, 1, -1))
        cut(fold[:], ALU.not_equal, 1.0, 1, -1, base=-4).then_inc(consts_ready, 1)

        def stage(u, unit, q_col):
            pool.wait_ge(unit_turned, unit + 1)
            dst = staged[:, u % 2, :].rearrange("p (a m n) -> p a m n", a=2, m=MT)
            for a in range(2):
                ins = g.tensor_copy(dst[:, a], qkv[:, :, bass.ds(q_col + a * COLS, P)])
            return ins

        def rotate(u):
            t = staged[:, u % 2, :].rearrange("p (g n) -> p g n", n=HD)
            t1, t2 = t[:, :, 0:8], t[:, :, 8:16]
            cos, sin = (rope[:, i, :].rearrange("p (g n) -> p g n", n=8) for i in range(2))
            p = [rope_tmp[:, i, :].rearrange("p (g n) -> p g n", n=8) for i in range(4)]
            g.tensor_tensor(p[0], t1, cos, ALU.mult)
            g.tensor_tensor(p[1], t2, sin, ALU.mult)
            g.tensor_tensor(p[2], t2, cos, ALU.mult)
            pool_step.link(pool, g.tensor_tensor(p[3], t1, sin, ALU.mult))
            g.tensor_tensor(t1, p[0], p[1], ALU.subtract)
            return g.tensor_tensor(t2, p[2], p[3], ALU.add)

        rope_tmp = sb("rope_tmp", [P, 4, 64])

        def keep_later(tile):
            d = diagonals(tile)
            return g.tensor_tensor(d, d, later[:].unsqueeze(1).broadcast_to([P, 2, P]), ALU.mult)

        def attention_turn(l, i):
            unit = UNITS * l + 4 * i
            pool.wait_ge(block_read, READ_AT_START + 2 * ((QKV_BLOCKS + GATE_BLOCKS) * l + QKV_BLOCKS))
            for u in (D0, D1):
                pool_step.link(pool, stage(u, unit + u, DIFF + 2 * P * i + P * u))
                rotate(u).then_inc(unit_staged, 1)
            stage(SB, unit + SB, STICK + P * i).then_inc(unit_staged, 1)
            stage(FX, unit + FX, FOX + P * i).then_inc(unit_staged, 1)
            for c in range(2):
                pool.wait_ge(stick_softplus, 4 * l + 2 * i + c + 1)
                keep_later(prob_t[:, 0, c, :]).then_inc(stick_masked, 1)

        def merge(l, j, m):
            pool.wait_ge(branch_read, 12 * l + 6 * j + 3 * m + 3)
            stick, diff, fox = gated[m]
            pool_step.link(pool, g.tensor_tensor(stick, stick, diff, ALU.add))
            g.tensor_tensor(rows[:, m, j * COLS:(j + 1) * COLS], stick, fox, ALU.add).then_inc(mixed_ready, 1)

        def step_taps(l, s, par):
            pool.wait_ge(conv_done, 2 * (l * STEPS + s) + 2)
            g.tensor_copy(taps[:, par, :], all_params[:, bass.ds(l, 1), bass.ds(s * 16 + CONV, 16)]
                          .rearrange("p a n -> p (a n)")).then_inc(taps_ready, 1)

        pool.wait_ge(gains_loaded, 16)
        with pool.Fori(0, DEPTH) as l:
            per_layer = 2 * 4 + MT * OUT_BLOCKS
            kept = pool_step.enter(l, per_layer)
            g.tensor_copy(now[:], all_params[:, bass.ds(l, 1), 0:NOW].rearrange("p a n -> p (a n)")) \
                .then_inc(now_ready, 1)
            pool.wait_ge(rope_loaded, 16)
            with pool.Fori(0, 2) as i:
                kept_turn = pool_step.enter(i, 4)
                attention_turn(l, i)
                pool_step.leave(kept_turn, 2, 4)
            for j in range(OUT_BLOCKS):
                for m in range(MT):
                    merge(l, j, m)
            pool.wait_ge(conv_loaded, 16)
            pool.wait_ge(norm_lo, 4 * (2 * l + 2))
            step_taps(l, 0, 0)
            with pool.Fori(0, 4) as i:
                for k in range(2):
                    step_taps(l, 2 * i + k + 1, (k + 1) % 2)
            for s in (STEPS - 2, STEPS - 1):
                step_taps(l, s, s % 2)
            pool_step.leave(kept, DEPTH, per_layer)
        pool.wait_ge(g_loaded, 16)
        for j in range(2):
            cols = slice(j * COLS, (j + 1) * COLS)
            pool.wait_ge(x_ready, 4 * DEPTH + 2 * j + 2)
            for m in range(MT - j):
                ins = g.tensor_tensor(rows[:, m, cols], x[:, m, cols], g_fin[:, cols], ALU.mult)
            ins.then_inc(xg_ready, 1)

    @block.scalar
    def _(act):
        a = nc.scalar

        def round_piece(l, n, slot, r, free=None):
            act.wait_ge(raw_landed[slot], 16 * (l * landed_uses[slot] + r + 1))
            act.wait_ge(piece_used, l * PIECES + n + 1 if free is None else free)
            a.activation(w_hi[:, slot, :], raw[:, slot, :], ACT.Copy).then_inc(hi_ready, 1)

        def first_piece(l, k):
            before = PIECES - PIECES % RING + k - (0 if k < PIECES % RING else RING)
            round_piece(l, k, k, 0, free=RING + l * PIECES - (PIECES - before - 1))

        def ahead(l, used, i=0, per=0):
            n = used + RING
            if n < PIECES:
                round_piece(l, n + i * per, n % RING, n // RING + i * (per // RING))

        def norm_stats(j, ready, before):
            for m in range(MT):
                act.wait_ge(ready, before + 2 * j + m + 1)
                last = a.activation(unused[j][:, m * COLS:(m + 1) * COLS], x[:, m, j * COLS:(j + 1) * COLS], ACT.Square,
                                    accum_out=norm[:, 0, MT * j + m:MT * j + m + 1])
            last.then_inc(squares_ready, 1)

        def norm_round(n, i, banks, dst, gain):
            act.wait_ge(x_turned, 4 * n + i + 1)
            for k in range(2):
                kc = 2 * i + k
                ins = a.activation(dst[:, kc, :], ps[banks[i]][:, k * S:(k + 1) * S], ACT.Copy,
                                   scale=now[:, gain + kc:gain + kc + 1])
            ins.then_inc(norm_hi, 1)

        def read_block(l, b, m, bank, piece, dst, factor):
            if m == 0:
                act.wait_ge(half_ready, HALVES * l + b + 1)
            else:
                act.wait_ge(piece_used, RING + PIECES * l + piece + PER_BLOCK)
            a.activation(dst, ps[bank][:], ACT.Copy, scale=r_tok[:, factor + m:factor + m + 1]).then_inc(block_read, 1)

        def read_turned(unit, u):
            act.wait_ge(unit_turned, 2 + unit + 1)
            a.activation(turned[:, u % 2, :], ps[QK_BANK][:], ACT.Copy).then_inc(turned_ready, 1)

        def softmax_exp(l, i, u, c):
            k = 6 * l + 3 * i + SOFT[u]
            act.wait_ge(max_ready, 2 * k + c + 1)
            sc = score_bank(u, c)
            for q, (lo, hi) in enumerate(((0, P), (P, 3 * P))):
                col = 2 * c + q
                ins = a.activation(prob[:, u % 2, c, lo:hi], sc[:, lo:hi], ACT.Exp,
                                   bias=stats[:, u % 2, 0, col:col + 1],
                                   accum_out=stats[:, u % 2, 1, col:col + 1])
            ins.then_inc(exps_done, 1)

        def read_prob(k, u, c):
            act.wait_ge(prob_turned, k + 1)
            a.activation(prob_t[:, u % 2, c, :], score_bank(u, c)[:, 0:384], ACT.Copy).then_inc(prob_t_ready, 1)

        def read_out(unit, col):
            act.wait_ge(unit_done, unit + 1)
            a.activation(o_all[:, :, bass.ds(col, P)], ps[OUT_BANK][:, 0:2 * P].rearrange("p (m n) -> p m n", m=MT),
                         ACT.Copy).then_inc(out_read, 1)

        def stick_log(l, i, c):
            act.wait_ge(scores_ready, 2 * (UNITS * l + 4 * i + SB) + c + 1)
            t = prob[:, 0, c, :]
            act_step.link(act, a.activation(t, score_bank(0, c)[:, 0:384], ACT.Abs))
            act_step.link(act, a.activation(t, t, ACT.Exp, scale=-1.0))
            a.activation(t, t, ACT.Ln, bias=1.0).then_inc(stick_logs, 1)

        def stick_exp(l, i, c):
            act.wait_ge(stick_sums, 4 * l + 2 * i + c + 1)
            a.activation(prob[:, 0, c, :], score_bank(0, c)[:, 0:384], ACT.Exp).then_inc(stick_exps, 1)

        def round_pair(ready, value, bank, dst, i, done):
            act.wait_ge(ready, value)
            a.activation(pair(dst, i), ps[bank][:], ACT.Copy).then_inc(done, 1)

        def conv_begin(l, s, par, p):
            act.wait_ge(up_read, 4 + 2 * (STEPS * l + s) + p + 1)
            if p == 0:
                act.wait_ge(taps_ready, STEPS * l + s + 1)
            for g in range(2):
                c = 4 * (2 * p + g)
                ins = a.activation(conv[:, par, p, g, :], hidden[:, p, g, :], ACT.Identity,
                                   scale=taps[:, par, c + 2:c + 3], bias=taps[:, par, c + 3:c + 4])
            ins.then_inc(conv_begun, 1)

        def gate_tanh(l, s, par, p):
            act.wait_ge(conv_done, 4 + 2 * (STEPS * l + s) + p + 1)
            a.activation(squash[:, par, p, :], conv[:, par, p, 0, :], ACT.Tanh, scale=0.5).then_inc(tanh_done, 1)

        def round_h(l, s, par, p):
            act.wait_ge(h_ready, 2 * (STEPS * l + s) + p + 1)
            a.activation(a_hi[:, H_AT + 2 * par + p, :], conv[:, par, p, 0, :], ACT.Copy).then_inc(h_hi, 1)

        def finish_step(l, s, par, j):
            if j == 0:
                gate_tanh(l, s, par, 1)
            if j == 1:
                round_h(l, s, par, 0)
            if j == 2:
                round_h(l, s, par, 1)

        def first_step(l):
            for j in range(4):
                ahead(l, P_FFN + j)
                if j < 2:
                    conv_begin(l, 0, 0, j)
                if j == 2:
                    gate_tanh(l, 0, 0, 0)

        def mlp_step(l, s, par, first, i, per):
            for j in range(6):
                ahead(l, first + j, i, per)
                finish_step(l, s - 1, 1 - par, j)
                if j == 3:
                    conv_begin(l, s, par, 0)
                if j == 4:
                    conv_begin(l, s, par, 1)
                if j == 5:
                    gate_tanh(l, s, par, 0)

        def last_step(l, s, par):
            ahead(l, PIECES - RING - 2)
            finish_step(l, s - 1, 1 - par, 0)
            ahead(l, PIECES - RING - 1)
            finish_step(l, s - 1, 1 - par, 1)
            finish_step(l, s - 1, 1 - par, 2)
            conv_begin(l, s, par, 0)
            conv_begin(l, s, par, 1)
            for p in range(2):
                gate_tanh(l, s, par, p)
                round_h(l, s, par, p)

        act.dma_start(all_params[:, :, 0:NOW], params[:, :, 0:NOW]).then_inc(gains_loaded, 16)
        load_x(act, 1)
        a.preload_act_table_set("exp_and_others")
        act.dma_start(lam_in[:], lam_rows.partition_broadcast(P)).then_inc(lam_loaded, 16)
        act.dma_start(rope[:], rope_in).then_inc(rope_loaded, 16)
        act.dma_start(all_params[:, :, NOW:PARAMS], params[:, :, NOW:PARAMS]).then_inc(conv_loaded, 16)
        act.sem_inc(block_read, READ_AT_START)

        with act.Fori(0, DEPTH) as l:
            per_layer = 2 + 2 * 4
            kept = act_step.enter(l, per_layer)
            n1, n2 = 2 * l, 2 * l + 1
            first_piece(l, 0)
            act.wait_ge(now_ready, l + 1)
            norm_round(n1, 0, ATTN_BANKS, a_hi, G_ATTN)
            norm_round(n1, 1, ATTN_BANKS, a_hi, G_ATTN)
            first_piece(l, 1)
            norm_round(n1, 2, ATTN_BANKS, a_hi, G_ATTN)
            norm_round(n1, 3, ATTN_BANKS, a_hi, G_ATTN)
            first_piece(l, 2)
            norm_stats(0, x_ready, 4 * l)
            first_piece(l, 3)
            norm_stats(1, x_ready, 4 * l)
            first_piece(l, 4)
            a.preload_act_table_set("natural_log_exp_and_others")
            act.wait_ge(r_ready, n1 + 1)
            with act.Fori(0, 2) as i:
                for b in range(3):
                    B = 3 * i + b
                    for j in range(PER_BLOCK):
                        ahead(l, PER_BLOCK * b + j - 1, i, 3 * PER_BLOCK)
                        if j >= 2:
                            m = j - 2
                            read_block(l, B, m, QKV_BANKS[b][m], PER_BLOCK * B, qkv[:, m, bass.ds(B * COLS, COLS)],
                                       2 if b == 0 else 0)
            act.wait_ge(f_summed, l + 1)
            a.activation(f_row[:], ps[OUT_BANK][0:8, 0:S], ACT.Copy).then_inc(f_copied, 1)
            act.wait_ge(lam_sums, l + 1)
            a.activation(lam[:, 2:4], lam[:, 0:2], ACT.Exp).then_inc(lam_exps, 1)
            act.wait_ge(f_biased, l + 1)
            act_step.link(act, a.activation(logf[:, 1, :], logf[:, 0, :], ACT.Abs))
            act_step.link(act, a.activation(logf[:, 1, :], logf[:, 1, :], ACT.Exp, scale=-1.0))
            a.activation(logf[:, 1, :], logf[:, 1, :], ACT.Ln, bias=1.0).then_inc(f_logs, 1)
            with act.Fori(0, 2) as i:
                kept_turn = act_step.enter(i, 4)
                unit = UNITS * l + 4 * i
                for tick in range(TICKS + 1):
                    for u, (turn, score, third, values) in enumerate(UNIT_TICKS):
                        if tick == turn:
                            read_turned(unit + u, u)
                        if u == SB:
                            if tick in (score, score + 1):
                                stick_log(l, i, tick - score)
                            if tick == third:
                                stick_exp(l, i, 0)
                                stick_exp(l, i, 1)
                        else:
                            if tick in (score, score + 1):
                                softmax_exp(l, i, u, tick - score)
                            if tick == third:
                                k = 8 * l + 4 * i + TURNS[u]
                                for c in range(2 if u == FX else 1):
                                    read_prob(k + c, u, c)
                        if tick == values:
                            col = (O_DIFF + 2 * P * i, O_DIFF + 2 * P * i + P, O_STICK + P * i, O_FOX + P * i)[u]
                            read_out(unit + u, col)
                    if tick % 8 in (6, 0) and tick:
                        b, m = (tick - 1) // 8, int(tick % 8 == 0)
                        B = QKV_BLOCKS + 3 * i + b
                        read_block(l, B, m, m, PER_BLOCK * B, gates[:, m, bass.ds((3 * i + b) * COLS, COLS)], 0)
                    for j in range(3 * PER_BLOCK):
                        if SPLIT_TICKS[j] == tick:
                            ahead(l, P_GATES + j - 1, i, 3 * PER_BLOCK)
                act_step.leave(kept_turn, 2, 4)
            for i in range(4):
                round_pair(o_turned, 4 * l + i + 1, O_BANKS[i], b_hi, i, o_hi)
            ahead(l, P_BRANCH - 1)
            a.preload_act_table_set("exp_and_others")
            for j in range(OUT_BLOCKS):
                for m in range(MT):
                    g = gate_cols(m, j)
                    a.activation(g, g, ACT.Tanh, scale=0.5).then_inc(gates_ready, 1)
                for k in range(2):
                    ahead(l, P_BRANCH + PER_BLOCK * j + k)
                if j == 1:
                    for i in range(2):
                        round_pair(mixed_turned, 4 * l + i + 1, MIXED_BANKS[i], a_hi, i, mixed_hi)
                for k in range(2, PER_BLOCK):
                    ahead(l, P_BRANCH + PER_BLOCK * j + k)
            ahead(l, P_OUT)
            ahead(l, P_OUT + 1)
            for i in (2, 3):
                round_pair(mixed_turned, 4 * l + i + 1, MIXED_BANKS[i], a_hi, i, mixed_hi)
            for k in range(2, 6):
                ahead(l, P_OUT + k)
            norm_stats(0, mix_added, 4 * l)
            norm_round(n2, 0, FFN_BANKS, b_hi, G_FFN)
            norm_round(n2, 1, FFN_BANKS, b_hi, G_FFN)
            ahead(l, P_OUT + 6)
            norm_round(n2, 2, FFN_BANKS, b_hi, G_FFN)
            norm_round(n2, 3, FFN_BANKS, b_hi, G_FFN)
            norm_stats(1, mix_added, 4 * l)
            ahead(l, P_OUT + 7)
            act.wait_ge(r_spread, l + 1)
            a.activation(r_row[:], ps[6][:, 0:S], ACT.Copy).then_inc(r_row_ready, 1)
            first_step(l)
            with act.Fori(0, 4) as i:
                for k in range(2):
                    mlp_step(l, 2 * i + k + 1, (k + 1) % 2, P_FFN + 4 + 6 * k, i, 12)
            mlp_step(l, STEPS - 2, STEPS % 2, P_FFN + 4 + 6 * (STEPS - 3), 0, 0)
            last_step(l, STEPS - 1, (STEPS - 1) % 2)
            act_step.leave(kept, DEPTH, per_layer)
        norm_stats(0, x_ready, 4 * DEPTH)
        norm_stats(1, x_ready, 4 * DEPTH)
        act.wait_ge(r_last, 1)
        for j in range(2):
            act.wait_ge(xg_ready, j + 1)
            y = rows[:, 0, j * COLS:(j + 1) * COLS]
            a.activation(y, y, ACT.Copy, scale=norm[:, 2, 0:1]).then_inc(y_ready[0], 1)

    @block.vector
    def _(dve):
        v = nc.vector

        def rest(l, n, slot):
            dve.wait_ge(hi_ready, l * PIECES + n + 1)
            v.tensor_tensor(w_lo[:, slot, :], raw[:, slot, :], w_hi[:, slot, :].bitcast(F32), ALU.subtract) \
                .then_inc(split_done, 1)

        def ahead(l, used, i=0, per=0):
            n = used + RING
            if n < PIECES:
                rest(l, n + i * per, n % RING)

        def inverse_root(cols):
            mean, y, t = norm[:, 1, 0:cols], norm[:, 2, 0:cols], norm[:, 3, 0:cols]
            dve_step.link(dve, v.tensor_scalar(y.bitcast(I32), mean.bitcast(I32), -0.5, float(0x5F3759DF),
                                               ALU.mult, ALU.add))
            for step in range(3):
                dve_step.link(dve, v.tensor_tensor(t, y, mean, ALU.mult))
                dve_step.link(dve, v.scalar_tensor_tensor(out=t, in0=t, scalar=-0.5, in1=y, op0=ALU.mult, op1=ALU.mult))
                last = v.scalar_tensor_tensor(out=y, in0=t, scalar=1.5, in1=y, op0=ALU.add, op1=ALU.mult)
                if step < 2:
                    dve_step.link(dve, last)
            return last

        def norm_factor(n):
            dve.wait_ge(squares_ready, 2 * n + 2)
            mean = norm[:, 1, 0:MT]
            dve_step.link(dve, v.tensor_tensor(mean, norm[:, 0, 0:MT], norm[:, 0, MT:2 * MT], ALU.add))
            dve_step.link(dve, v.tensor_scalar(mean, mean, 1.0 / D, EPS, ALU.mult, ALU.add))
            return inverse_root(MT)

        def keep_factor(n):
            dve_step.link(dve, norm_factor(n))
            v.tensor_copy(r_tok[:, 0:MT], norm[:, 2, 0:MT])
            v.tensor_scalar(r_tok[:, MT:2 * MT], norm[:, 2, 0:MT], HD ** -0.5, None, ALU.mult).then_inc(r_ready, 1)

        def norm_rest(n, i, banks, hi, lo, gain):
            dve.wait_ge(norm_hi, 4 * n + i + 1)
            for k in range(2):
                kc = 2 * i + k
                ins = v.scalar_tensor_tensor(out=lo[:, kc, :], in0=ps[banks[i]][:, k * S:(k + 1) * S],
                                             scalar=now[:, gain + kc:gain + kc + 1],
                                             in1=hi[:, kc, :].bitcast(F32), op0=ALU.mult, op1=ALU.subtract)
            ins.then_inc(norm_lo, 1)

        def rest_pair(ready, value, bank, hi, lo, i, done):
            dve.wait_ge(ready, value)
            v.tensor_tensor(pair(lo, i), ps[bank][:], pair(hi, i).bitcast(F32), ALU.subtract).then_inc(done, 1)

        def decays(l, i):
            dve.wait_ge(logf_ready, l + 1)
            for c in range(2):
                head = 2 * i + c
                v.tensor_scalar(decay[:, c, 0:2 * P], tri_ones[:], logf[:, 2, bass.ds(head, 1)], None, ALU.mult)
                ins = v.tensor_scalar(decay[:, c, 2 * P:3 * P], tri_ones[:, 0:P], logf[:, 2, bass.ds(head + 4, 1)],
                                      None, ALU.mult)
            ins.then_inc(decay_ready, 1)

        def softmax_max(l, i, u, c):
            dve.wait_ge(scores_ready, 2 * (UNITS * l + 4 * i + u) + c + 1)
            sc = score_bank(u, c)
            for q, (lo, hi) in enumerate(((0, P), (P, 3 * P))):
                col = 2 * c + q
                ins = v.tensor_reduce(stats[:, u % 2, 0, col:col + 1], sc[:, lo:hi], AX.X, ALU.max, negate=True)
            ins.then_inc(max_ready, 1)

        def softmax_scale(l, i, u, c):
            dve.wait_ge(exps_done, 2 * (6 * l + 3 * i + SOFT[u]) + c + 1)
            r = stats[:, u % 2, 2, 2 * c:2 * c + 2]
            dve_step.link(dve, v.reciprocal(r, stats[:, u % 2, 1, 2 * c:2 * c + 2]))
            parts = ((0, P), (P, 3 * P))
            if u != FX and c == 1:
                dve_step.link(dve, v.tensor_scalar(r, r, lam[:, 7:8], None, ALU.mult))
                for q, (lo, hi) in enumerate(parts):
                    ins = v.scalar_tensor_tensor(out=prob[:, u % 2, 0, lo:hi], in0=prob[:, u % 2, 1, lo:hi],
                                                 scalar=r[:, q:q + 1], in1=prob[:, u % 2, 0, lo:hi],
                                                 op0=ALU.mult, op1=ALU.add)
            else:
                for q, (lo, hi) in enumerate(parts):
                    p = prob[:, u % 2, c, lo:hi]
                    ins = v.tensor_scalar(p, p, r[:, q:q + 1], None, ALU.mult)
            if u == FX or c == 1:
                ins.then_inc(prob_ready, 1)
            else:
                dve_step.link(dve, ins)

        def subln_square(l, i):
            dve.wait_ge(out_read, UNITS * l + 4 * i + D1 + 1)
            both = o_all[:, :, bass.ds(O_DIFF + 2 * P * i, 2 * P)]
            dve_step.link(dve, v.tensor_tensor(square, both, both, ALU.mult))
            dve_step.link(dve, v.tensor_reduce(norm[:, 0, :].rearrange("p (m h) -> p m h", m=MT),
                                               square.rearrange("p m (h n) -> p m h n", h=2), AX.X, ALU.add))

        def subln_scale(l, i):
            dve_step.link(dve, v.tensor_scalar(norm[:, 1, :], norm[:, 0, :], 1.0 / (2 * HD), EPS, ALU.mult, ALU.add))
            dve_step.link(dve, inverse_root(4))
            for m in range(MT):
                for h in range(2):
                    o = o_all[:, m, bass.ds(O_DIFF + 2 * P * i + P * h, P)]
                    ins = v.scalar_tensor_tensor(out=o, in0=o, scalar=norm[:, 2, 2 * m + h:2 * m + h + 1],
                                                 in1=now[:, SUBLN:SUBLN + P], op0=ALU.mult, op1=ALU.mult)
            ins.then_inc(diff_ready, 1)

        def softplus(l, i, c):
            dve.wait_ge(stick_logs, 4 * l + 2 * i + c + 1)
            v.scalar_tensor_tensor(out=prob_t[:, 0, c, :], in0=score_bank(0, c)[:, 0:384], scalar=0.0,
                                   in1=prob[:, 0, c, :], op0=ALU.max, op1=ALU.add).then_inc(stick_softplus, 1)

        def scale_hidden(l, s, par, p, piece):
            dve.wait_ge(piece_used, RING + PIECES * l + piece + 2 * p + 2)
            dve.wait_ge(r_row_ready, l + 1)
            v.tensor_tensor(hidden[:, p], ps[2 * par + p][:].rearrange("p (g t) -> p g t", g=2),
                            r_row[:].unsqueeze(1).broadcast_to([P, 2, S]), ALU.mult).then_inc(up_read, 1)

        def conv_tap(l, s, par, p, tap):
            back = 2 - tap
            for g in range(2):
                c = 4 * (2 * p + g)
                y = conv[:, par, p, g, back:S]
                ins = v.scalar_tensor_tensor(out=y, in0=hidden[:, p, g, 0:S - back],
                                             scalar=taps[:, par, c + tap:c + tap + 1], in1=y,
                                             op0=ALU.mult, op1=ALU.add)
            return ins

        def conv_finish(l, s, par, p):
            dve.wait_ge(conv_begun, 2 * (STEPS * l + s) + p + 1)
            dve_step.link(dve, conv_tap(l, s, par, p, 1))
            conv_tap(l, s, par, p, 0).then_inc(conv_done, 1)

        def gate_value(l, s, par, p):
            dve.wait_ge(tanh_done, 2 * (STEPS * l + s) + p + 1)
            t, gate, value = squash[:, par, p, :], conv[:, par, p, 0, :], conv[:, par, p, 1, :]
            dve_step.link(dve, v.scalar_tensor_tensor(out=t, in0=t, scalar=1.0, in1=gate, op0=ALU.add, op1=ALU.mult))
            v.tensor_tensor(gate, t, value, ALU.mult).then_inc(h_ready, 1)

        def rest_h(l, s, par, p):
            dve.wait_ge(h_hi, 2 * (STEPS * l + s) + p + 1)
            v.tensor_tensor(a_lo[:, H_AT + 2 * par + p, :], conv[:, par, p, 0, :], a_hi[:, H_AT + 2 * par + p, :].bitcast(F32),
                            ALU.subtract).then_inc(h_lo, 1)

        def first_step(l):
            scale_hidden(l, 0, 0, 0, P_FFN)
            ahead(l, P_FFN)
            scale_hidden(l, 0, 0, 1, P_FFN)
            conv_finish(l, 0, 0, 0)
            ahead(l, P_FFN + 1)
            conv_finish(l, 0, 0, 1)
            ahead(l, P_FFN + 2)
            ahead(l, P_FFN + 3)

        def mlp_step(l, s, par, first, i, per):
            for j in range(6):
                if j in (0, 1):
                    gate_value(l, s - 1, 1 - par, j)
                if j in (1, 2):
                    rest_h(l, s - 1, 1 - par, j - 1)
                ahead(l, first + j, i, per)
                if j in (2, 3):
                    scale_hidden(l, s, par, j - 2, first + i * per)
                if j in (4, 5):
                    conv_finish(l, s, par, j - 4)

        def last_step(l, s, par, first):
            ahead(l, PIECES - RING - 2)
            gate_value(l, s - 1, 1 - par, 0)
            ahead(l, PIECES - RING - 1)
            gate_value(l, s - 1, 1 - par, 1)
            rest_h(l, s - 1, 1 - par, 0)
            scale_hidden(l, s, par, 0, first)
            rest_h(l, s - 1, 1 - par, 1)
            scale_hidden(l, s, par, 1, first)
            conv_finish(l, s, par, 0)
            gate_value(l, s, par, 0)
            dve.wait_ge(conv_begun, 2 * (STEPS * l + s) + 2)
            dve_step.link(dve, conv_tap(l, s, par, 1, 1))
            rest_h(l, s, par, 0)
            conv_tap(l, s, par, 1, 0).then_inc(conv_done, 1)
            gate_value(l, s, par, 1)
            rest_h(l, s, par, 1)

        def add_out(ready, value, bank, m, j, done):
            dve.wait_ge(ready, value)
            part = x[:, m, j * COLS:(j + 1) * COLS]
            v.scalar_tensor_tensor(out=part, in0=ps[bank][:], scalar=0.5, in1=part,
                                   op0=ALU.mult, op1=ALU.add).then_inc(done, 1)

        dve.sem_inc(split_done, RING)
        dve.sem_inc(conv_done, 4)
        dve.sem_inc(up_read, 4)

        with dve.Fori(0, DEPTH) as l:
            n1, n2 = 2 * l, 2 * l + 1
            per_layer = 12 + 4 + 2 * IN_TURN + 12 + 2 * 2 * STEPS
            kept = dve_step.enter(l, per_layer)
            dve.wait_ge(now_ready, l + 1)
            rest(l, 0, 0)
            norm_rest(n1, 0, ATTN_BANKS, a_hi, a_lo, G_ATTN)
            norm_rest(n1, 1, ATTN_BANKS, a_hi, a_lo, G_ATTN)
            rest(l, 1, 1)
            norm_rest(n1, 2, ATTN_BANKS, a_hi, a_lo, G_ATTN)
            rest(l, 2, 2)
            norm_rest(n1, 3, ATTN_BANKS, a_hi, a_lo, G_ATTN)
            rest(l, 3, 3)
            keep_factor(n1)
            rest(l, 4, 4)
            wf_now = now[:, WF:WF + 4 * KC].rearrange("p (k n) -> p k n", k=KC)
            dve_step.link(dve, v.tensor_copy(wf[:, :, 0:4], wf_now))
            v.tensor_tensor(wf[:, :, 4:8], wf_now, wf[:, :, 0:4].bitcast(F32), ALU.subtract).then_inc(wf_ready, 1)
            q_k = lam_in[:, bass.ds(l, 1), :].rearrange("p a (b c d) -> p (a b) c d", b=2, c=2)
            products = square[:, 0, 0:2 * HD].rearrange("p (b d) -> p b d", b=2)
            dve.wait_ge(lam_loaded, 16)
            dve_step.link(dve, v.tensor_tensor(products, q_k[:, :, 0, :], q_k[:, :, 1, :], ALU.mult))
            v.tensor_reduce(lam[:, 0:2], products, AX.X, ALU.add).then_inc(lam_sums, 1)
            with dve.Fori(0, 2) as i:
                for b in range(3):
                    for j in range(PER_BLOCK):
                        ahead(l, PER_BLOCK * b + j - 1, i, 3 * PER_BLOCK)
            dve.wait_ge(lam_exps, l + 1)
            dve_step.link(dve, v.tensor_tensor(lam[:, 4:5], lam[:, 3:4], lam[:, 2:3], ALU.subtract))
            first = lam_first[:, bass.ds(l, 1), :].rearrange("p a n -> p (a n)")
            v.tensor_tensor(lam[:, 7:8], lam[:, 4:5], first[:, 0:1], ALU.add)
            gain = now[:, SUBLN:SUBLN + P]
            dve_step.link(dve, v.tensor_scalar(gain, gain, first[:, 1:2], None, ALU.mult))
            dve.wait_ge(f_ready, l + 1)
            for m in range(MT):
                ins = v.scalar_tensor_tensor(out=logf[:, 0, 4 * m:4 * m + 4], in0=ps[OUT_BANK][:, 4 * m:4 * m + 4],
                                             scalar=r_tok[:, m:m + 1], in1=now[:, FBIAS:FBIAS + 4],
                                             op0=ALU.mult, op1=ALU.add)
            ins.then_inc(f_biased, 1)
            dve.wait_ge(f_logs, l + 1)
            v.scalar_tensor_tensor(out=logf[:, 2, :], in0=logf[:, 0, :], scalar=0.0, in1=logf[:, 1, :],
                                   op0=ALU.min, op1=ALU.subtract).then_inc(logf_ready, 1)
            with dve.Fori(0, 2) as i:
                kept_turn = dve_step.enter(i, IN_TURN)
                for tick in range(TICKS + 1):
                    for u, (turn, score, third, values) in enumerate(UNIT_TICKS):
                        c = tick - score
                        if u == SB:
                            if c in (0, 1):
                                softplus(l, i, c)
                        else:
                            if c in (0, 1):
                                softmax_max(l, i, u, c)
                            if c - 1 in (0, 1):
                                softmax_scale(l, i, u, c - 1)
                    if tick == 6:
                        decays(l, i)
                    if tick == SUBLN_TICK - 1:
                        subln_square(l, i)
                    if tick == SUBLN_TICK:
                        subln_scale(l, i)
                    for j in range(3 * PER_BLOCK):
                        if SPLIT_TICKS[j] == tick:
                            ahead(l, P_GATES + j - 1, i, 3 * PER_BLOCK)
                dve_step.leave(kept_turn, 2, IN_TURN)
            for i in range(4):
                rest_pair(o_hi, 4 * l + i + 1, O_BANKS[i], b_hi, b_lo, i, o_lo)
            ahead(l, P_BRANCH - 1)
            for j in range(OUT_BLOCKS):
                for m in range(MT):
                    dve.wait_ge(gates_ready, 4 * l + 2 * j + m + 1)
                    if j == 1:
                        dve.wait_ge(mixed_ready, 4 * l + m + 1)
                    for b in range(3):
                        if m == 0:
                            dve.wait_ge(branch_ready, 6 * l + 3 * j + b + 1)
                        else:
                            dve.wait_ge(piece_used, RING + PIECES * l + P_BRANCH + PER_BLOCK * j + (1, 3, 4)[b])
                        v.scalar_tensor_tensor(out=gated[m][b], in0=gate_cols(m, j)[:, 2 - b, :], scalar=1.0,
                                               in1=ps[2 + 3 * m + b][:], op0=ALU.add, op1=ALU.mult) \
                            .then_inc(branch_read, 1)
                    if m == 0:
                        if j == 1:
                            for i in range(2):
                                rest_pair(mixed_hi, 4 * l + i + 1, MIXED_BANKS[i], a_hi, a_lo, i, mixed_lo)
                        ahead(l, P_BRANCH + PER_BLOCK * j)
                        ahead(l, P_BRANCH + PER_BLOCK * j + 1)
                for k in range(2, PER_BLOCK):
                    ahead(l, P_BRANCH + PER_BLOCK * j + k)
            ahead(l, P_OUT)
            ahead(l, P_OUT + 1)
            for i in (2, 3):
                rest_pair(mixed_hi, 4 * l + i + 1, MIXED_BANKS[i], a_hi, a_lo, i, mixed_lo)
            out_half = HALVES * l + QKV_BLOCKS + GATE_BLOCKS
            out_used = RING + PIECES * l + P_OUT
            ahead(l, P_OUT + 2)
            ahead(l, P_OUT + 3)
            add_out(half_ready, out_half + 1, 0, 0, 0, mix_added)
            add_out(piece_used, out_used + 6, 1, 1, 0, mix_added)
            ahead(l, P_OUT + 4)
            ahead(l, P_OUT + 5)
            add_out(half_ready, out_half + 2, 2, 0, 1, mix_added)
            norm_rest(n2, 0, FFN_BANKS, b_hi, b_lo, G_FFN)
            norm_rest(n2, 1, FFN_BANKS, b_hi, b_lo, G_FFN)
            add_out(piece_used, out_used + 8, 3, 1, 1, mix_added)
            norm_rest(n2, 2, FFN_BANKS, b_hi, b_lo, G_FFN)
            norm_rest(n2, 3, FFN_BANKS, b_hi, b_lo, G_FFN)
            ahead(l, P_OUT + 6)
            keep_factor(n2)
            ahead(l, P_OUT + 7)
            first_step(l)
            with dve.Fori(0, 4) as i:
                kept_turn = dve_step.enter(i, 8)
                for k in range(2):
                    mlp_step(l, 2 * i + k + 1, (k + 1) % 2, P_FFN + 4 + 6 * k, i, 12)
                dve_step.leave(kept_turn, 4, 8)
            mlp_step(l, STEPS - 2, STEPS % 2, P_FFN + 4 + 6 * (STEPS - 3), 0, 0)
            last_step(l, STEPS - 1, (STEPS - 1) % 2, PIECES - 8)
            for k, (j, m) in enumerate(((0, 0), (0, 1), (1, 0), (1, 1))):
                if k < 3:
                    add_out(down_ready, 3 * l + k + 1, 4 + 2 * m + j, m, j, x_ready)
                else:
                    add_out(piece_used, RING + PIECES * (l + 1), 4 + 2 * m + j, m, j, x_ready)
            dve_step.leave(kept, DEPTH, per_layer)
        norm_factor(2 * DEPTH).then_inc(r_last, 1)
        dve.wait_ge(r_last, 1)
        dve.wait_ge(xg_ready, 1)
        y = rows[:, 1, 0:COLS]
        v.tensor_scalar(y, y, norm[:, 2, 1:2], None, ALU.mult).then_inc(y_ready[1], 1)
        dve.wait_ge(g_loaded, 16)
        v.scalar_tensor_tensor(out=rows[:, 1, COLS:D], in0=x[:, 1, COLS:D], scalar=norm[:, 2, 1:2],
                               in1=g_fin[:, COLS:D], op0=ALU.mult, op1=ALU.mult).then_inc(y_ready[1], 1)

    @block.tensor
    def _(pe):
        t = nc.tensor

        def product(out_ap, left, right, start, stop):
            (lh, ll), (rh, rl) = left, right
            t.matmul(out_ap, lh, rh, start=start, stop=False, skip_group_check=True)
            t.matmul(out_ap, lh, rl, start=False, stop=False, skip_group_check=True)
            return t.matmul(out_ap, ll, rh, start=False, stop=stop, skip_group_check=True)

        def left_of(act_pair, kc, m):
            return [z[:, kc, m * P:(m + 1) * P] for z in act_pair]

        def right_of(slot, k):
            return [z[:, slot, k * COLS:(k + 1) * COLS] for z in (w_hi, w_lo)]

        def quarter(l, n, slot, act_pair, bank, m, i):
            if m == 0:
                pe.wait_ge(split_done, RING + PIECES * l + n + 1)
            for k in range(2):
                ins = product(bank[:], left_of(act_pair, 2 * i + k, m), right_of(slot, k),
                              start=(i == 0 and k == 0), stop=(i == 3 and k == 1))
            if m == 1:
                ins.then_inc(piece_used, 1)
            elif i == 3:
                ins.then_inc(half_ready, 1)

        def turn_rows(src, i, bank, done):
            for k in range(2):
                for m in range(MT):
                    ins = t.transpose(ps[bank][:, k * S + m * P:k * S + (m + 1) * P],
                                      src[:, m, (2 * i + k) * P:(2 * i + k + 1) * P], ident[:])
            ins.then_inc(done, 1)

        def turn_x(ready, value, pairs, banks):
            pe.wait_ge(ready, value)
            for i in pairs:
                turn_rows(x, i, banks[i], x_turned)

        def turn_unit(unit, u):
            pe.wait_ge(unit_staged, unit + 1)
            for b in range(4):
                ins = t.transpose(ps[QK_BANK][:, b * P:(b + 1) * P], staged[:, u % 2, b * P:(b + 1) * P], ident[:])
            ins.then_inc(unit_turned, 1)

        def heads_of(u, c):
            both = turned[c * HD:(c + 1) * HD, u % 2, :]
            return both[:, 0:S], both[:, S:2 * S]

        def add(out_ap, left, right, start=False, stop=False):
            return t.matmul(out_ap, left, right, start=start, stop=stop, skip_group_check=True)

        def softmax_scores(l, i, u):
            pe.wait_ge(turned_ready, UNITS * l + 4 * i + u + 1)
            if u == FX:
                pe.wait_ge(decay_ready, 2 * l + i + 1)
            heads = [(heads_of(u, c), score_bank(u, c)) for c in range(2)]
            for (q, k), sc in heads:
                add(sc[:, 0:P], q[:, 0:P], k[:, 0:P], start=True)
            for (q, k), sc in heads:
                add(sc[:, P:3 * P], q[:, P:S], k)
            for c, (_, sc) in enumerate(heads):
                if u == FX:
                    add(sc[:, 0:P], decay[:, c, 0:P], ones_later[:, P:2 * P])
                    add(sc[:, P:2 * P], decay[:, c, P:2 * P], ones_later[:, P:2 * P])
                    add(sc[:, P:3 * P], decay[:, c, 2 * P:3 * P], ones_later[:])
                add(sc[:, 0:P], ident_bf[:], mask_bf[:])
                add(sc[:, 2 * P:3 * P], ident_bf[:], mask_bf[:], stop=True).then_inc(scores_ready, 1)

        def turn_prob(l, i, u):
            k = 8 * l + 4 * i + TURNS[u]
            for c in range(2 if u == FX else 1):
                pe.wait_ge(prob_ready, k + c + 1)
                for b in range(3):
                    ins = t.transpose(score_bank(u, c)[:, b * P:(b + 1) * P], prob[:, u % 2, c, b * P:(b + 1) * P],
                                      ident[:])
                ins.then_inc(prob_turned, 1)

        def stick_scores(l, i):
            pe.wait_ge(turned_ready, UNITS * l + 4 * i + SB + 1)
            heads = [(heads_of(SB, c), score_bank(SB, c)) for c in range(2)]
            for (q, k), sc in heads:
                add(sc[:, 0:S], k[:, 0:P], q, start=True)
            for (q, k), sc in heads:
                add(sc[:, S:3 * P], k[:, P:S], q[:, P:S]).then_inc(scores_ready, 1)

        def stick_sum(l, i):
            for c in range(2):
                pe.wait_ge(stick_masked, 4 * l + 2 * i + c + 1)
                sc, sp = score_bank(SB, c), prob_t[:, 0, c, :]
                add(sc[:, 0:S], neg_from[:, 0:P], sp[:, 0:S])
                add(sc[:, P:S], neg_from[:, P:2 * P], sp[:, S:3 * P])
                add(sc[:, S:3 * P], neg_from[:, 0:P], sp[:, S:3 * P])
                add(sc[:, 0:P], ident_bf[:], later_bf[:])
                add(sc[:, S:3 * P], ident_bf[:], later_bf[:], stop=True).then_inc(stick_sums, 1)

        def values(l, i, u):
            if u == SB:
                pe.wait_ge(stick_exps, 4 * l + 2 * i + 2)
            else:
                pe.wait_ge(prob_t_ready, 8 * l + 4 * i + TURNS[u] + (2 if u == FX else 1))
            v_col = (V_DIFF + 2 * P * i, V_DIFF + 2 * P * i + P, V_STICK + P * i, V_FOX + P * i)[u]
            width = P if u in (D0, D1) else HD
            for c in range(P // width):
                w = prob[:, 0, c, :] if u == SB else prob_t[:, u % 2, c, :]
                v = [qkv[:, m, bass.ds(v_col + c * width, width)] for m in range(MT)]
                o = ps[OUT_BANK]
                add(o[:, c * width:(c + 1) * width], w[:, 0:P], v[0], start=True, stop=True)
                o1 = o[:, P + c * width:P + (c + 1) * width]
                add(o1, w[:, P:2 * P], v[0], start=True)
                ins = add(o1, w[:, 2 * P:3 * P], v[1], stop=True)
            ins.then_inc(unit_done, 1)

        def branch(l, j, m, i):
            b = (0, 1, 1, 2)[i]
            if m == 0 and j == 0:
                pe.wait_ge(o_lo, 4 * l + i + 1)
            if i != 2 and j == 1:
                pe.wait_ge(branch_read, 12 * l + 3 * m + b + 1)
            n = P_BRANCH + PER_BLOCK * j + i
            if m == 0:
                pe.wait_ge(split_done, RING + PIECES * l + n + 1)
            for k in range(2):
                ins = product(ps[2 + 3 * m + b][:], left_of((b_hi, b_lo), 2 * i + k, m),
                              right_of(n % RING, k), start=(i != 2 and k == 0), stop=(i != 1 and k == 1))
            if m == 1:
                ins.then_inc(piece_used, 1)
            elif i != 1:
                ins.then_inc(branch_ready, 1)

        def chunk(l, s, par, j, kcs, slot):
            p, g = j // 2, j % 2
            for kc in kcs:
                ins = product(ps[2 * par + p][:, g * S:(g + 1) * S],
                              [z[:, slot, kc * P:(kc + 1) * P] for z in (w_hi, w_lo)],
                              [z[:, kc, :] for z in (b_hi, b_lo)],
                              start=(kc == 0 and g == 0), stop=(kc == KC - 1 and g == 1))
            return ins

        def up(l, s, par, slots, piece):
            for j in range(4):
                if j % 2 == 0:
                    pe.wait_ge(up_read, 2 * (STEPS * l + s) + j // 2 + 1)
                pe.wait_ge(split_done, RING + PIECES * l + piece + j + 1)
                chunk(l, s, par, j, range(KC), slots[j]).then_inc(piece_used, 1)

        def spread_factor(l):
            pe.wait_ge(r_ready, 2 * l + 2)
            for m in range(MT):
                ins = add(ps[6][:, m * P:(m + 1) * P], r_tok[:, m:m + 1].broadcast_to([P, P]), ident[:],
                          start=True, stop=True)
            ins.then_inc(r_spread, 1)

        def first_up(l, n2, slots):
            for j in range(4):
                pe.wait_ge(split_done, RING + PIECES * l + P_FFN + j + 1)
                for i in range(2):
                    if j == 0:
                        pe.wait_ge(norm_lo, 4 * n2 + i + 1)
                    chunk(l, 0, 0, j, (2 * i, 2 * i + 1), slots[j])
                if j == 0:
                    turn_x(mix_added, 4 * l + 4, (2, 3), FFN_BANKS)
            for j in range(4):
                for i in (2, 3):
                    if j == 0:
                        pe.wait_ge(norm_lo, 4 * n2 + i + 1)
                    last = chunk(l, 0, 0, j, (2 * i, 2 * i + 1), slots[j])
                last.then_inc(piece_used, 1)
                if j == 1:
                    spread_factor(l)

        def down(l, s, par, slots, piece, final=False):
            for p in range(2):
                pe.wait_ge(h_lo, 2 * (STEPS * l + s) + p + 1)
                pe.wait_ge(split_done, RING + PIECES * l + piece + p + 1)
                ending = final and p == 1
                for k, (j, m) in enumerate(((0, 0), (0, 1), (1, 0), (1, 1))):
                    ins = product(ps[4 + 2 * m + j][:], left_of((a_hi, a_lo), H_AT + 2 * par + p, m),
                                  right_of(slots[p], j), start=False, stop=ending)
                    if ending and k < 3:
                        ins.then_inc(down_ready, 1)
                ins.then_inc(piece_used, 1)
            if final:
                turn_x(x_ready, 4 * (l + 1) + 2, (0, 1), ATTN_BANKS)
                turn_x(x_ready, 4 * (l + 1) + 4, (2, 3), ATTN_BANKS)

        def slots_from(n, count):
            return [(n + k) % RING for k in range(count)]

        pe.sem_inc(piece_used, RING)
        pe.sem_inc(unit_turned, 2)
        pe.wait_ge(ident_ready, 1)
        for j in range(2):
            pe.wait_ge(x_loaded[j], 16)
            pe.sem_inc(x_ready, 2)
            turn_x(x_ready, 2 * j + 2, (2 * j, 2 * j + 1), ATTN_BANKS)
        with pe.Fori(0, DEPTH) as l:
            n1, n2 = 2 * l, 2 * l + 1
            with pe.Fori(0, 2) as turn:
                for b in range(3):
                    B = 3 * turn + b
                    for m, i in QUARTERS:
                        if i == 0:
                            pe.wait_ge(block_read, 2 * ((QKV_BLOCKS + GATE_BLOCKS) * l + B) + m + 1)
                        if m == 0 and b == 0:
                            pe.wait_ge(norm_lo, 4 * n1 + i + 1)
                        quarter(l, PER_BLOCK * B + i, (PER_BLOCK * b + i) % RING, (a_hi, a_lo), ps[QKV_BANKS[b][m]],
                                m, i)
            pe.wait_ge(wf_ready, l + 1)
            pe.wait_ge(block_read, READ_AT_START + 2 * ((QKV_BLOCKS + GATE_BLOCKS) * l + QKV_BLOCKS - 1))
            for kc in range(KC):
                for z in (a_hi, a_lo):
                    ins = add(ps[OUT_BANK][0:8, 0:S], wf[:, kc, :], z[:, kc, :], start=(kc == 0 and z is a_hi),
                              stop=(kc == KC - 1 and z is a_lo))
            ins.then_inc(f_summed, 1)
            pe.wait_ge(consts_ready, 1)
            pe.wait_ge(f_copied, l + 1)
            for m in range(MT):
                ins = add(ps[OUT_BANK][:, 4 * m:4 * m + 4], f_row[:, m * P:(m + 1) * P], fold[:],
                          start=True, stop=True)
            ins.then_inc(f_ready, 1)
            pe.wait_ge(consts_ready, 1)
            with pe.Fori(0, 2) as turn:
                for tick in range(TICKS):
                    for u, (first, score, third, value) in enumerate(UNIT_TICKS):
                        if tick == first:
                            turn_unit(UNITS * l + 4 * turn + u, u)
                        if tick == score:
                            stick_scores(l, turn) if u == SB else softmax_scores(l, turn, u)
                        if tick == third:
                            stick_sum(l, turn) if u == SB else turn_prob(l, turn, u)
                        if tick == value:
                            values(l, turn, u)
                    b = tick // 8
                    m, i = QUARTERS[tick % 8]
                    B = 3 * turn + b
                    if i == 0:
                        pe.wait_ge(block_read, 4 + 2 * ((QKV_BLOCKS + GATE_BLOCKS) * l + QKV_BLOCKS + B) + m + 1)
                    quarter(l, P_GATES + PER_BLOCK * B + i, (PER_BLOCK * b + i) % RING, (a_hi, a_lo), ps[m], m, i)
            pe.wait_ge(out_read, UNITS * l + 4 + SB + 1)
            turn_rows(o_all, 0, O_BANKS[0], o_turned)
            pe.wait_ge(diff_ready, 2 * l + 2)
            turn_rows(o_all, 1, O_BANKS[1], o_turned)
            turn_rows(o_all, 2, O_BANKS[2], o_turned)
            pe.wait_ge(out_read, UNITS * (l + 1))
            turn_rows(o_all, 3, O_BANKS[3], o_turned)
            for j in range(OUT_BLOCKS):
                for k, (m, i) in enumerate(QUARTERS):
                    if j == 1 and k == 4:
                        pe.wait_ge(mixed_ready, 4 * l + 2)
                        pe.wait_ge(block_read, READ_AT_START + 2 * (QKV_BLOCKS + GATE_BLOCKS) * (l + 1))
                        for pair_ in (0, 1):
                            turn_rows(rows, pair_, MIXED_BANKS[pair_], mixed_turned)
                    branch(l, j, m, i)
            for half in range(2):
                for j in range(OUT_BLOCKS):
                    for m in range(MT):
                        if half == 0 and j == 1:
                            pe.wait_ge(branch_read, 12 * l + 6 + m + 1)
                        if half == 0 and (j, m) == (1, 1):
                            pe.wait_ge(mixed_ready, 4 * l + 4)
                            for pair_ in (2, 3):
                                turn_rows(rows, pair_, MIXED_BANKS[pair_], mixed_turned)
                        if half == 1 and (j, m) == (1, 1):
                            turn_x(mix_added, 4 * l + 2, (0, 1), FFN_BANKS)
                        for i in (2 * half, 2 * half + 1):
                            if j == 0 and m == 0:
                                pe.wait_ge(mixed_lo, 4 * l + i + 1)
                            n = P_OUT + 4 * half + 2 * j + i % 2
                            quarter(l, n, n % RING, (a_hi, a_lo), ps[2 * j + m], m, i)
            first_up(l, n2, slots_from(P_FFN, 4))
            pe.wait_ge(r_row_ready, l + 1)
            for b in range(4):
                add(ps[4 + b][:, 0:ZEROS], zero_bf[:], zero_bf[:, 0:ZEROS], start=True)
            with pe.Fori(0, 4) as turn:
                for k in range(2):
                    s, n = 2 * turn + k + 1, P_FFN + 4 + 6 * k
                    up(l, s, (k + 1) % 2, slots_from(n, 4), n + 12 * turn)
                    down(l, s - 1, k % 2, slots_from(n + 4, 2), n + 12 * turn + 4)
            for s in (STEPS - 2, STEPS - 1):
                n = P_FFN + 4 + 6 * (s - 1)
                up(l, s, s % 2, slots_from(n, 4), n)
                down(l, s - 1, (s - 1) % 2, slots_from(n + 4, 2), n + 4)
            n = PIECES - 2
            down(l, STEPS - 1, (STEPS - 1) % 2, slots_from(n, 2), n, final=True)

    block.__exit__(None, None, None)


def _blocks(w):
    n = w.shape[1] // COLS
    return w.reshape(PER_BLOCK, 2, P, n, COLS).transpose(3, 0, 2, 1, 4).reshape(n * PER_BLOCK, P, PIECE)


def _stream(w_in, w_br, w_out, w_up, w_down):
    cuts = {name: (lo, hi) for name, lo, hi in (
        ("fq", 0, 256), ("fk", 256, 512), ("fv", 512, 768), ("dq", 768, 1280), ("dk", 1280, 1792),
        ("dv", 1792, 2304), ("sq", 2304, 2560), ("sk", 2560, 2816), ("sv", 2816, 3072))}
    order = ("sq", "fq", "sk", "fk", "sv", "fv", "dq", "dk", "dv")
    parts = [w_in[:, cuts[k][0]:cuts[k][1]] for k in order] + [w_in[:, QKV + 4:], w_br]
    blocks = [_blocks(np.concatenate(parts, axis=1))]
    halves = _blocks(w_out).reshape(OUT_BLOCKS, 2, 2, P, PIECE).transpose(1, 0, 2, 3, 4)
    blocks.append(halves.reshape(-1, P, PIECE))
    ups = w_up.reshape(KC, P, 2, STEPS, 2, P).transpose(3, 4, 2, 1, 0, 5).reshape(STEPS, 4, P, PIECE)
    downs = w_down.reshape(STEPS, 2, P, D)
    blocks.append(ups[0])
    for s in range(1, STEPS):
        blocks += [ups[s], downs[s - 1]]
    blocks.append(downs[STEPS - 1])
    return np.concatenate(blocks, axis=0)


def _params(l, g_attn, w_in, g_ffn, bias, subln, conv_w, conv_b):
    def tall(v):
        return v.reshape(-1, P).T

    def wide(v):
        return np.broadcast_to(v.reshape(1, -1), (P, v.size))

    wf = w_in[:, QKV:QKV + 4].reshape(KC, P, 4).transpose(1, 0, 2).reshape(P, 4 * KC)
    conv = np.concatenate([conv_w, conv_b[None]], axis=0)
    conv = conv.reshape(4, 2, STEPS, 2, P).transpose(4, 2, 3, 1, 0).reshape(P, 16 * STEPS)
    return np.concatenate([tall(g_attn), tall(g_ffn), wf, wide(bias), wide(subln), conv], axis=1)


def kernel(x, attn_norm_g, w_in, forget_bias, lam_q1, lam_k1, lam_q2, lam_k2, diff_subln_g, w_br_fox,
           w_br_diff, w_br_stick, w_out, ffn_norm_g, w_up, conv_w, conv_b, w_down, final_norm_g):
    import concourse.bacc as _bacc
    from concourse.bass_utils import run_bass_kernel_spmd as _run

    a = {k: np.asarray(v) for k, v in locals().items() if not k.startswith("_")}
    stream, params = [], []
    for l in range(DEPTH):
        w_br = np.concatenate([a["w_br_stick"][l], a["w_br_diff"][l], a["w_br_fox"][l]], axis=0)
        stream.append(_stream(a["w_in"][l], w_br, a["w_out"][l], a["w_up"][l], a["w_down"][l]))
        params.append(_params(l, a["attn_norm_g"][l], a["w_in"][l], a["ffn_norm_g"][l], a["forget_bias"][l],
                              a["diff_subln_g"][l], a["conv_w"][l], a["conv_b"][l]))
    lam_rows = np.stack([a["lam_q1"], a["lam_k1"], a["lam_q2"], a["lam_k2"]], axis=1)
    half = HD // 8
    inv_freq = np.float32(500000.0) ** (-np.arange(0, 2 * half, 2, dtype=np.float32) / np.float32(2 * half))
    ang = np.arange(S, dtype=np.float32)[:, None] * inv_freq[None, :].astype(np.float32)
    table = np.stack([np.cos(ang), np.sin(ang)]).astype(np.float32).reshape(2, MT, P, half).transpose(2, 0, 1, 3)
    table = np.broadcast_to(table[:, :, None, :, None, :], (P, 2, 2, MT, 2, half)).reshape(P, 2, 64)

    nc = _bacc.Bacc("TRN2", target_bir_lowering=False, num_devices=1)
    arrays = {
        "x_in": a["x"].reshape(S, D),
        "stream": np.concatenate(stream, axis=0),
        "params": np.ascontiguousarray(np.stack(params, axis=1)),
        "lam_rows": np.ascontiguousarray(lam_rows.reshape(DEPTH, LAMS)),
        "rope_in": np.ascontiguousarray(table),
        "g_final": np.ascontiguousarray(a["final_norm_g"]),
    }
    args = [nc.dram_tensor(n, v.shape, F32, kind="ExternalInput").ap() for n, v in arrays.items()]
    args.append(nc.dram_tensor("y", (S, D), F32, kind="ExternalOutput").ap())
    build(nc, *args)
    r = _run(nc, [arrays], core_ids=[0])
    return r.results[0]["y"].reshape(1, S, D)
```
